# Optimizing a Trainium2 kernel written in Bass

```python
import math
import jax, jax.numpy as jnp
from jax import lax
import numpy as np

D_MODEL = 1024
BATCH = 1
SEQ = 512
DEPTH = 1

N_META = 16
BLOCK_Q = 128
EPS = 1e-6
NEG_INF = -1e30

SSM_WIDTH = D_MODEL // 2
SSM_GROUP = 16
SSM_GROUPS = SSM_WIDTH // SSM_GROUP
SSM_STATE = 64
DT_MIN = 1e-3
DT_MAX = 1e-1

ATT_HEADS = 4
QK_DIM = 64
V_DIM = 2 * QK_DIM
ATT_WIDTH = ATT_HEADS * V_DIM
QK_COLS = ATT_HEADS * 2 * QK_DIM

IN_COLS = SSM_WIDTH + 2 * QK_COLS + ATT_WIDTH + 2 * D_MODEL
SPLITS = (SSM_WIDTH,
          SSM_WIDTH + QK_COLS,
          SSM_WIDTH + 2 * QK_COLS,
          SSM_WIDTH + 2 * QK_COLS + ATT_WIDTH,
          SSM_WIDTH + 2 * QK_COLS + ATT_WIDTH + D_MODEL)

D_FF = ((8 * D_MODEL // 3 + 127) // 128) * 128
CONV_W = 3


def rmsnorm(x, g):
    xf = x.astype(jnp.float32)
    r = lax.rsqrt(jnp.mean(xf * xf, axis=-1, keepdims=True) + EPS)
    return (xf * r).astype(x.dtype) * g

def s5_mixer(u, a_re, a_im, log_dt, b_re, b_im, c_re, c_im, d, glu_w, glu_b):
    bsz, seq_len, _ = u.shape
    ug = u.astype(jnp.float32).reshape(bsz, seq_len, SSM_GROUPS, SSM_GROUP)
    a_re = a_re.astype(jnp.float32); a_im = a_im.astype(jnp.float32)
    dt = jnp.exp(log_dt.astype(jnp.float32))[:, None]
    mag = jnp.exp(a_re * dt)
    lb_re = mag * jnp.cos(a_im * dt)
    lb_im = mag * jnp.sin(a_im * dt)
    den = a_re * a_re + a_im * a_im
    n_re = lb_re - 1.0
    f_re = (n_re * a_re + lb_im * a_im) / den
    f_im = (lb_im * a_re - n_re * a_im) / den
    b_re = b_re.astype(jnp.float32); b_im = b_im.astype(jnp.float32)
    bb_re = f_re[..., None] * b_re - f_im[..., None] * b_im
    bb_im = f_re[..., None] * b_im + f_im[..., None] * b_re
    x_re = jnp.einsum('blgc,gpc->blgp', ug, bb_re)
    x_im = jnp.einsum('blgc,gpc->blgp', ug, bb_im)
    shp = (1, seq_len, SSM_GROUPS, SSM_STATE)
    a_re_t = jnp.broadcast_to(lb_re, shp)
    a_im_t = jnp.broadcast_to(lb_im, shp)

    def combine(left, right):
        ar_l, ai_l, br_l, bi_l = left
        ar_r, ai_r, br_r, bi_r = right
        return (ar_r * ar_l - ai_r * ai_l,
                ar_r * ai_l + ai_r * ar_l,
                ar_r * br_l - ai_r * bi_l + br_r,
                ar_r * bi_l + ai_r * br_l + bi_r)

    _, _, s_re, s_im = lax.associative_scan(combine, (a_re_t, a_im_t, x_re, x_im), axis=1)
    y = (jnp.einsum('blgp,gcp->blgc', s_re, c_re.astype(jnp.float32))
         - jnp.einsum('blgp,gcp->blgc', s_im, c_im.astype(jnp.float32))
         + d.astype(jnp.float32) * ug)
    y = jax.nn.gelu(y.reshape(bsz, seq_len, SSM_WIDTH)).astype(u.dtype)
    return y * jax.nn.sigmoid(y @ glu_w + glu_b)

def diff_attention(q, k, v, lam, slopes):
    bsz, seq_len = q.shape[:2]
    nb = seq_len // BLOCK_Q
    qb = jnp.moveaxis(q.reshape(bsz, nb, BLOCK_Q, ATT_HEADS, 2, QK_DIM), 1, 0)
    starts = jnp.arange(nb, dtype=jnp.int32) * BLOCK_Q
    kpos = jnp.arange(seq_len, dtype=jnp.int32)

    def one_block(args):
        q_blk, start = args
        s = jnp.einsum('bqhjd,bkhjd->bhjqk', q_blk, k,
                       preferred_element_type=jnp.float32)
        dist = (start + jnp.arange(BLOCK_Q, dtype=jnp.int32))[:, None] - kpos[None, :]
        s = s - slopes[None, :, None, None, None] * dist.astype(jnp.float32)[None, None, None]
        s = jnp.where(dist[None, None, None] >= 0, s, NEG_INF)
        p = jax.nn.softmax(s, axis=-1)
        w = p[:, :, 0] - lam * p[:, :, 1]
        return jnp.einsum('bhqk,bkhe->bqhe', w.astype(v.dtype), v)

    o = lax.map(one_block, (qb, starts))
    return jnp.moveaxis(o, 0, 1).reshape(bsz, seq_len, ATT_HEADS, V_DIM)

def conv_glu_ffn(h, w_up, conv_w, conv_b, w_down):
    seq_len = h.shape[1]
    up = h @ w_up
    a, b = up[..., :D_FF], up[..., D_FF:]
    a_pad = jnp.pad(a, ((0, 0), (CONV_W - 1, 0), (0, 0)))
    c = (a_pad[:, 0:seq_len] * conv_w[0] + a_pad[:, 1:seq_len + 1] * conv_w[1]
         + a_pad[:, 2:seq_len + 2] * conv_w[2] + conv_b)
    return (jax.nn.gelu(c) * b) @ w_down

def first_inputs(seed: int = 0) -> dict:
    key = jax.random.key(seed)
    ks = jax.random.split(key, 32)
    f32 = jnp.float32
    nrm = lambda k, shp, s: s * jax.random.normal(k, shp, f32)
    L_ = DEPTH
    return {
        'x': jax.random.normal(ks[0], (BATCH, SEQ, D_MODEL), f32),
        'meta_tokens': nrm(ks[1], (N_META, D_MODEL), 1.0),
        'norm1_g': 1.0 + nrm(ks[2], (L_, D_MODEL), 0.02),
        'w_in': nrm(ks[3], (L_, D_MODEL, IN_COLS), D_MODEL ** -0.5),
        'ssm_a_re': -0.5 + nrm(ks[4], (L_, SSM_GROUPS, SSM_STATE), 0.01),
        'ssm_a_im': math.pi * jnp.arange(SSM_STATE, dtype=f32)[None, None, :]
                    + nrm(ks[5], (L_, SSM_GROUPS, SSM_STATE), 0.01),
        'ssm_log_dt': jax.random.uniform(ks[6], (L_, SSM_GROUPS), f32,
                                         math.log(DT_MIN), math.log(DT_MAX)),
        'ssm_b_re': nrm(ks[7], (L_, SSM_GROUPS, SSM_STATE, SSM_GROUP), (2 * SSM_GROUP) ** -0.5),
        'ssm_b_im': nrm(ks[8], (L_, SSM_GROUPS, SSM_STATE, SSM_GROUP), (2 * SSM_GROUP) ** -0.5),
        'ssm_c_re': nrm(ks[9], (L_, SSM_GROUPS, SSM_GROUP, SSM_STATE), (2 * SSM_STATE) ** -0.5),
        'ssm_c_im': nrm(ks[10], (L_, SSM_GROUPS, SSM_GROUP, SSM_STATE), (2 * SSM_STATE) ** -0.5),
        'ssm_d': nrm(ks[11], (L_, SSM_GROUPS, SSM_GROUP), 1.0),
        'ssm_glu_w': nrm(ks[12], (L_, SSM_WIDTH, SSM_WIDTH), SSM_WIDTH ** -0.5),
        'ssm_glu_b': nrm(ks[13], (L_, SSM_WIDTH), 0.01),
        'q_norm_g': 1.0 + nrm(ks[14], (L_, QK_DIM), 0.02),
        'k_norm_g': 1.0 + nrm(ks[15], (L_, QK_DIM), 0.02),
        'lam_q1': nrm(ks[16], (L_, QK_DIM), 0.1),
        'lam_k1': nrm(ks[17], (L_, QK_DIM), 0.1),
        'lam_q2': nrm(ks[18], (L_, QK_DIM), 0.1),
        'lam_k2': nrm(ks[19], (L_, QK_DIM), 0.1),
        'subln_g': 1.0 + nrm(ks[20], (L_, V_DIM), 0.02),
        'w_ssm_out': nrm(ks[21], (L_, SSM_WIDTH, D_MODEL), SSM_WIDTH ** -0.5),
        'w_att_out': nrm(ks[22], (L_, ATT_WIDTH, D_MODEL), ATT_WIDTH ** -0.5),
        'w_o': nrm(ks[23], (L_, D_MODEL, D_MODEL), D_MODEL ** -0.5),
        'norm2_g': 1.0 + nrm(ks[24], (L_, D_MODEL), 0.02),
        'w_up': nrm(ks[25], (L_, D_MODEL, 2 * D_FF), D_MODEL ** -0.5),
        'conv_w': nrm(ks[26], (L_, CONV_W, D_FF), CONV_W ** -0.5),
        'conv_b': nrm(ks[27], (L_, D_FF), 0.01),
        'w_down': nrm(ks[28], (L_, D_FF, D_MODEL), D_FF ** -0.5),
    }

def first_block(x, meta_tokens, norm1_g, w_in, ssm_a_re, ssm_a_im, ssm_log_dt, ssm_b_re, ssm_b_im,
              ssm_c_re, ssm_c_im, ssm_d, ssm_glu_w, ssm_glu_b, q_norm_g, k_norm_g,
              lam_q1, lam_k1, lam_q2, lam_k2, subln_g, w_ssm_out, w_att_out, w_o,
              norm2_g, w_up, conv_w, conv_b, w_down):
    bsz, seq, _ = x.shape
    seq_len = seq + N_META
    seq_pad = -(-seq_len // BLOCK_Q) * BLOCK_Q
    meta = jnp.broadcast_to(meta_tokens[None].astype(x.dtype), (bsz, N_META, D_MODEL))
    h = jnp.concatenate([meta, x, jnp.zeros((bsz, seq_pad - seq_len, D_MODEL), x.dtype)], axis=1)
    slopes = 2.0 ** (-8.0 * jnp.arange(1, ATT_HEADS + 1, dtype=jnp.float32) / ATT_HEADS)
    q_scale = QK_DIM ** -0.5

    for l in range(DEPTH):
        lam_init = 0.8 - 0.6 * math.exp(-0.3 * l)
        hn = rmsnorm(h, norm1_g[l])
        proj = hn @ w_in[l]
        u, q, k, v, g_ssm, g_att = jnp.split(proj, SPLITS, axis=-1)
        y_ssm = s5_mixer(u, ssm_a_re[l], ssm_a_im[l], ssm_log_dt[l], ssm_b_re[l], ssm_b_im[l],
                         ssm_c_re[l], ssm_c_im[l], ssm_d[l], ssm_glu_w[l], ssm_glu_b[l])
        q = rmsnorm(q.reshape(bsz, seq_pad, ATT_HEADS, 2, QK_DIM), q_norm_g[l]) * q_scale
        k = rmsnorm(k.reshape(bsz, seq_pad, ATT_HEADS, 2, QK_DIM), k_norm_g[l])
        v = v.reshape(bsz, seq_pad, ATT_HEADS, V_DIM)
        lam = (jnp.exp(jnp.sum(lam_q1[l] * lam_k1[l]).astype(jnp.float32))
               - jnp.exp(jnp.sum(lam_q2[l] * lam_k2[l]).astype(jnp.float32)) + lam_init)
        o = diff_attention(q, k, v, lam, slopes)
        y_att = (rmsnorm(o, subln_g[l]) * (1.0 - lam_init)).reshape(bsz, seq_pad, ATT_WIDTH)
        mixed = (jax.nn.sigmoid(g_ssm) * (y_ssm @ w_ssm_out[l])
                 + jax.nn.sigmoid(g_att) * (y_att @ w_att_out[l]))
        h = h + mixed @ w_o[l]
        h = h + conv_glu_ffn(rmsnorm(h, norm2_g[l]), w_up[l], conv_w[l], conv_b[l], w_down[l])

    return h[:, N_META:N_META + seq]


DEPTH_2 = 2

GLA_HEADS = 4
GLA_DK = D_MODEL // 2 // GLA_HEADS
GLA_DV = D_MODEL // GLA_HEADS
GLA_GATE_RANK = 16
GLA_TAU = 16.0
GLA_CHUNK = 64

NSA_HEADS = 16
NSA_GROUPS = 4
NSA_HPG = NSA_HEADS // NSA_GROUPS
NSA_HEAD_DIM = D_MODEL // NSA_HEADS
CMP_BLOCK = 32
CMP_STRIDE = 16
CMP_HIDDEN = 256
SLC_BLOCK = 64
SLC_TOP_N = 16
WINDOW = 512
Q_BLOCK = 128

ROPE_THETA = 500000.0
ROT_DIM = NSA_HEAD_DIM // 4

N_EXPERTS = 16
N_EXPERT_GROUPS = 4
EXPERTS_PER_GROUP = N_EXPERTS // N_EXPERT_GROUPS
TOP_K = 2
D_FF_EXPERT = D_MODEL // 4

DN_ALPHA = (2 * DEPTH_2) ** 0.25
DN_BETA = (8 * DEPTH_2) ** -0.25
LN_EPS = 1e-5
NEG = -1e30
BIG = 1e30

N_GLA_LAYERS = (DEPTH_2 + 1) // 2
N_NSA_LAYERS = DEPTH_2 // 2
GLA_IN = 2 * GLA_HEADS * GLA_DK + 2 * GLA_HEADS * GLA_DV + GLA_GATE_RANK
NSA_IN = NSA_HEADS * NSA_HEAD_DIM + 6 * NSA_GROUPS * NSA_HEAD_DIM + 3 * NSA_HEADS


def layer_norm(x, g, b):
    xf = x.astype(jnp.float32)
    mu = jnp.mean(xf, axis=-1, keepdims=True)
    var = jnp.mean(jnp.square(xf - mu), axis=-1, keepdims=True)
    y = (xf - mu) * lax.rsqrt(var + LN_EPS) * g.astype(jnp.float32) + b.astype(jnp.float32)
    return y.astype(x.dtype)

def partial_rope(t, pos):
    half = ROT_DIM // 2
    inv_freq = jnp.power(ROPE_THETA, -jnp.arange(half, dtype=jnp.float32) * (2.0 / ROT_DIM))
    ang = pos.astype(jnp.float32)[:, None] * inv_freq[None, :]
    cos = jnp.cos(ang).astype(t.dtype)
    sin = jnp.sin(ang).astype(t.dtype)
    x1 = t[..., :half]
    x2 = t[..., half:ROT_DIM]
    return jnp.concatenate([x1 * cos - x2 * sin, x2 * cos + x1 * sin, t[..., ROT_DIM:]], axis=-1)

def masked_softmax(scores, mask):
    return jax.nn.softmax(jnp.where(mask, scores.astype(jnp.float32), NEG), axis=-1)

def gla_mixer(x, w_in, w_gate_up, b_gate, norm_g, w_out):
    B, S, _ = x.shape
    H, DK, DV, C = GLA_HEADS, GLA_DK, GLA_DV, GLA_CHUNK
    N = S // C
    f32 = jnp.float32
    proj = x @ w_in
    cuts = np.cumsum([H * DK, H * DK, H * DV, GLA_GATE_RANK]).tolist()
    q, k, v, g_low, r = jnp.split(proj, cuts, axis=-1)
    log_a = jax.nn.log_sigmoid((g_low @ w_gate_up + b_gate).astype(f32)) / GLA_TAU

    def chunks(t, d):
        return t.reshape(B, N, C, H, d).transpose(0, 3, 1, 2, 4).astype(f32)

    q = chunks(q, DK) * (DK ** -0.5)
    k = chunks(k, DK)
    v = chunks(v, DV)
    b = jnp.cumsum(chunks(log_a, DK), axis=3)
    b_last = b[:, :, :, -1:, :]
    q_dec = q * jnp.exp(b)
    causal = jnp.tril(jnp.ones((C, C), dtype=bool))
    scores = jnp.einsum('bhnid,bhnjd->bhnij', q_dec, k * jnp.exp(-b))
    o_intra = jnp.einsum('bhnij,bhnjv->bhniv', jnp.where(causal, scores, 0.0), v)
    kv = jnp.einsum('bhncd,bhncv->bhndv', k * jnp.exp(b_last - b), v)
    decay = jnp.exp(b_last[:, :, :, 0, :])

    def step(state, inp):
        dec, kv_n = inp
        return dec[..., None] * state + kv_n, state

    _, states = lax.scan(step, jnp.zeros((B, H, DK, DV), f32),
                         (jnp.moveaxis(decay, 2, 0), jnp.moveaxis(kv, 2, 0)))
    o_inter = jnp.einsum('bhncd,nbhdv->bhncv', q_dec, states)
    o = (o_intra + o_inter).transpose(0, 2, 3, 1, 4).reshape(B, S, H, DV)
    o = o * lax.rsqrt(jnp.mean(jnp.square(o), axis=-1, keepdims=True) + LN_EPS) * norm_g.astype(f32)
    o = o.reshape(B, S, H * DV) * jax.nn.silu(r.astype(f32))
    return o.astype(x.dtype) @ w_out

def compress(t, w1, w2, pe):
    B, G, S, Dh = t.shape
    n_chunk = S // CMP_STRIDE
    span = CMP_BLOCK // CMP_STRIDE
    nc = n_chunk - span + 1
    ch = t.reshape(B, G, n_chunk, CMP_STRIDE, Dh)
    blocks = jnp.concatenate([ch[:, :, i:i + nc] for i in range(span)], axis=3)
    blocks = (blocks + pe).reshape(B, G, nc, CMP_BLOCK * Dh)
    return jax.nn.silu(blocks @ w1) @ w2

def nsa_mixer(x, w_in, w_ck1, w_ck2, w_cv1, w_cv2, cmp_pe, w_out):
    B, S, _ = x.shape
    H, G, HPG, Dh = NSA_HEADS, NSA_GROUPS, NSA_HPG, NSA_HEAD_DIM
    f32 = jnp.float32
    proj = x @ w_in
    cuts = np.cumsum([H * Dh] + [G * Dh] * 6).tolist()
    q, kc, vc, ks, vs, kw, vw, gates = jnp.split(proj, cuts, axis=-1)
    pos = jnp.arange(S, dtype=jnp.int32)

    def kv_heads(t):
        return t.reshape(B, S, G, Dh).transpose(0, 2, 1, 3)

    q = partial_rope(q.reshape(B, S, G, HPG, Dh).transpose(0, 2, 3, 1, 4), pos) * (Dh ** -0.5)
    gates = jax.nn.sigmoid(gates.astype(f32)).reshape(B, S, G, HPG, 3).transpose(0, 2, 3, 1, 4)

    span = CMP_BLOCK // CMP_STRIDE
    nc = S // CMP_STRIDE - span + 1
    cmp_end = jnp.arange(nc, dtype=jnp.int32) * CMP_STRIDE + (CMP_BLOCK - 1)
    k_cmp = partial_rope(compress(kv_heads(kc), w_ck1, w_ck2, cmp_pe), cmp_end)
    v_cmp = compress(kv_heads(vc), w_cv1, w_cv2, cmp_pe).astype(f32)

    ns = S // SLC_BLOCK
    n_sel = min(SLC_TOP_N, ns)
    k_slc = partial_rope(kv_heads(ks), pos).reshape(B, G, ns, SLC_BLOCK, Dh)
    v_slc = kv_heads(vs).reshape(B, G, ns, SLC_BLOCK, Dh)
    ratio = SLC_BLOCK // CMP_STRIDE
    pad_amt = ratio * ns + span - 1 - nc

    pad = ((0, 0), (0, 0), (WINDOW, 0), (0, 0))
    k_win = jnp.pad(partial_rope(kv_heads(kw), pos), pad)
    v_win = jnp.pad(kv_heads(vw), pad)

    bi = jnp.arange(B)[:, None, None, None]
    gi = jnp.arange(G)[None, :, None, None]
    blk_ids = jnp.arange(ns)
    in_blk = jnp.arange(SLC_BLOCK)
    win_off = jnp.arange(WINDOW + Q_BLOCK) - WINDOW

    def query_block(qi):
        s0 = qi * Q_BLOCK
        qpos = s0 + jnp.arange(Q_BLOCK)
        qb = lax.dynamic_slice_in_dim(q, s0, Q_BLOCK, axis=3)
        gb = lax.dynamic_slice_in_dim(gates, s0, Q_BLOCK, axis=3)

        cmask = cmp_end[None, :] <= qpos[:, None]
        p_cmp = masked_softmax(jnp.einsum('bghqd,bgcd->bghqc', qb, k_cmp), cmask)
        p_cmp = p_cmp * jnp.any(cmask, axis=-1)[:, None]
        o_cmp = jnp.einsum('bghqc,bgcd->bghqd', p_cmp, v_cmp)

        p_grp = jnp.pad(p_cmp.sum(axis=2), ((0, 0), (0, 0), (0, 0), (0, pad_amt)))
        imp = p_grp[..., 0:ratio * ns:ratio]
        for m in range(ratio):
            for n in range(span):
                if m + n > 0:
                    imp = imp + p_grp[..., m + n:m + n + ratio * ns:ratio]
        cur = (qpos // SLC_BLOCK)[:, None]
        forced = (blk_ids == 0) | (blk_ids == cur) | (blk_ids == cur - 1)
        imp = jnp.where(blk_ids <= cur, jnp.where(forced, BIG, imp), NEG)
        _, sel = lax.top_k(imp, n_sel)
        k_sel = k_slc[bi, gi, sel].reshape(B, G, Q_BLOCK, n_sel * SLC_BLOCK, Dh)
        v_sel = v_slc[bi, gi, sel].reshape(B, G, Q_BLOCK, n_sel * SLC_BLOCK, Dh)
        kpos = (sel[..., None] * SLC_BLOCK + in_blk).reshape(B, G, Q_BLOCK, n_sel * SLC_BLOCK)
        smask = (kpos <= qpos[:, None])[:, :, None]
        p_slc = masked_softmax(jnp.einsum('bghqd,bgqkd->bghqk', qb, k_sel), smask)
        o_slc = jnp.einsum('bghqk,bgqkd->bghqd', p_slc, v_sel.astype(f32))

        kw_b = lax.dynamic_slice_in_dim(k_win, s0, WINDOW + Q_BLOCK, axis=2)
        vw_b = lax.dynamic_slice_in_dim(v_win, s0, WINDOW + Q_BLOCK, axis=2)
        kwpos = s0 + win_off
        rel = qpos[:, None] - kwpos[None, :]
        wmask = (rel >= 0) & (rel < WINDOW) & (kwpos[None, :] >= 0)
        p_win = masked_softmax(jnp.einsum('bghqd,bgkd->bghqk', qb, kw_b), wmask)
        o_win = jnp.einsum('bghqk,bgkd->bghqd', p_win, vw_b.astype(f32))

        o = gb[..., 0:1] * o_cmp + gb[..., 1:2] * o_slc + gb[..., 2:3] * o_win
        return o.astype(x.dtype)

    outs = lax.map(query_block, jnp.arange(S // Q_BLOCK))
    o = outs.transpose(1, 0, 4, 2, 3, 5).reshape(B, S, H * Dh)
    return o @ w_out

def moe_ffn(x, w_router, b_router, w_gate, w_up, w_down):
    B, S, D = x.shape
    xt = x.reshape(B * S, D)
    n = xt.shape[0]
    s = jax.nn.sigmoid((xt @ w_router).astype(jnp.float32))
    biased = s + b_router.astype(jnp.float32)
    grp_score = lax.top_k(biased.reshape(n, N_EXPERT_GROUPS, EXPERTS_PER_GROUP), TOP_K)[0].sum(-1)
    grp = jnp.argmax(grp_score, axis=-1)
    in_grp = (jnp.arange(N_EXPERTS) // EXPERTS_PER_GROUP)[None, :] == grp[:, None]
    _, top_e = lax.top_k(jnp.where(in_grp, biased, NEG), TOP_K)
    w = jnp.take_along_axis(s, top_e, axis=-1)
    w = w / jnp.sum(w, axis=-1, keepdims=True)
    gate = jnp.zeros((n, N_EXPERTS), jnp.float32).at[jnp.arange(n)[:, None], top_e].set(w)
    h = jax.nn.silu(jnp.einsum('nd,edf->nef', xt, w_gate)) * jnp.einsum('nd,edf->nef', xt, w_up)
    h = h * gate[:, :, None].astype(h.dtype)
    return jnp.einsum('nef,efd->nd', h, w_down).reshape(B, S, D)

def second_inputs(seed: int = 0) -> dict:
    key = jax.random.key(seed)
    ks = jax.random.split(key, 20)
    f32 = jnp.float32

    def nrm(k, shape, scale):
        return jax.random.normal(k, shape, f32) * scale

    D = D_MODEL
    nG, nN = N_GLA_LAYERS, N_NSA_LAYERS
    cmp_in = CMP_BLOCK * NSA_HEAD_DIM
    return {
        'x': nrm(ks[0], (BATCH, SEQ, D), 1.0),
        'gla_w_in': nrm(ks[1], (nG, D, GLA_IN), D ** -0.5),
        'gla_w_gate_up': nrm(ks[2], (nG, GLA_GATE_RANK, GLA_HEADS * GLA_DK), GLA_GATE_RANK ** -0.5),
        'gla_b_gate': nrm(ks[3], (nG, GLA_HEADS * GLA_DK), 0.1),
        'gla_norm_g': 1.0 + nrm(ks[4], (nG, GLA_DV), 0.02),
        'gla_w_out': nrm(ks[5], (nG, GLA_HEADS * GLA_DV, D), DN_BETA * (GLA_HEADS * GLA_DV) ** -0.5),
        'nsa_w_in': nrm(ks[6], (nN, D, NSA_IN), D ** -0.5),
        'nsa_w_cmp_k1': nrm(ks[7], (nN, cmp_in, CMP_HIDDEN), cmp_in ** -0.5),
        'nsa_w_cmp_k2': nrm(ks[8], (nN, CMP_HIDDEN, NSA_HEAD_DIM), CMP_HIDDEN ** -0.5),
        'nsa_w_cmp_v1': nrm(ks[9], (nN, cmp_in, CMP_HIDDEN), cmp_in ** -0.5),
        'nsa_w_cmp_v2': nrm(ks[10], (nN, CMP_HIDDEN, NSA_HEAD_DIM), CMP_HIDDEN ** -0.5),
        'nsa_cmp_pe': nrm(ks[11], (nN, CMP_BLOCK, NSA_HEAD_DIM), 0.1),
        'nsa_w_out': nrm(ks[12], (nN, NSA_HEADS * NSA_HEAD_DIM, D), DN_BETA * (NSA_HEADS * NSA_HEAD_DIM) ** -0.5),
        'moe_w_router': nrm(ks[13], (D, N_EXPERTS), D ** -0.5),
        'moe_b_router': nrm(ks[14], (N_EXPERTS,), 0.01),
        'moe_w_gate': nrm(ks[15], (DEPTH_2, N_EXPERTS, D, D_FF_EXPERT), D ** -0.5),
        'moe_w_up': nrm(ks[16], (DEPTH_2, N_EXPERTS, D, D_FF_EXPERT), D ** -0.5),
        'moe_w_down': nrm(ks[17], (DEPTH_2, N_EXPERTS, D_FF_EXPERT, D), DN_BETA * D_FF_EXPERT ** -0.5),
        'ln_g': 1.0 + nrm(ks[18], (DEPTH_2, 2, D), 0.02),
        'ln_b': nrm(ks[19], (DEPTH_2, 2, D), 0.02),
    }

def second_block(x, gla_w_in, gla_w_gate_up, gla_b_gate, gla_norm_g, gla_w_out,
              nsa_w_in, nsa_w_cmp_k1, nsa_w_cmp_k2, nsa_w_cmp_v1, nsa_w_cmp_v2, nsa_cmp_pe, nsa_w_out,
              moe_w_router, moe_b_router, moe_w_gate, moe_w_up, moe_w_down, ln_g, ln_b):
    for i in range(DEPTH_2):
        j = i // 2
        if i % 2 == 0:
            h = gla_mixer(x, gla_w_in[j], gla_w_gate_up[j], gla_b_gate[j], gla_norm_g[j], gla_w_out[j])
        else:
            h = nsa_mixer(x, nsa_w_in[j], nsa_w_cmp_k1[j], nsa_w_cmp_k2[j], nsa_w_cmp_v1[j],
                          nsa_w_cmp_v2[j], nsa_cmp_pe[j], nsa_w_out[j])
        x = layer_norm(DN_ALPHA * x + h, ln_g[i, 0], ln_b[i, 0])
        f = moe_ffn(x, moe_w_router, moe_b_router, moe_w_gate[i], moe_w_up[i], moe_w_down[i])
        x = layer_norm(DN_ALPHA * x + f, ln_g[i, 1], ln_b[i, 1])
    return x


def setup_inputs(seed=0):
    out = dict(first_inputs(seed))
    for name, value in second_inputs(seed + 1).items():
        if name != "x":
            out[name + "_2"] = value
    return out


def reference(
    x, meta_tokens, norm1_g, w_in, ssm_a_re, ssm_a_im, ssm_log_dt, ssm_b_re, ssm_b_im, ssm_c_re,
    ssm_c_im, ssm_d, ssm_glu_w, ssm_glu_b, q_norm_g, k_norm_g, lam_q1, lam_k1, lam_q2, lam_k2,
    subln_g, w_ssm_out, w_att_out, w_o, norm2_g, w_up, conv_w, conv_b, w_down, gla_w_in_2,
    gla_w_gate_up_2, gla_b_gate_2, gla_norm_g_2, gla_w_out_2, nsa_w_in_2, nsa_w_cmp_k1_2,
    nsa_w_cmp_k2_2, nsa_w_cmp_v1_2, nsa_w_cmp_v2_2, nsa_cmp_pe_2, nsa_w_out_2, moe_w_router_2,
    moe_b_router_2, moe_w_gate_2, moe_w_up_2, moe_w_down_2, ln_g_2, ln_b_2,
):
    x = first_block(
        x, meta_tokens, norm1_g, w_in, ssm_a_re, ssm_a_im, ssm_log_dt, ssm_b_re, ssm_b_im,
        ssm_c_re, ssm_c_im, ssm_d, ssm_glu_w, ssm_glu_b, q_norm_g, k_norm_g, lam_q1, lam_k1,
        lam_q2, lam_k2, subln_g, w_ssm_out, w_att_out, w_o, norm2_g, w_up, conv_w, conv_b,
        w_down,
    )
    return second_block(
        x, gla_w_in_2, gla_w_gate_up_2, gla_b_gate_2, gla_norm_g_2, gla_w_out_2, nsa_w_in_2,
        nsa_w_cmp_k1_2, nsa_w_cmp_k2_2, nsa_w_cmp_v1_2, nsa_w_cmp_v2_2, nsa_cmp_pe_2,
        nsa_w_out_2, moe_w_router_2, moe_b_router_2, moe_w_gate_2, moe_w_up_2, moe_w_down_2,
        ln_g_2, ln_b_2,
    )


_drawn_inputs = setup_inputs


def setup_inputs(seed=0):
    import zlib

    import numpy as np

    out = dict(_drawn_inputs(seed))
    spreads = {}
    factors = {'ssm_a_re': 200.0,
     'ssm_glu_b': 8.0,
     'conv_b': 3.193,
     'gla_norm_g_2': 3.464,
     'nsa_cmp_pe_2': 3.792,
     'ssm_a_im': 10.739,
     'ssm_log_dt': 2.73,
     'ssm_b_re': 11.721,
     'ssm_b_im': 19.061,
     'ssm_c_re': 11.363,
     'ssm_c_im': 14.065}
    for name, (base, spread) in spreads.items():
        noise = np.random.default_rng([zlib.crc32(name.encode()), seed]).standard_normal(out[name].shape)
        drawn = base * np.exp(spread * noise) if base else spread * noise
        out[name] = __import__('jax').numpy.asarray(drawn.astype(out[name].dtype))
    for name, factor in factors.items():
        out[name] = (out[name] * factor).astype(out[name].dtype)
    return out
```

```python
from contextlib import ExitStack, contextmanager
import math

import numpy as np
import concourse.bass as bass
from concourse import mybir

F32 = mybir.dt.float32
I32 = mybir.dt.int32
U32 = mybir.dt.uint32
ALU = mybir.AluOpType
ACT = mybir.ActivationFunctionType
AX = mybir.AxisListType

P = 128
D = 1024
KD = D // P
SEQ = 512
META = 16
T1 = SEQ + META
HALF = T1 // 2
TT = SEQ // P
EPS = 1e-6
LN_EPS = 1e-5
NEG = -1e30

H1 = 4
PAIRS = 16
SC = 16
NCH = T1 // SC
FF = 2816
ATT = 512
FT = FF // P
GH = 4
NH = 16
NG = 4
NCMP = 31
NE = 16
ALPHA = 4 ** 0.25
EG = 4

RING = 6


def constants():
    c = {}
    eye = np.eye(P, dtype=np.float32)
    c["ident"] = eye
    half = np.zeros((P, P), np.float32)
    half[:64, :64] = half[64:, 64:] = 1 / 64
    c["mean64"] = half
    c["mean128"] = np.full((P, P), 1 / 128, np.float32)
    q = np.arange(P)[:, None]
    dist = q - (np.arange(T1)[None] - 400)
    c["alibi"] = np.where(dist >= 0, -dist.astype(np.float32), np.float32(NEG)).astype(np.float32)
    odd = (np.arange(P) // 16) % 2
    c["parity"] = np.stack([odd == 0, odd == 1], 1).astype(np.float32)
    c1 = np.concatenate([c[k] for k in ("ident", "mean64", "mean128", "alibi", "parity")], 1)
    s = {}
    s["causal"] = np.where(q >= np.arange(P)[None], 0, NEG).astype(np.float32)
    end = np.arange(NCMP) * 16 + 31
    pos = np.arange(SEQ).reshape(TT, P)
    s["cmpmask"] = np.where(end[None, None] <= pos.T[:, :, None], 0, NEG).astype(np.float32).reshape(P, -1)
    s["cmpany"] = (end[0] <= pos.T).astype(np.float32)
    j = np.arange(P) % 64
    s["glamask"] = (j[:, None] <= np.arange(64)[None]).astype(np.float32)
    s["restart"] = np.broadcast_to((np.arange(SEQ) % 64 != 0).astype(np.float32), (P, SEQ))
    inv = np.power(np.float32(500000.0), -np.arange(8, dtype=np.float32) * np.float32(2.0 / 16)).astype(np.float32)

    def rope(p):
        ang = (p.astype(np.float32)[:, None] * inv[None]).astype(np.float32).astype(np.float64)
        cs = np.ones((P, len(p)), np.float32)
        sn = np.zeros((P, len(p)), np.float32)
        for b in (0, 64):
            for k in range(8):
                cs[b + k] = cs[b + 8 + k] = np.cos(ang[:, k])
                sn[b + k] = -np.sin(ang[:, k])
                sn[b + 8 + k] = np.sin(ang[:, k])
        return cs, sn

    s["cos"], s["sin"] = rope(np.arange(SEQ))
    s["coscmp"], s["sincmp"] = rope(end)
    swap = np.zeros((P, P), np.float32)
    for b in (0, 64):
        for k in range(8):
            swap[b + k + 8, b + k] = 1
            swap[b + k, b + 8 + k] = 1
    s["swap"] = swap
    pick = np.zeros((P, NE, P), np.float32)
    for e in range(NE):
        pick[e, e] = 1
    s["pick"] = pick.reshape(P, -1)
    c2 = np.concatenate(list(s.values()), 1)

    def places(d, names):
        at, out = 0, {}
        for n in names:
            w = d[n].shape[1]
            out[n] = (at, at + w)
            at += w
        return out

    return (np.ascontiguousarray(c1, np.float32), places(c, ("ident", "mean64", "mean128", "alibi", "parity")),
            np.ascontiguousarray(c2, np.float32), places(s, list(s)))


class Chain:

    def __init__(self, eng, sem):
        self.eng, self.sem, self.n = eng, sem, 0

    def __call__(self, ins):
        self.n += 1
        ins.then_inc(self.sem, 1)
        self.eng.wait_ge(self.sem, self.n)


class Weights:

    def __init__(self, ring, landed, used):
        self.ring, self.landed, self.used = ring, landed, used
        self.parts, self.target, self.total = [], [], [0] * RING
        self.sent, self.n_used, self.free = 0, 0, {}

    def add(self, *parts):
        n = len(self.parts)
        self.parts.append(parts)
        self.total[n % RING] += 16 * len(parts)
        self.target.append(self.total[n % RING])
        return n

    def slot(self, n):
        return self.ring[:, n % RING, :]

    def retire(self, n, ins):
        ins.then_inc(self.used, 1)
        self.n_used += 1
        self.free[n] = (self.used, self.n_used)

    def retired_by(self, n, sem, value):
        self.free[n] = (sem, value)

    def send(self, sp):
        while self.sent < len(self.parts) and (self.sent < RING or self.sent - RING in self.free):
            n = self.sent
            if n >= RING:
                sp.wait_ge(*self.free[n - RING])
            for view, src in self.parts[n]:
                sp.dma_start(view(self.slot(n)), src).then_inc(self.landed[n % RING], 16)
            self.sent += 1

    def arrived(self, pe, n):
        pe.wait_ge(self.landed[n % RING], self.target[n])


def slab_view(k, w):
    return lambda s: s[:, 0:k * w].rearrange("p (k w) -> p k w", k=k)


def tile_of(v, r=P):
    return v[0:r]


TILES1 = [(P, t, META + P * t) for t in range(TT)] + [(META, TT, 0)]
TILES2 = [(P, t, P * t) for t in range(TT)]
HALVES = ((0, HALF), (HALF, T1))


class Program:

    def __init__(self, nc, A, places1, places2, root):
        self.nc, self.A, self.p1, self.p2, self.root, self.stage_sems = nc, A, places1, places2, root, []
        self.ps = root.enter_context(nc.psum_tensor("ps", [P, 8, 512], F32))
        self.ring = self.sb(root, "ring", [P, RING, 2048])
        self.ident = self.sb(root, "ident", [P, P])
        self.h = self.sb(root, "h", [P, TT + 1, D])
        self.W = Weights(self.ring, self.sems("slab_landed", *range(RING)), self.sem("slab_used"))
        self.out_stored = self.sem("out_stored")
        self.stage_sems = []
        self.weight_order()

    @contextmanager
    def new_stage(self):
        with ExitStack() as ctx:
            yield ctx

    def recycle_semaphores(self):
        self.nc.clear_and_free_semaphores(self.stage_sems)
        self.stage_sems = []
        self.nc.all_engine_barrier()

    def sem(self, name):
        s = self.nc.alloc_semaphore(name=name)
        self.stage_sems.append(s)
        return s

    def sems(self, tag, *names):
        return [self.sem(f"{tag}_{x}") for x in names]

    def sb(self, ctx, name, shape, dt=F32):
        return ctx.enter_context(self.nc.sbuf_tensor(name, shape, dt))

    def const(self, which, name):
        a, b = (self.p1 if which == 1 else self.p2)[name]
        return self.A[f"const{which}"][:, a:b]

    def fm_slabs(self, w, c0, n, width=256):
        k = w.shape[0] // P
        return [self.W.add((slab_view(k, width), w[:, c0 + i * width:c0 + (i + 1) * width]
                            .rearrange("(k p) w -> p k w", p=P))) for i in range(n)]

    def tm_slabs(self, w, c0=0):
        return [self.W.add((slab_view(2, D), w[i * 256:(i + 1) * 256, c0:c0 + D]
                            .rearrange("(k p) w -> p k w", p=P))) for i in range(w.shape[0] // 256)]

    def cmp_slabs(self, w):
        return [self.W.add(*[(lambda s, h=h: s[64 * h:64 * h + 64, :].rearrange("p (k w) -> p k w", k=8),
                              w[i * 512:(i + 1) * 512, :].rearrange("(k p) w -> p k w", p=64)) for h in range(2)])
                for i in range(4)]

    def moe_slabs(self, l):
        groups = []
        for g in range(NE // EG):
            gu, dn = [], []
            for e in range(g * EG, g * EG + EG):
                gu.append((self.fm_slabs(self.A["moe_w_gate_2"][l, e], 0, 1)[0],
                           self.fm_slabs(self.A["moe_w_up_2"][l, e], 0, 1)[0]))
            for e in range(g * EG, g * EG + EG):
                dn += self.tm_slabs(self.A["moe_w_down_2"][l, e])
            groups.append((gu, dn))
        return groups

    def weight_order(self):
        A = self.A
        self.n_in = self.fm_slabs(A["w_in"][0], 0, 16)
        self.n_glu = self.fm_slabs(A["ssm_glu_w"][0], 0, 1, 512)
        self.n_so, self.n_ao = [], []
        for i in range(2):
            self.n_so += self.fm_slabs(A["w_ssm_out"][0], i * 512, 1, 512)
            self.n_ao += self.fm_slabs(A["w_att_out"][0], i * 512, 1, 512)
        self.n_o = self.tm_slabs(A["w_o"][0])
        self.n_up = []
        for i in range(FT // 2):
            self.n_up.append((self.fm_slabs(A["w_up"][0], i * 256, 1)[0],
                              self.fm_slabs(A["w_up"][0], FF + i * 256, 1)[0]))
        self.n_dn = self.tm_slabs(A["w_down"][0])
        w = A["gla_w_in_2"][0]
        self.n_gqk = self.fm_slabs(w, 0, 4)
        self.n_glow = self.fm_slabs(w, 2048, 1, 16)
        self.n_gv = self.tm_slabs(w, 1024)
        self.n_gr = self.tm_slabs(w, 2064)
        self.n_go = self.tm_slabs(A["gla_w_out_2"][0])
        self.n_moe = [self.moe_slabs(0)]
        w = A["nsa_w_in_2"][0]
        self.n_nq = self.fm_slabs(w, 0, 4)
        self.n_nkv = [self.fm_slabs(w, c, 1)[0] for c in (1024, 1280, 1536, 2048)]
        self.n_nv = [self.fm_slabs(w, c, 1)[0] for c in (1792, 2304)]
        self.n_gate = self.fm_slabs(w, 2560, 1, 48)[0]
        self.n_cmp = [self.cmp_slabs(A["nsa_w_cmp_k1_2"][0]), self.cmp_slabs(A["nsa_w_cmp_v1_2"][0])]
        self.n_no = self.tm_slabs(A["nsa_w_out_2"][0])
        self.n_moe.append(self.moe_slabs(1))

    def fm_product(self, slab, kt, w, col, rhs, spans, done, m=P):
        v = slab_view(kt, w)(self.W.slot(slab))
        for bank, a, b in spans:
            for k in range(kt):
                ins = self.nc.tensor.matmul(self.ps[0:m, bank, 0:b - a], v[:, k, col:col + m], rhs(k, a, b),
                                            start=(k == 0), stop=(k == kt - 1))
        ins.then_inc(done, 1)
        return ins

    def tm_product(self, pe, slabs, lhsT, done, before=0, bank_free=None):
        n = 2 * len(slabs)
        for i, s in enumerate(slabs):
            self.W.arrived(pe, s)
            v = slab_view(2, D)(self.W.slot(s))
            for kk in range(2):
                k = 2 * i + kk
                for t in range(TT):
                    if k == 0 and bank_free:
                        bank_free(t)
                    for hf in range(2):
                        ins = self.nc.tensor.matmul(self.ps[:, 2 * t + hf, :], lhsT(k, t),
                                                    v[:, kk, hf * 512:hf * 512 + 512],
                                                    start=(k == 0), stop=(k == n - 1))
                    if k == n - 1:
                        ins.then_inc(done, 1)
            if i < len(slabs) - 1:
                self.W.retire(s, ins)
            else:
                self.W.retired_by(s, done, before + TT)

    def norm_stage(self, tag, tiles, src, dst, dstT, kind, gam, bet, eps, loads=(), to_dram=None):
        nc, ps, W = self.nc, self.ps, self.W
        with self.new_stage() as ctx:
            n = len(tiles)
            y = self.sb(ctx, tag + "_y", [P, 2, D])
            junk = self.sb(ctx, tag + "_junk", [P, D])
            st = self.sb(ctx, tag + "_st", [P, 5, 8])
            epsb = self.sb(ctx, tag + "_eps", [P, 1])
            loaded, epsset, centred, rs, normed, turned, evac, dve_own, act_own = self.sems(
                tag, "loaded", "epsset", "centred", "rs", "normed", "turned", "evac", "dve_own", "act_own")
            block = ctx.enter_context(nc.Block())

            @block.scalar
            def _(act):
                for to, frm in loads:
                    act.dma_start(to, frm).then_inc(loaded, 16)
                if kind:
                    act.wait_ge(epsset, 1)
                    link = Chain(act, act_own)
                    for i, (r, t, c0) in enumerate(tiles):
                        if kind == "ln":
                            act.wait_ge(centred, i + 1)
                        link(nc.scalar.activation(junk[0:r], src[0:r, t, :], ACT.Square,
                                                  accum_out=st[0:r, 0, t:t + 1]))
                        link(nc.scalar.activation(st[0:r, 1, t:t + 1], st[0:r, 0, t:t + 1], ACT.Ln,
                                                  bias=epsb[0:r, :], scale=1 / D))
                        nc.scalar.activation(st[0:r, 2, t:t + 1], st[0:r, 1, t:t + 1], ACT.Exp,
                                             scale=-0.5).then_inc(rs, 1)
                if dstT is None:
                    return
                for i, (r, t, c0) in enumerate(tiles):
                    for hf in range(2):
                        act.wait_ge(turned, 2 * i + hf + 1)
                        v = ps[:, (2 * i + hf) % 8, :].rearrange("p (k c) -> p k c", k=4)[:, :, 0:r]
                        nc.scalar.copy(dstT[:, 4 * hf:4 * hf + 4, c0:c0 + r], v).then_inc(evac, 1)

            @block.vector
            def _(dve):
                if not kind:
                    return
                nc.vector.memset(epsb[:], eps).then_inc(epsset, 1)
                link = Chain(dve, dve_own)
                if kind == "ln":
                    for i, (r, t, c0) in enumerate(tiles):
                        x = src[0:r, t, :]
                        link(nc.vector.reduce_sum(st[0:r, 3, t:t + 1], x, AX.X))
                        link(nc.vector.tensor_scalar(st[0:r, 4, t:t + 1], st[0:r, 3, t:t + 1], -1 / D, None, ALU.mult))
                        nc.vector.tensor_scalar(x, x, st[0:r, 4, t:t + 1], None, ALU.add).then_inc(centred, 1)
                    dve.wait_ge(centred, n)
                if loads:
                    dve.wait_ge(loaded, 16 * len(loads))
                for i, (r, t, c0) in enumerate(tiles):
                    x = src[0:r, t, :]
                    dve.wait_ge(rs, i + 1)
                    if kind == "rms":
                        if i >= 2:
                            dve.wait_ge(turned, 2 * (i - 1))
                        nc.vector.scalar_tensor_tensor(y[0:r, i % 2, :], x, st[0:r, 2, t:t + 1], gam[0:r, :],
                                                       ALU.mult, ALU.mult).then_inc(normed, 1)
                    else:
                        link(nc.vector.scalar_tensor_tensor(dst[0:r, t, :], x, st[0:r, 2, t:t + 1], gam[0:r, :],
                                                            ALU.mult, ALU.mult))
                        nc.vector.tensor_tensor(dst[0:r, t, :], dst[0:r, t, :], bet[0:r, :], ALU.add)\
                            .then_inc(normed, 1)

            @block.tensor
            def _(pe):
                if dstT is None:
                    return
                for i, (r, t, c0) in enumerate(tiles):
                    if kind:
                        pe.wait_ge(normed, i + 1)
                    for k in range(KD):
                        n4 = 2 * i + k // 4
                        if k % 4 == 0 and n4 >= 8:
                            pe.wait_ge(evac, n4 - 7)
                        s = y[0:r, i % 2, k * P:(k + 1) * P] if kind == "rms" else \
                            (dst if kind else src)[0:r, t, k * P:(k + 1) * P]
                        ins = nc.tensor.transpose(ps[:, n4 % 8, (k % 4) * P:(k % 4) * P + r], s, self.ident[0:r, 0:r])
                        if k % 4 == 3:
                            ins.then_inc(turned, 1)

            @block.sync
            def _(sp):
                W.send(sp)
                if to_dram is not None:
                    for i, (r, t, c0) in enumerate(tiles):
                        sp.wait_ge(normed, i + 1)
                        sp.dma_start(to_dram[t * P:(t + 1) * P, :], dst[:, t, :]).then_inc(self.out_stored, 16)
                    sp.wait_ge(self.out_stored, 16 * n)

    def s5_prepare(self, m, first_loads):
        nc, ps, W, A = self.nc, self.ps, self.W, self.A
        with self.new_stage() as ctx:
            ident = self.ident
            prm = self.sb(ctx, "s5_prm", [P, 28, PAIRS])
            ki = self.sb(ctx, "s5_ki", [P, PAIRS], I32)
            bre, bim = (self.sb(ctx, n, [P, PAIRS, 16]) for n in ("s5_bre", "s5_bim"))
            bt = self.sb(ctx, "s5_bt", [P, 2, PAIRS, 16])
            bpad = self.sb(ctx, "s5_bpad", [P, 2, PAIRS, 2, 16])
            craw = self.sb(ctx, "s5_craw", [P, 2, 4, 64])
            cpad = self.sb(ctx, "s5_cpad", [P, 2, 4, 2, 64])
            parity = self.sb(ctx, "s5_parity", [P, 2])
            loaded, par, padded, turned, sin_in, sin_out, own = self.sems(
                "s5", "loaded", "par", "padded", "turned", "sin_in", "sin_out", "own")
            names = ("are", "aim", "ldt", "dt", "th", "mag", "lr", "li", "sn", "sh", "nre", "den", "rden",
                     "fre", "fim", "x", "kf", "r", "q", "p2", "t0", "t1", "at", "one")
            v = {n: prm[:, i, :] for i, n in enumerate(names)}
            loads = [(v["are"], A["ssm_a_re"].rearrange("o (j g) p -> (o g p) j", g=2)),
                     (v["aim"], A["ssm_a_im"].rearrange("o (j g) p -> (o g p) j", g=2)),
                     (bre[:], A["ssm_b_re"].rearrange("o (j g) p c -> (o g p) j c", g=2)),
                     (bim[:], A["ssm_b_im"].rearrange("o (j g) p c -> (o g p) j c", g=2)),
                     (craw[:, 0], A["ssm_c_re"].rearrange("o (t j) c p -> (o j c) t p", t=4)),
                     (craw[:, 1], A["ssm_c_im"].rearrange("o (t j) c p -> (o j c) t p", t=4)),
                     (m["dcol"][:], A["ssm_d"].rearrange("o (t j) c -> (o j c) t", t=4)),
                     (parity[:], self.const(1, "parity"))]
            for g in range(2):
                loads.append((prm[64 * g:64 * g + 64, 2, :],
                              A["ssm_log_dt"].rearrange("o (j g) -> (o g) j", g=2)[g].partition_broadcast(64)))
            pw = m["pw"]
            block = ctx.enter_context(nc.Block())

            @block.scalar
            def _(act):
                for to, frm in loads:
                    act.dma_start(to, frm).then_inc(loaded, 16)
                act.wait_ge(sin_in, 1)
                nc.scalar.activation(v["sn"], v["r"], ACT.Sin).then_inc(sin_out, 1)
                nc.scalar.activation(v["sh"], v["r"], ACT.Sin, scale=0.5).then_inc(sin_out, 1)
                for i in range(4):
                    act.wait_ge(turned, i + 1)
                    nc.scalar.copy(m["s5m"][:, i, :, :], ps[:, i, :].rearrange("p (t c) -> p t c", t=4))

            @block.vector
            def _(dve):
                link = Chain(dve, own)
                V = nc.vector
                dve.wait_ge(loaded, 16 * (len(loads) + len(first_loads)))

                def round_of(x, scale):
                    link(V.tensor_scalar(v["kf"], x, scale, 12582912.0, ALU.mult, ALU.add))
                    link(V.tensor_scalar(v["kf"], v["kf"], 12582912.0, None, ALU.subtract))

                def reduce_by(x, parts):
                    src = x
                    for c in parts:
                        link(V.scalar_tensor_tensor(v["r"], v["kf"], -c, src, ALU.mult, ALU.add))
                        src = v["r"]

                def exp_of(dst, x):
                    link(V.tensor_scalar(v["x"], x, -87.0, 88.0, ALU.max, ALU.min))
                    round_of(v["x"], 1.4426950408889634)
                    reduce_by(v["x"], (0.693359375, -2.12194440e-4))
                    link(V.tensor_scalar(v["q"], v["r"], 1 / 5040, None, ALU.mult))
                    for c in (1 / 720, 1 / 120, 1 / 24, 1 / 6, 1 / 2, 1.0):
                        link(V.scalar_tensor_tensor(v["q"], v["q"], c, v["r"], ALU.add, ALU.mult))
                    link(V.tensor_scalar(v["kf"], v["kf"], 127.0, 8388608.0, ALU.add, ALU.mult))
                    link(V.tensor_copy(ki[:], v["kf"]))
                    link(V.scalar_tensor_tensor(dst, v["q"], 1.0, ki[:].bitcast(F32), ALU.add, ALU.mult))

                def mul(d, a, b):
                    link(V.tensor_tensor(d, a, b, ALU.mult))

                exp_of(v["dt"], v["ldt"])
                mul(v["at"], v["are"], v["dt"])
                exp_of(v["mag"], v["at"])
                mul(v["th"], v["aim"], v["dt"])
                round_of(v["th"], 1 / (2 * math.pi))
                reduce_by(v["th"], (6.28125, 0.0019340515136718750, 1.2556659146e-06))
                V.tensor_scalar(v["r"], v["r"], 3.1415925, -3.1415925, ALU.min, ALU.max).then_inc(sin_in, 1)
                dve.wait_ge(sin_out, 2)
                mul(v["li"], v["mag"], v["sn"])
                mul(v["t0"], v["sh"], v["sh"])
                link(V.tensor_scalar(v["t0"], v["t0"], -2.0, 1.0, ALU.mult, ALU.add))
                mul(v["lr"], v["mag"], v["t0"])
                link(V.tensor_scalar(v["nre"], v["lr"], -1.0, None, ALU.add))
                mul(v["t0"], v["are"], v["are"])
                mul(v["t1"], v["aim"], v["aim"])
                link(V.tensor_tensor(v["den"], v["t0"], v["t1"], ALU.add))
                link(V.reciprocal(v["rden"], v["den"]))
                for d, x0, x1, op in (("fre", "nre", "li", ALU.add), ("fim", "li", "nre", ALU.subtract)):
                    mul(v["t0"], v[x0], v["are"])
                    mul(v["t1"], v[x1], v["aim"])
                    link(V.tensor_tensor(v["t0"], v["t0"], v["t1"], op))
                    mul(v[d], v["t0"], v["rden"])
                link(V.memset(bpad[:], 0.0))

                def over_c(x):
                    return x.unsqueeze(2).broadcast_to([P, PAIRS, 16])

                for part, (x0, x1, op) in enumerate(((bre, bim, ALU.subtract), (bim, bre, ALU.add))):
                    mul(bt[:, 0], over_c(v["fre"]), x0[:])
                    mul(bt[:, 1], over_c(v["fim"]), x1[:])
                    for g in range(2):
                        q = slice(64 * g, 64 * g + 64)
                        link(V.tensor_tensor(bpad[q, part, :, g, :], bt[q, 0], bt[q, 1], op))
                for part in range(2):
                    for g in range(2):
                        link(V.tensor_scalar(cpad[:, part, :, g, :], craw[:, part], parity[:, g:g + 1],
                                             1.0 if part == 0 else -1.0, ALU.mult, ALU.mult))
                V.tensor_copy(v["one"], v["lr"]).then_inc(padded, 1)
                link(V.tensor_copy(pw[:, 0, :, 0], v["lr"]))
                link(V.tensor_copy(pw[:, 1, :, 0], v["li"]))
                for k in range(1, SC):
                    a, b = pw[:, 0, :, k - 1], pw[:, 1, :, k - 1]
                    mul(v["t0"], a, v["lr"])
                    mul(v["t1"], b, v["li"])
                    link(V.tensor_tensor(pw[:, 0, :, k], v["t0"], v["t1"], ALU.subtract))
                    mul(v["t0"], a, v["li"])
                    mul(v["t1"], b, v["lr"])
                    link(V.tensor_tensor(pw[:, 1, :, k], v["t0"], v["t1"], ALU.add))
                link(V.tensor_scalar(pw[:, 2], pw[:, 1], -1.0, None, ALU.mult))

            @block.tensor
            def _(pe):
                pe.wait_ge(loaded, 16 * (len(loads) + len(first_loads)))
                pe.wait_ge(padded, 1)
                for i in range(4):
                    for t in range(4):
                        src = bpad[:, i, 4 * t:4 * t + 4].rearrange("p j g c -> p (j g c)") if i < 2 else \
                            cpad[:, i - 2, t].rearrange("p g c -> p (g c)")
                        ins = nc.tensor.transpose(ps[:, i, t * P:(t + 1) * P], src, ident[:])
                    ins.then_inc(turned, 1)

            @block.sync
            def _(sp):
                for to, frm in first_loads:
                    sp.dma_start(to, frm).then_inc(loaded, 16)
                sp.wait_ge(loaded, 16 * (len(loads) + len(first_loads)))
                W.send(sp)

    def project_and_s5(self, m):
        nc, ps, W = self.nc, self.ps, self.W
        with self.new_stage() as ctx:
            HP = PAIRS // 2
            z = self.sb(ctx, "z", [P, 2, HP, T1])
            ab = self.sb(ctx, "ab", [P, 2, 2, HP * NCH])
            proj_done, proj_out, x_done, x_out, z_done, y_done, y_out, own = self.sems(
                "pj", "proj_done", "proj_out", "x_done", "x_out", "z_done", "y_done", "y_out", "own")
            hT, uT, gT, s5m, pw = m["hT"], m["qkvT"], m["gateT"], m["s5m"], m["pw"]
            order = [("p", i) for i in range(4)] + [("x", 0)] + [("p", i) for i in range(4, 18)] + [("y", 0), ("x", 1)] + \
                [("p", i) for i in range(18, 32)] + [("y", 1)]
            block = ctx.enter_context(nc.Block())

            @block.tensor
            def _(pe):
                for what, i in order:
                    if what == "p":
                        W.arrived(pe, self.n_in[i // 2])
                        if i >= 2:
                            pe.wait_ge(proj_out, i - 1)
                        b = 2 * (i % 2)
                        ins = self.fm_product(self.n_in[i // 2], KD, 256, (i % 2) * P, lambda k, a, c: hT[:, k, a:c],
                                              [(b, *HALVES[0]), (b + 1, *HALVES[1])], proj_done)
                        if i % 2:
                            W.retired_by(self.n_in[i // 2], proj_done, i + 1)
                    elif what == "x":
                        pe.wait_ge(proj_out, 4)
                        if i:
                            pe.wait_ge(y_out, 2)
                        for lp in range(HP):
                            u, r = divmod(i * HP + lp, 4)
                            r *= 32
                            for part in range(2):
                                n = i * 16 + lp * 2 + part
                                if lp * 2 + part >= 2:
                                    pe.wait_ge(x_out, n - 1)
                                for hf, (a, c) in enumerate(HALVES):
                                    ins = nc.tensor.matmul(ps[:, 4 + 2 * (n % 2) + hf, 0:HALF], s5m[r:r + 32, part, u, :],
                                                           uT[r:r + 32, u, a:c], start=True, stop=True)
                                ins.then_inc(x_done, 1)
                    else:
                        pe.wait_ge(z_done, i + 1)
                        for tl in range(2):
                            u = 2 * i + tl
                            for hf, (a, c) in enumerate(HALVES):
                                for j in range(4):
                                    r = 32 * j
                                    for part in range(2):
                                        ins = nc.tensor.matmul(ps[r:r + 32, 4 + 2 * tl + hf, 0:HALF],
                                                               s5m[:, 2 + part, u, r:r + 32],
                                                               z[:, part, 4 * tl + j, a:c],
                                                               start=(part == 0), stop=(part == 1))
                            ins.then_inc(y_done, 1)

            @block.scalar
            def _(act):
                for what, i in order:
                    if what == "p":
                        act.wait_ge(proj_done, i + 1)
                        b = 2 * (i % 2)
                        src = ps[:, b:b + 2, 0:HALF]
                        if i < 16:
                            dst, f = uT[:, i, :], ACT.Copy
                        else:
                            dst, f = gT[:, i - 16, :], ACT.Sigmoid
                        nc.scalar.activation(dst.rearrange("p (a c) -> p a c", a=2), src, f).then_inc(proj_out, 1)
                    elif what == "x":
                        for n in range(16 * i, 16 * i + 16):
                            act.wait_ge(x_done, n + 1)
                            b = 4 + 2 * (n % 2)
                            nc.scalar.copy(z[:, n % 2, (n // 2) % HP, :].rearrange("p (a c) -> p a c", a=2),
                                           ps[:, b:b + 2, 0:HALF]).then_inc(x_out, 1)

            @block.vector
            def _(dve):
                link = Chain(dve, own)
                z5 = z[:].rearrange("p r j (n t) -> p r j n t", t=SC)

                def step(dst, src, k, half, n):
                    def power(r):
                        return pw[:, r, half * HP:(half + 1) * HP, k].unsqueeze(2).broadcast_to([P, HP, n])
                    A4 = ab[:, 0, :, 0:HP * n].rearrange("p r (j n) -> p r j n", j=HP)
                    B4 = ab[:, 1, :, 0:HP * n].rearrange("p r (j n) -> p r j n", j=HP)
                    V = nc.vector
                    for r in range(2):
                        V.tensor_tensor(A4[:, r], src(r), power(0), ALU.mult).then_inc(own, 1)
                        V.tensor_tensor(B4[:, r], src(1 - r), power(2 if r == 0 else 1), ALU.mult).then_inc(own, 1)
                    link.n += 4
                    dve.wait_ge(own, link.n)
                    link(V.tensor_tensor(ab[:, 0, :, 0:HP * n], ab[:, 0, :, 0:HP * n], ab[:, 1, :, 0:HP * n], ALU.add))
                    for r in range(2):
                        V.tensor_tensor(dst(r), dst(r), A4[:, r], ALU.add).then_inc(own, 1)
                    link.n += 2
                    dve.wait_ge(own, link.n)

                for half in range(2):
                    dve.wait_ge(x_out, 16 * half + 16)
                    for t in range(1, SC):
                        step(lambda r: z5[:, r, :, :, t], lambda r: z5[:, r, :, :, t - 1], 0, half, NCH)
                    for n in range(1, NCH):
                        step(lambda r: z5[:, r, :, n:n + 1, SC - 1], lambda r: z5[:, r, :, n - 1:n, SC - 1], SC - 1, half, 1)
                    for t in range(SC - 1):
                        step(lambda r: z5[:, r, :, 1:, t], lambda r: z5[:, r, :, :-1, SC - 1], t, half, NCH - 1)
                    nc.vector.tensor_copy(ab[:, 0, 0, 0:1], ab[:, 0, 0, 1:2]).then_inc(z_done, 1)
                    for tl in range(2):
                        dve.wait_ge(y_done, 2 * half + tl + 1)
                        u = 2 * half + tl
                        o = uT[:, u, :].rearrange("p (a c) -> p a c", a=2)
                        nc.vector.scalar_tensor_tensor(o, o, m["dcol"][:, u:u + 1], ps[:, 4 + 2 * tl:6 + 2 * tl, 0:HALF],
                                                       ALU.mult, ALU.add).then_inc(y_out, 1)

            @block.sync
            def _(sp):
                W.send(sp)



    def qk_norm_stage(self, m):
        nc, ps, W, A = self.nc, self.ps, self.W, self.A
        with self.new_stage() as ctx:
            sq = self.sb(ctx, "qn_sq", [P, 2, T1])
            r = self.sb(ctx, "qn_r", [P, 2, T1])
            mean64 = self.sb(ctx, "mean64", [P, P])
            gc = self.sb(ctx, "qn_gc", [P, 2])
            lam4 = self.sb(ctx, "lam4", [P, 4, 64])
            lt = self.sb(ctx, "lt", [P, 4])
            eps = self.sb(ctx, "qn_eps", [P, 1])
            loaded, start, sq_done, mean_done, r_done, q_out, v_done, v_out, lam_in, lam_exp, own, actown = self.sems(
                "qn", "loaded", "start", "sq_done", "mean_done", "r_done", "q_out", "v_done", "v_out", "lam_in",
                "lam_exp", "own", "act_own")
            qk = m["qkvT"]
            loads = [(mean64[:], self.const(1, "mean64")), (m["alibi"][:], self.const(1, "alibi"))]
            for i, n in enumerate(("q_norm_g", "k_norm_g")):
                for g in range(2):
                    loads.append((gc[64 * g:64 * g + 64, i:i + 1], A[n].rearrange("o d -> d o")))
            for i, n in enumerate(("lam_q1", "lam_k1", "lam_q2", "lam_k2")):
                loads.append((lam4[:, i, :], A[n][0].partition_broadcast(P)))
            KT = [(META, 0)] + [(P, META + P * t) for t in range(TT)]
            block = ctx.enter_context(nc.Block())

            @block.tensor
            def _(pe):
                for b, (n, c0) in enumerate(KT):
                    if b == 4:
                        pe.wait_ge(v_out, 1)
                    for hd in range(H1):
                        ins = nc.tensor.transpose(ps[0:n, b % 4, hd * P:(hd + 1) * P], qk[:, 12 + hd, c0:c0 + n],
                                                  self.ident[:])
                    ins.then_inc(v_done, 1)
                pe.wait_ge(loaded, 16 * len(loads))
                for i in range(8):
                    pe.wait_ge(sq_done, i + 1)
                    if i >= 2:
                        pe.wait_ge(r_done, i - 1)
                    for hf, (a, c) in enumerate(HALVES):
                        ins = nc.tensor.matmul(ps[:, 4 + 2 * (i % 2) + hf, 0:HALF], mean64[:], sq[:, i % 2, a:c],
                                               start=True, stop=True)
                    ins.then_inc(mean_done, 1)

            @block.scalar
            def _(act):
                for to, frm in loads:
                    act.dma_start(to, frm).then_inc(loaded, 16)
                act.wait_ge(start, 1)
                link = Chain(act, actown)

                def square(i):
                    if i >= 2:
                        act.wait_ge(mean_done, i - 1)
                    nc.scalar.activation(sq[:, i % 2], qk[:, 4 + i], ACT.Square).then_inc(sq_done, 1)

                square(0)
                square(1)
                for i in range(8):
                    act.wait_ge(mean_done, i + 1)
                    if i >= 2:
                        act.wait_ge(q_out, i - 1)
                    b = 4 + 2 * (i % 2)
                    rr = r[:, i % 2].rearrange("p (a c) -> p a c", a=2)
                    link(nc.scalar.activation(rr, ps[:, b:b + 2, 0:HALF], ACT.Ln, bias=eps[:]))
                    nc.scalar.activation(rr, rr, ACT.Exp, scale=-0.5).then_inc(r_done, 1)
                    if i + 2 < 8:
                        square(i + 2)
                act.wait_ge(lam_in, 1)
                nc.scalar.activation(lt[:, 2:4], lt[:, 0:2], ACT.Exp).then_inc(lam_exp, 1)

            @block.vector
            def _(dve):
                link = Chain(dve, own)
                V = nc.vector
                V.memset(eps[:], EPS).then_inc(start, 1)
                dve.wait_ge(loaded, 16 * len(loads))
                link(V.tensor_scalar(gc[:, 0:1], gc[:, 0:1], 0.125, None, ALU.mult))
                for i in range(2):
                    link(V.tensor_tensor(lam4[:, 2 * i], lam4[:, 2 * i], lam4[:, 2 * i + 1], ALU.mult))
                    ins = V.reduce_sum(lt[:, i:i + 1], lam4[:, 2 * i], AX.X)
                    if i == 0:
                        link(ins)
                    else:
                        ins.then_inc(lam_in, 1)
                for b, (n, c0) in enumerate(KT):
                    dve.wait_ge(v_done, b + 1)
                    V.tensor_copy(m["v"][0:n, b, :], ps[0:n, b % 4, :]).then_inc(v_out, 1)
                for i in range(8):
                    dve.wait_ge(r_done, i + 1)
                    V.scalar_tensor_tensor(qk[:, 4 + i], qk[:, 4 + i], gc[:, i // 4:i // 4 + 1], r[:, i % 2],
                                           ALU.mult, ALU.mult).then_inc(q_out, 1)
                dve.wait_ge(lam_exp, 1)
                link(V.tensor_tensor(lt[:, 0:1], lt[:, 3:4], lt[:, 2:3], ALU.subtract))
                link(V.tensor_scalar(m["mlam"][:], lt[:, 0:1], -0.2, None, ALU.add))

            @block.sync
            def _(sp):
                W.send(sp)

    def diff_attention(self, m):
        nc, ps, W = self.nc, self.ps, self.W
        units = [(hd, i) for hd in range(H1) for i in range(TT + 1)]
        shape = [(META, META, 0)] + [(P, META + P * i, META + P * (i - 1)) for i in range(1, TT + 1)]
        KT = [(META, 0)] + [(P, META + P * t) for t in range(TT)]
        with self.new_stage() as ctx:
            s = self.sb(ctx, "da_s", [P, 2, 2, T1])
            w = self.sb(ctx, "da_w", [P, 2, T1])
            wT = self.sb(ctx, "da_wT", [P, 2, 5, P])
            st = self.sb(ctx, "da_st", [P, 2, 8])
            s_done, s_read, maxed, exped, w_done, t_done, t_out, o_done, o_out, own = self.sems(
                "da", "s_done", "s_read", "maxed", "exped", "w_done", "t_done", "t_out", "o_done", "o_out", "own")
            qk, v, oT, alibi = m["qkvT"], m["v"], m["oT"], m["alibi"]
            N = len(units)
            flat = ps[:].rearrange("p b c -> p (b c)")
            block = ctx.enter_context(nc.Block())

            @block.tensor
            def _(pe):
                for it in range(N + 2):
                    if it < N:
                        hd, i = units[it]
                        nq, nk, q0 = shape[i]
                        if it:
                            pe.wait_ge(s_read, it)
                        for j in range(2):
                            for a in range(0, nk, 512):
                                c = min(nk, a + 512)
                                ins = nc.tensor.matmul(flat[0:nq, 1024 * j + a:1024 * j + c],
                                                       qk[64 * j:64 * j + 64, 4 + hd, q0:q0 + nq],
                                                       qk[64 * j:64 * j + 64, 8 + hd, a:c], start=True, stop=True)
                        ins.then_inc(s_done, 1)
                    u = it - 1
                    if 0 <= u < N:
                        hd, i = units[u]
                        nq, nk, q0 = shape[i]
                        pe.wait_ge(w_done, u + 1)
                        if u:
                            pe.wait_ge(t_out, u)
                        for b in range(i + 1):
                            n, c0 = KT[b]
                            ins = nc.tensor.transpose(flat[0:n, 2048 + P * b:2048 + P * b + nq], w[0:nq, u % 2, c0:c0 + n],
                                                      self.ident[0:nq, 0:nq])
                        ins.then_inc(t_done, 1)
                    u = it - 2
                    if u >= 0:
                        hd, i = units[u]
                        nq, nk, q0 = shape[i]
                        pe.wait_ge(t_out, u + 1)
                        if u >= 2:
                            pe.wait_ge(o_out, u - 1)
                        for b in range(i + 1):
                            n, c0 = KT[b]
                            ins = nc.tensor.matmul(ps[:, 6 + u % 2, 0:nq], v[0:n, b, hd * P:(hd + 1) * P],
                                                   wT[0:n, u % 2, b, 0:nq], start=(b == 0), stop=(b == i))
                        ins.then_inc(o_done, 1)

            @block.scalar
            def _(act):
                for it in range(N + 1):
                    if it < N:
                        nq, nk, q0 = shape[units[it][1]]
                        act.wait_ge(maxed, it + 1)
                        for j in range(2):
                            x = s[0:nq, it % 2, j, 0:nk]
                            nc.scalar.activation(x, x, ACT.Exp, bias=st[0:nq, it % 2, j:j + 1],
                                                 accum_out=st[0:nq, it % 2, 2 + j:3 + j]).then_inc(exped, 1)
                    u = it - 1
                    if u >= 0:
                        i = units[u][1]
                        nq = shape[i][0]
                        act.wait_ge(t_done, u + 1)
                        if u >= 2:
                            act.wait_ge(o_done, u - 1)
                        ins = nc.scalar.copy(wT[0:META, u % 2, 0, 0:nq], flat[0:META, 2048:2048 + nq])
                        if i:
                            ins = nc.scalar.copy(wT[:, u % 2, 1:i + 1, 0:nq],
                                                 flat[:, 2048 + P:2048 + P + P * i].rearrange("p (b c) -> p b c", b=i)[:, :, 0:nq])
                        ins.then_inc(t_out, 1)

            @block.vector
            def _(dve):
                link = Chain(dve, own)
                V = nc.vector
                for it in range(N + 3):
                    if it < N:
                        hd, i = units[it]
                        nq, nk, q0 = shape[i]
                        dve.wait_ge(s_done, it + 1)
                        for j in range(2):
                            V.scalar_tensor_tensor(s[0:nq, it % 2, j, 0:nk], alibi[0:nq, 400 - q0:400 - q0 + nk],
                                                   2.0 ** (-2 * (hd + 1)), flat[0:nq, 1024 * j:1024 * j + nk],
                                                   ALU.mult, ALU.add).then_inc(s_read if j else own, 1)
                        link.n += 1
                        dve.wait_ge(own, link.n)
                        dve.wait_ge(s_read, it + 1)
                        V.tensor_reduce(st[0:nq, it % 2, 0:2], s[0:nq, it % 2, :, 0:nk], AX.X, ALU.max,
                                        negate=True).then_inc(maxed, 1)
                    u = it - 1
                    if 0 <= u < N:
                        nq, nk, q0 = shape[units[u][1]]
                        x = st[0:nq, u % 2]
                        dve.wait_ge(exped, 2 * u + 2)
                        link(V.reciprocal(x[:, 4:6], x[:, 2:4]))
                        link(V.tensor_scalar(x[:, 5:6], x[:, 5:6], m["mlam"][0:nq, :], None, ALU.mult))
                        if u >= 2:
                            dve.wait_ge(t_done, u - 1)
                        link(V.tensor_scalar(w[0:nq, u % 2, 0:nk], s[0:nq, u % 2, 0, 0:nk], x[:, 4:5], None, ALU.mult))
                        V.scalar_tensor_tensor(w[0:nq, u % 2, 0:nk], s[0:nq, u % 2, 1, 0:nk], x[:, 5:6],
                                               w[0:nq, u % 2, 0:nk], ALU.mult, ALU.add).then_inc(w_done, 1)
                    u = it - 3
                    if u >= 0:
                        hd, i = units[u]
                        nq, nk, q0 = shape[i]
                        dve.wait_ge(o_done, u + 1)
                        V.tensor_copy(oT[:, hd, q0:q0 + nq], ps[:, 6 + u % 2, 0:nq]).then_inc(o_out, 1)

            @block.sync
            def _(sp):
                W.send(sp)

    def mix_stage(self, m):
        nc, ps, W, A = self.nc, self.ps, self.W, self.A
        with self.new_stage() as ctx:
            sq = self.sb(ctx, "mx_sq", [P, H1, T1])
            r = self.sb(ctx, "mx_r", [P, 2, T1])
            sg = self.sb(ctx, "mx_sg", [P, 2, T1])
            mean128 = self.sb(ctx, "mean128", [P, P])
            gb = self.sb(ctx, "mx_gb", [P, 4])
            sub = self.sb(ctx, "mx_sub", [P, 1])
            eps = self.sb(ctx, "mx_eps", [P, 1])
            tmp = self.sb(ctx, "mx_tmp", [P, 2, T1])
            loaded, start, sq_done, mean_done, r_done, att_done, y_done, glu_done, sg_done, ys_done, pr_done, mx_done, \
                o_done, o_out, meta_done, own, actown = self.sems(
                    "mx", "loaded", "start", "sq_done", "mean_done", "r_done", "att_done", "y_done", "glu_done",
                    "sg_done", "ys_done", "pr_done", "mx_done", "o_done", "o_out", "meta_done", "own", "act_own")
            yT, ysT, oT, gT, mixT, h = m["qkvT"][:, 0:4], m["qkvT"][:, 4:8], m["oT"], m["gateT"], m["hT"], self.h
            loads = [(mean128[:], self.const(1, "mean128")), (gb[:], A["ssm_glu_b"].rearrange("o (t p) -> p (o t)", p=P)),
                     (sub[:], A["subln_g"].rearrange("o p -> p o"))]
            block = ctx.enter_context(nc.Block())

            def pair(b):
                return ps[:, b:b + 2, 0:HALF]

            @block.tensor
            def _(pe):
                pe.wait_ge(loaded, 16 * len(loads))
                for hd in range(H1):
                    pe.wait_ge(sq_done, hd + 1)
                    for hf, (a, c) in enumerate(HALVES):
                        ins = nc.tensor.matmul(ps[:, 2 * hd + hf, 0:HALF], mean128[:], sq[:, hd, a:c], start=True, stop=True)
                    ins.then_inc(mean_done, 1)
                W.arrived(pe, self.n_glu[0])
                pe.wait_ge(y_done, 1)
                for i in range(4):
                    pe.wait_ge(r_done, i + 1)
                    self.fm_product(self.n_glu[0], 4, 512, i * P, lambda k, a, c: yT[:, k, a:c],
                                    [(2 * i, *HALVES[0]), (2 * i + 1, *HALVES[1])], glu_done)
                W.retired_by(self.n_glu[0], glu_done, 4)
                pe.wait_ge(ys_done, 4)
                pe.wait_ge(att_done, 4)
                for i in range(KD):
                    q = i // 4
                    if i >= 2:
                        pe.wait_ge(mx_done, i - 1)
                    b = 4 * (i % 2)
                    if i % 4 == 0:
                        W.arrived(pe, self.n_so[q])
                        W.arrived(pe, self.n_ao[q])
                    for j, (n, x) in enumerate(((self.n_so[q], ysT), (self.n_ao[q], oT))):
                        self.fm_product(n, 4, 512, (i % 4) * P, lambda k, a, c, x=x: x[:, k, a:c],
                                        [(b + 2 * j, *HALVES[0]), (b + 2 * j + 1, *HALVES[1])], pr_done)
                    if i % 4 == 3:
                        W.retired_by(self.n_so[q], pr_done, 2 * i + 2)
                        W.retired_by(self.n_ao[q], pr_done, 2 * i + 2)
                pe.wait_ge(mx_done, KD)
                for i, n in enumerate(self.n_o):
                    W.arrived(pe, n)
                    v = slab_view(2, D)(W.slot(n))
                    for kk in range(2):
                        for t in range(TT):
                            for hf in range(2):
                                ins = nc.tensor.matmul(ps[:, 2 * t + hf, :], mixT[:, 2 * i + kk, META + P * t:META + P * (t + 1)],
                                                       v[:, kk, 512 * hf:512 * hf + 512], start=(i == 0 and kk == 0),
                                                       stop=(i == 3 and kk == 1))
                            if i == 3 and kk == 1:
                                ins.then_inc(o_done, 1)
                pe.wait_ge(o_out, 1)
                for i, n in enumerate(self.n_o):
                    v = slab_view(2, D)(W.slot(n))
                    for kk in range(2):
                        for hf in range(2):
                            ins = nc.tensor.matmul(ps[0:META, hf, :], mixT[:, 2 * i + kk, 0:META],
                                                   v[:, kk, 512 * hf:512 * hf + 512], start=(i == 0 and kk == 0),
                                                   stop=(i == 3 and kk == 1))
                    if i < 3:
                        W.retire(n, ins)
                ins.then_inc(meta_done, 1)
                W.retired_by(self.n_o[3], meta_done, 1)

            @block.scalar
            def _(act):
                for to, frm in loads:
                    act.dma_start(to, frm).then_inc(loaded, 16)
                act.wait_ge(start, 1)
                link = Chain(act, actown)
                for hd in range(H1):
                    nc.scalar.activation(sq[:, hd], oT[:, hd], ACT.Square).then_inc(sq_done, 1)
                nc.scalar.activation(yT, yT, ACT.Gelu_apprx_tanh).then_inc(y_done, 1)
                for hd in range(H1):
                    act.wait_ge(mean_done, hd + 1)
                    if hd >= 2:
                        act.wait_ge(att_done, hd - 1)
                    rr = r[:, hd % 2].rearrange("p (a c) -> p a c", a=2)
                    link(nc.scalar.activation(rr, pair(2 * hd), ACT.Ln, bias=eps[:]))
                    nc.scalar.activation(rr, rr, ACT.Exp, scale=-0.5).then_inc(r_done, 1)
                act.wait_ge(loaded, 16 * len(loads))
                for i in range(4):
                    act.wait_ge(glu_done, i + 1)
                    if i >= 2:
                        act.wait_ge(ys_done, i - 1)
                    nc.scalar.activation(sg[:, i % 2].rearrange("p (a c) -> p a c", a=2), pair(2 * i), ACT.Sigmoid,
                                         bias=gb[:, i:i + 1]).then_inc(sg_done, 1)

            @block.vector
            def _(dve):
                link = Chain(dve, own)
                V = nc.vector
                V.memset(eps[:], EPS).then_inc(start, 1)
                dve.wait_ge(loaded, 16 * len(loads))
                link(V.tensor_scalar(sub[:], sub[:], 0.8, None, ALU.mult))
                for hd in range(H1):
                    dve.wait_ge(r_done, hd + 1)
                    V.scalar_tensor_tensor(oT[:, hd], oT[:, hd], sub[:], r[:, hd % 2], ALU.mult, ALU.mult)\
                        .then_inc(att_done, 1)
                dve.wait_ge(y_done, 1)
                for i in range(4):
                    dve.wait_ge(sg_done, i + 1)
                    V.tensor_tensor(ysT[:, i], yT[:, i], sg[:, i % 2], ALU.mult).then_inc(ys_done, 1)
                for i in range(KD):
                    b = 4 * (i % 2)
                    dve.wait_ge(pr_done, 2 * i + 2)
                    if i:
                        dve.wait_ge(mx_done, i)
                    g = [gT[:, 8 * j + i].rearrange("p (a c) -> p a c", a=2) for j in range(2)]
                    t2 = [tmp[:, j].rearrange("p (a c) -> p a c", a=2) for j in range(2)]
                    for j in range(2):
                        link(V.tensor_tensor(t2[j], g[j], pair(b + 2 * j), ALU.mult))
                    V.tensor_tensor(mixT[:, i], tmp[:, 0], tmp[:, 1], ALU.add).then_inc(mx_done, 1)
                for t in range(TT):
                    dve.wait_ge(o_done, t + 1)
                    x = h[:, t, :].rearrange("p (a c) -> p a c", a=2)
                    V.tensor_tensor(x, x, ps[:, 2 * t:2 * t + 2, :], ALU.add).then_inc(o_out, 1)
                dve.wait_ge(meta_done, 1)
                x = h[0:META, TT, :].rearrange("p (a c) -> p a c", a=2)
                V.tensor_tensor(x, x, ps[0:META, 0:2, :], ALU.add).then_inc(o_out, 1)

            @block.sync
            def _(sp):
                W.send(sp)

    def ffn_stage(self, hT, gT):
        nc, ps, W, A, h = self.nc, self.ps, self.W, self.A, self.h
        with self.new_stage() as ctx:
            a_sb = self.sb(ctx, "ff_a", [P, 2, T1])
            c = self.sb(ctx, "ff_c", [P, 2, SEQ])
            ge = self.sb(ctx, "ff_ge", [P, 2, SEQ])
            cw = self.sb(ctx, "ff_cw", [P, 4, FT])
            loaded, a_done, a_out, b_done, c_done, ge_done, g_done, o_done, o_out, own = self.sems(
                "ff", "loaded", "a_done", "a_out", "b_done", "c_done", "ge_done", "g_done", "o_done", "o_out", "own")
            loads = [(cw[:, j, :], A["conv_w"][0, j].rearrange("(t p) -> p t", p=P)) for j in range(3)]
            loads.append((cw[:, 3, :], A["conv_b"][0].rearrange("(t p) -> p t", p=P)))
            block = ctx.enter_context(nc.Block())

            @block.tensor
            def _(pe):
                for i in range(FT):
                    na, nb = self.n_up[i // 2]
                    W.arrived(pe, na)
                    if i >= 2:
                        pe.wait_ge(a_out, i - 1)
                    s = i % 2
                    self.fm_product(na, KD, 256, s * P, lambda k, a, b: hT[:, k, a:b],
                                    [(2 * s, *HALVES[0]), (2 * s + 1, *HALVES[1])], a_done)
                    W.arrived(pe, nb)
                    if i >= 2:
                        pe.wait_ge(g_done, i - 1)
                    self.fm_product(nb, KD, 256, s * P, lambda k, a, b: hT[:, k, a:b], [(4 + s, META, T1)], b_done)
                    if s:
                        W.retired_by(na, a_done, i + 1)
                        W.retired_by(nb, b_done, i + 1)
                pe.wait_ge(g_done, FT)
                pe.wait_ge(a_out, FT)
                self.tm_product(pe, self.n_dn, lambda k, t: gT[:, k, P * t:P * (t + 1)], o_done)

            @block.scalar
            def _(act):
                for to, frm in loads:
                    act.dma_start(to, frm).then_inc(loaded, 16)
                for it in range(FT + 1):
                    if it < FT:
                        s = it % 2
                        act.wait_ge(a_done, it + 1)
                        if it >= 2:
                            act.wait_ge(c_done, it - 1)
                        nc.scalar.copy(a_sb[:, s].rearrange("p (a c) -> p a c", a=2), ps[:, 2 * s:2 * s + 2, 0:HALF])\
                            .then_inc(a_out, 1)
                    i = it - 1
                    if i >= 0:
                        act.wait_ge(c_done, i + 1)
                        if i >= 2:
                            act.wait_ge(g_done, i - 1)
                        nc.scalar.activation(ge[:, i % 2], c[:, i % 2], ACT.Gelu_apprx_tanh).then_inc(ge_done, 1)

            @block.vector
            def _(dve):
                link = Chain(dve, own)
                V = nc.vector
                dve.wait_ge(loaded, 16 * len(loads))
                for it in range(FT + 1):
                    if it < FT:
                        s = it % 2
                        dve.wait_ge(a_out, it + 1)
                        if it >= 2:
                            dve.wait_ge(ge_done, it - 1)
                        link(V.tensor_scalar(c[:, s], a_sb[:, s, META - 2:T1 - 2], cw[:, 0, it:it + 1], cw[:, 3, it:it + 1],
                                             ALU.mult, ALU.add))
                        link(V.scalar_tensor_tensor(c[:, s], a_sb[:, s, META - 1:T1 - 1], cw[:, 1, it:it + 1], c[:, s],
                                                    ALU.mult, ALU.add))
                        V.scalar_tensor_tensor(c[:, s], a_sb[:, s, META:T1], cw[:, 2, it:it + 1], c[:, s],
                                               ALU.mult, ALU.add).then_inc(c_done, 1)
                    i = it - 1
                    if i >= 0:
                        dve.wait_ge(ge_done, i + 1)
                        dve.wait_ge(b_done, i + 1)
                        V.tensor_tensor(gT[:, i], ge[:, i % 2], ps[:, 4 + i % 2, :], ALU.mult).then_inc(g_done, 1)
                for t in range(TT):
                    dve.wait_ge(o_done, t + 1)
                    x = h[:, t, :].rearrange("p (a c) -> p a c", a=2)
                    V.tensor_tensor(x, x, ps[:, 2 * t:2 * t + 2, :], ALU.add).then_inc(o_out, 1)

            @block.sync
            def _(sp):
                W.send(sp)

    def first_block(self, stop=None):
        A, sb = self.A, self.sb
        with ExitStack() as ctx:
            m = {"hT": sb(ctx, "hT", [P, KD, T1]), "s5m": sb(ctx, "s5m", [P, 4, 4, P]),
                 "pw": sb(ctx, "pw", [P, 3, PAIRS, SC]), "dcol": sb(ctx, "dcol", [P, 4])}
            with ExitStack() as mid:
                m["qkvT"] = sb(mid, "qkvT", [P, 16, T1])
                m["gateT"] = sb(mid, "gateT", [P, 16, T1])
                loads = [(self.h[:, t, :], A["x"][0, t * P:(t + 1) * P, :]) for t in range(TT)]
                loads += [(self.h[0:META, TT, :], A["meta_tokens"]), (self.ident[:], self.const(1, "ident"))]
                self.s5_prepare(m, loads)
                with ExitStack() as n1:
                    g1 = sb(n1, "g1", [P, D])
                    self.norm_stage("n1", TILES1, self.h, None, m["hT"], "rms", g1, None, EPS,
                                    loads=[(g1[:], A["norm1_g"][0].partition_broadcast(P))])
                self.project_and_s5(m)
                if stop == "s5":
                    return
                m["v"] = sb(mid, "v", [P, TT + 1, ATT])
                m["oT"] = sb(mid, "oT", [P, H1, T1])
                m["alibi"] = sb(mid, "alibi", [P, T1])
                m["mlam"] = sb(mid, "mlam", [P, 1])
                self.recycle_semaphores()
                self.qk_norm_stage(m)
                self.diff_attention(m)
                self.mix_stage(m)
            if stop == "mix":
                return
            with ExitStack() as n2:
                g2 = sb(n2, "g2", [P, D])
                self.norm_stage("n2", TILES1, self.h, None, m["hT"], "rms", g2, None, EPS,
                                loads=[(g2[:], A["norm2_g"][0].partition_broadcast(P))])
            gT = sb(ctx, "ffgT", [P, FT, SEQ])
            self.ffn_stage(m["hT"], gT)

    def gla_project(self, m):
        nc, ps, W, A = self.nc, self.ps, self.W, self.A
        with self.new_stage() as ctx:
            sb = self.sb
            xT, qd, kn, kt = m["xT"], m["qd"], m["kn"], m["kt"]
            glow = sb(ctx, "gl_low", [16, SEQ])
            wup = sb(ctx, "gl_wup", [16, 512])
            bg = sb(ctx, "gl_bg", [P, GH])
            one = sb(ctx, "gl_one", [P, 1])
            restart = sb(ctx, "gl_restart", [P, SEQ])
            X, mn, e = (sb(ctx, n, [P, GH, SEQ]) for n in ("gl_x", "gl_mn", "gl_e"))
            loaded, start, qk_done, qk_out, low_done, low_out, z_done, z_out, e_done, cs_done, eb_done, dd_done, et_done, \
                v_done, v_out, r_done, r_out, own, actown = self.sems(
                    "gp", "loaded", "start", "qk_done", "qk_out", "low_done", "low_out", "z_done", "z_out", "e_done",
                    "cs_done", "eb_done", "dd_done", "et_done", "v_done", "v_out", "r_done", "r_out", "own", "act_own")
            loads = [(wup[:], A["gla_w_gate_up_2"][0]), (bg[:], A["gla_b_gate_2"].rearrange("o (t p) -> p (o t)", p=P)),
                     (restart[:], self.const(2, "restart"))]
            block = ctx.enter_context(nc.Block())

            @block.tensor
            def _(pe):
                for i in range(8):
                    n = self.n_gqk[i // 2]
                    W.arrived(pe, n)
                    self.fm_product(n, KD, 256, (i % 2) * P, lambda k, a, b: xT[:, k, a:b], [(i, 0, SEQ)], qk_done)
                    if i % 2:
                        W.retired_by(n, qk_done, i + 1)
                n = self.n_glow[0]
                W.arrived(pe, n)
                pe.wait_ge(qk_out, 1)
                self.fm_product(n, KD, 16, 0, lambda k, a, b: xT[:, k, a:b], [(0, 0, SEQ)], low_done, m=16)
                W.retired_by(n, low_done, 1)
                pe.wait_ge(low_out, 1)
                pe.wait_ge(loaded, 16 * len(loads))
                for hd in range(GH):
                    pe.wait_ge(qk_out, hd + 2)
                    nc.tensor.matmul(ps[:, 1 + hd, :], wup[:, hd * P:(hd + 1) * P], glow[:], start=True, stop=True)\
                        .then_inc(z_done, 1)
                pe.wait_ge(qk_out, 8)
                pe.wait_ge(z_out, GH)
                self.tm_product(pe, self.n_gv, lambda k, t: xT[:, k, P * t:P * (t + 1)], v_done)
                self.tm_product(pe, self.n_gr, lambda k, t: xT[:, k, P * t:P * (t + 1)], r_done,
                                bank_free=lambda t: pe.wait_ge(v_out, t + 1))

            @block.scalar
            def _(act):
                for to, frm in loads:
                    act.dma_start(to, frm).then_inc(loaded, 16)
                act.wait_ge(start, 1)
                for i in range(8):
                    act.wait_ge(qk_done, i + 1)
                    nc.scalar.copy((qd if i < 4 else kt)[:, i % 4, :], ps[:, i, :]).then_inc(qk_out, 1)
                act.wait_ge(low_done, 1)
                nc.scalar.copy(glow[:], ps[0:16, 0, :]).then_inc(low_out, 1)
                link = Chain(act, actown)
                for hd in range(GH):
                    act.wait_ge(z_out, hd + 1)
                    link(nc.scalar.activation(e[:, hd], e[:, hd], ACT.Exp, scale=-1.0))
                    nc.scalar.activation(e[:, hd], e[:, hd], ACT.Ln, bias=one[:]).then_inc(e_done, 1)
                for hd in range(GH):
                    act.wait_ge(cs_done, hd + 1)
                    nc.scalar.activation(e[:, hd], X[:, hd], ACT.Exp, scale=1 / 16).then_inc(eb_done, 1)
                    act.wait_ge(dd_done, hd + 1)
                    nc.scalar.activation(kn[:, hd], X[:, hd], ACT.Exp, scale=-1 / 16).then_inc(eb_done, 1)
                    nc.scalar.activation(mn[:, hd], mn[:, hd], ACT.Exp, scale=-1 / 16).then_inc(et_done, 1)
                for t in range(TT):
                    act.wait_ge(v_done, t + 1)
                    nc.scalar.copy(m["v"][:, t, :].rearrange("p (a c) -> p a c", a=2), ps[:, 2 * t:2 * t + 2, :])\
                        .then_inc(v_out, 1)
                for t in range(TT):
                    act.wait_ge(r_done, t + 1)
                    nc.scalar.activation(m["r"][:, t, :].rearrange("p (a c) -> p a c", a=2), ps[:, 2 * t:2 * t + 2, :],
                                         ACT.Silu).then_inc(r_out, 1)

            @block.vector
            def _(dve):
                link = Chain(dve, own)
                V = nc.vector
                V.memset(one[:], 1.0).then_inc(start, 1)
                dve.wait_ge(loaded, 16 * len(loads))
                for hd in range(GH):
                    dve.wait_ge(z_done, hd + 1)
                    link(V.tensor_scalar(X[:, hd], ps[:, 1 + hd, :], bg[:, hd:hd + 1], None, ALU.add))
                    link(V.tensor_scalar(mn[:, hd], X[:, hd], 0.0, None, ALU.min))
                    V.scalar_tensor_tensor(e[:, hd], mn[:, hd], -2.0, X[:, hd], ALU.mult, ALU.add).then_inc(z_out, 1)
                for hd in range(GH):
                    dve.wait_ge(e_done, hd + 1)
                    dve.wait_ge(z_out, GH)
                    link(V.tensor_tensor(mn[:, hd], mn[:, hd], e[:, hd], ALU.subtract))
                    V.tensor_tensor_scan(X[:, hd], restart[:], mn[:, hd], 0.0, ALU.mult, ALU.add).then_inc(cs_done, 1)
                    dve.wait_ge(cs_done, hd + 1)
                    c3 = X[:, hd].rearrange("p (n t) -> p n t", t=64)
                    V.tensor_tensor(mn[:, hd].rearrange("p (n t) -> p n t", t=64), c3,
                                    c3[:, :, 63:64].broadcast_to([P, 8, 64]), ALU.subtract).then_inc(dd_done, 1)
                dve.wait_ge(qk_out, 8)
                for hd in range(GH):
                    dve.wait_ge(eb_done, 2 * hd + 2)
                    V.tensor_copy(m["dec"][:, hd, :], e[:, hd].rearrange("p (n t) -> p n t", t=64)[:, :, 63]).then_inc(own, 1)
                    V.scalar_tensor_tensor(qd[:, hd], qd[:, hd], float(P) ** -0.5, e[:, hd], ALU.mult, ALU.mult).then_inc(own, 1)
                    V.tensor_tensor(kn[:, hd], kt[:, hd], kn[:, hd], ALU.mult).then_inc(own, 1)
                    link.n += 3
                    dve.wait_ge(own, link.n)
                    dve.wait_ge(et_done, hd + 1)
                    link(V.tensor_tensor(kt[:, hd], kt[:, hd], mn[:, hd], ALU.mult))

            @block.sync
            def _(sp):
                W.send(sp)

    def gla_chunks(self, m):
        nc, ps, W = self.nc, self.ps, self.W
        with self.new_stage() as ctx:
            sb = self.sb
            qd, kn, kt, v, o = m["qd"], m["kn"], m["kt"], m["v"], m["o"]
            ktok = sb(ctx, "gl_ktok", [P, TT, 512])
            S = sb(ctx, "gl_S", [P, 4, 64])
            state = sb(ctx, "gl_state", [P, 2, GH, 256])
            mask = sb(ctx, "gl_mask", [P, 64])
            loaded, zeroed, kt_done, kt_out, s_done, s_out, kv_done, st_done, o_done, o_out = self.sems(
                "gc", "loaded", "zeroed", "kt_done", "kt_out", "s_done", "s_out", "kv_done", "st_done", "o_done", "o_out")
            units = [(n, hd) for n in range(8) for hd in range(GH)]
            N = len(units)
            block = ctx.enter_context(nc.Block())

            def rows(n):
                return slice(64 * (n % 2), 64 * (n % 2) + 64)

            @block.tensor
            def _(pe):
                for t in range(TT):
                    for hd in range(GH):
                        ins = nc.tensor.transpose(ps[:, t, hd * P:(hd + 1) * P], kt[:, hd, t * P:(t + 1) * P], self.ident[:])
                    ins.then_inc(kt_done, 1)
                pe.wait_ge(kt_out, TT)
                for it in range(N + 2):
                    if it < N:
                        n, hd = units[it]
                        c = slice(64 * n, 64 * n + 64)
                        if it >= 2:
                            pe.wait_ge(s_out, it - 1)
                        nc.tensor.matmul(ps[rows(n), it % 2, 0:64], kn[:, hd, c], qd[:, hd, c], start=True, stop=True)\
                            .then_inc(s_done, 1)
                        if it >= 2:
                            pe.wait_ge(st_done, it - 1)
                        nc.tensor.matmul(ps[:, 6 + it % 2, 0:256], ktok[rows(n), n // 2, hd * P:(hd + 1) * P],
                                         v[rows(n), n // 2, 256 * hd:256 * hd + 256], start=True, stop=True)\
                            .then_inc(kv_done, 1)
                    u = it - 2
                    if u >= 0:
                        n, hd = units[u]
                        pe.wait_ge(s_out, u + 1)
                        if n >= 2:
                            pe.wait_ge(o_out, GH * (n // 2 - 1) + hd + 1)
                        dst = ps[rows(n), 2 + hd, 0:256]
                        ins = nc.tensor.matmul(dst, S[rows(n), u % 4, :], v[rows(n), n // 2, 256 * hd:256 * hd + 256],
                                               start=True, stop=(n == 0))
                        if n:
                            pe.wait_ge(st_done, u - 3)
                            ins = nc.tensor.matmul(dst, qd[:, hd, 64 * n:64 * n + 64], state[:, n % 2, hd, :],
                                                   start=False, stop=True)
                        ins.then_inc(o_done, 1)

            @block.scalar
            def _(act):
                act.dma_start(mask[:], self.const(2, "glamask")).then_inc(loaded, 16)
                for t in range(TT):
                    act.wait_ge(kt_done, t + 1)
                    nc.scalar.copy(ktok[:, t, :], ps[:, t, :]).then_inc(kt_out, 1)
                for t in range(TT):
                    for hd in range(GH):
                        act.wait_ge(o_done, GH * (2 * t + 1) + hd + 1)
                        nc.scalar.copy(o[:, t, 256 * hd:256 * hd + 256], ps[:, 2 + hd, 0:256])\
                            .then_inc(o_out, 1)

            @block.vector
            def _(dve):
                V = nc.vector
                V.memset(S[:], 0.0).then_inc(zeroed, 1)
                dve.wait_ge(zeroed, 1)
                dve.wait_ge(loaded, 16)
                for it in range(N):
                    n, hd = units[it]
                    dve.wait_ge(s_done, it + 1)
                    if it >= 4:
                        dve.wait_ge(o_done, it - 3)
                    V.copy_predicated(S[rows(n), it % 4, :], mask[rows(n), :].bitcast(U32), ps[rows(n), it % 2, 0:64])\
                        .then_inc(s_out, 1)
                    dve.wait_ge(kv_done, it + 1)
                    new = state[:, (n + 1) % 2, hd, :]
                    if n == 0:
                        V.tensor_copy(new, ps[:, 6 + it % 2, 0:256]).then_inc(st_done, 1)
                    else:
                        dve.wait_ge(st_done, it - 3)
                        if n >= 2:
                            dve.wait_ge(o_done, it - 3)
                        V.scalar_tensor_tensor(new, state[:, n % 2, hd, :], m["dec"][:, hd, n:n + 1],
                                               ps[:, 6 + it % 2, 0:256], ALU.mult, ALU.add).then_inc(st_done, 1)

            @block.sync
            def _(sp):
                W.send(sp)

    def gla_out(self, m):
        nc, ps, W, A, h = self.nc, self.ps, self.W, self.A, self.h
        with self.new_stage() as ctx:
            sb = self.sb
            o, oT = m["o"], m["xT"]
            junk = sb(ctx, "go_junk", [P, 256])
            st = sb(ctx, "go_st", [P, 3, 16])
            gn = sb(ctx, "go_gn", [P, 256])
            eps = sb(ctx, "go_eps", [P, 1])
            loaded, start, rs, o_ready, turned, t_out, y_done, y_out, own, actown = self.sems(
                "go", "loaded", "start", "rs", "o_ready", "turned", "t_out", "y_done", "y_out", "own", "act_own")
            block = ctx.enter_context(nc.Block())

            @block.tensor
            def _(pe):
                for t in range(TT):
                    pe.wait_ge(o_ready, t + 1)
                    for k in range(KD):
                        ins = nc.tensor.transpose(ps[:, 2 * t + k // 4, (k % 4) * P:(k % 4) * P + P], o[:, t, k * P:(k + 1) * P],
                                                  self.ident[:])
                    ins.then_inc(turned, 1)
                pe.wait_ge(t_out, TT)
                self.tm_product(pe, self.n_go, lambda k, t: oT[:, k, P * t:P * (t + 1)], y_done)

            @block.scalar
            def _(act):
                act.dma_start(gn[:], A["gla_norm_g_2"][0].partition_broadcast(P)).then_inc(loaded, 16)
                act.wait_ge(start, 1)
                link = Chain(act, actown)
                for t in range(TT):
                    for hd in range(GH):
                        link(nc.scalar.activation(junk[:], o[:, t, 256 * hd:256 * hd + 256], ACT.Square,
                                                  accum_out=st[:, 0, 4 * t + hd:4 * t + hd + 1]))
                link(nc.scalar.activation(st[:, 1], st[:, 0], ACT.Ln, bias=eps[:], scale=1 / 256))
                nc.scalar.activation(st[:, 2], st[:, 1], ACT.Exp, scale=-0.5).then_inc(rs, 1)
                for t in range(TT):
                    act.wait_ge(turned, t + 1)
                    nc.scalar.copy(oT[:, :, P * t:P * (t + 1)],
                                   ps[:, 2 * t:2 * t + 2, :].rearrange("p b (k c) -> p (b k) c", k=4)).then_inc(t_out, 1)

            @block.vector
            def _(dve):
                link = Chain(dve, own)
                V = nc.vector
                V.memset(eps[:], LN_EPS).then_inc(start, 1)
                dve.wait_ge(loaded, 16)
                dve.wait_ge(rs, 1)
                for t in range(TT):
                    for hd in range(GH):
                        x = o[:, t, 256 * hd:256 * hd + 256]
                        link(V.scalar_tensor_tensor(x, x, st[:, 2, 4 * t + hd:4 * t + hd + 1], gn[:], ALU.mult, ALU.mult))
                    V.tensor_tensor(o[:, t, :], o[:, t, :], m["r"][:, t, :], ALU.mult).then_inc(o_ready, 1)
                for t in range(TT):
                    dve.wait_ge(y_done, t + 1)
                    x = h[:, t, :].rearrange("p (a c) -> p a c", a=2)
                    V.scalar_tensor_tensor(x, x, ALPHA, ps[:, 2 * t:2 * t + 2, :], ALU.mult, ALU.add).then_inc(y_out, 1)

            @block.sync
            def _(sp):
                W.send(sp)

    def moe_stage(self, tag, groups, xT, pick):
        nc, ps, W, A, h = self.nc, self.ps, self.W, self.A, self.h
        with self.new_stage() as ctx:
            sb = self.sb
            wr = sb(ctx, tag + "_wr", [P, KD, NE])
            br = sb(ctx, tag + "_br", [P, NE])
            s, biased, sel, w, gate = (sb(ctx, f"{tag}_{n}", [P, TT * NE]) for n in ("s", "biased", "sel", "w", "gate"))
            beats = sb(ctx, tag + "_beats", [P, 4, 16, 4])
            gs = sb(ctx, tag + "_gs", [P, 16])
            gsel = sb(ctx, tag + "_gsel", [P, 16])
            ws = sb(ctx, tag + "_ws", [P, 2, TT])
            gateT = sb(ctx, tag + "_gateT", [NE, SEQ])
            sg, t1 = (sb(ctx, f"{tag}_{n}", [P, 2, SEQ]) for n in ("sg", "t1"))
            hT = sb(ctx, tag + "_hT", [P, 2 * EG, SEQ])
            loaded, lg_done, s_out, gate_done, gt_done, gt_out, gu_done, b_done, sg_out, h_done, y_done, y_out, own = self.sems(
                tag, "loaded", "lg_done", "s_out", "gate_done", "gt_done", "gt_out", "gu_done", "b_done", "sg_out",
                "h_done", "y_done", "y_out", "own")
            loads = [(wr[:], A["moe_w_router_2"].rearrange("(k p) e -> p k e", p=P)),
                     (br[:], A["moe_b_router_2"].partition_broadcast(P))]
            NGR = len(groups)
            block = ctx.enter_context(nc.Block())

            @block.tensor
            def _(pe):
                pe.wait_ge(loaded, 16 * len(loads))
                for t in range(TT):
                    for k in range(KD):
                        ins = nc.tensor.matmul(ps[:, 0, NE * t:NE * (t + 1)], xT[:, k, P * t:P * (t + 1)], wr[:, k, :],
                                               start=(k == 0), stop=(k == KD - 1))
                ins.then_inc(lg_done, 1)
                pe.wait_ge(gate_done, 1)
                for t in range(TT):
                    ins = nc.tensor.transpose(ps[0:NE, 7, P * t:P * (t + 1)], gate[:, NE * t:NE * (t + 1)], self.ident[:])
                ins.then_inc(gt_done, 1)
                for g, (gu, dn) in enumerate(groups):
                    for e, slabs in enumerate(gu):
                        ee = g * EG + e
                        for i in range(2):
                            y = 2 * ee + i
                            if e == 0 and g:
                                pe.wait_ge(y_out, TT * (g - 1) + i + 1)
                            if y >= 2:
                                pe.wait_ge(h_done, y - 1)
                            else:
                                pe.wait_ge(s_out, 1)
                            b = 2 * (y % 2)
                            for j, n in enumerate(slabs):
                                W.arrived(pe, n)
                                self.fm_product(n, KD, 256, i * P, lambda k, a, c: xT[:, k, a:c], [(b + j, 0, SEQ)], gu_done)
                                if i == 1:
                                    W.retired_by(n, gu_done, 2 * y + j + 1)
                            if i == 0:
                                if e == 0 and g:
                                    pe.wait_ge(y_out, TT * (g - 1) + 3)
                                if ee == 0:
                                    pe.wait_ge(gt_out, 1)
                                nc.tensor.matmul(ps[:, 4 + ee % 2, :], pick[:, ee, :], gateT[:], start=True, stop=True)\
                                    .then_inc(b_done, 1)
                    pe.wait_ge(h_done, 2 * EG * (g + 1))
                    if g:
                        pe.wait_ge(y_out, TT * g)
                    self.tm_product(pe, dn, lambda k, t: hT[:, k, P * t:P * (t + 1)], y_done, before=TT * g)

            @block.scalar
            def _(act):
                for to, frm in loads:
                    act.dma_start(to, frm).then_inc(loaded, 16)
                act.wait_ge(lg_done, 1)
                nc.scalar.activation(s[:], ps[:, 0, 0:TT * NE], ACT.Sigmoid).then_inc(s_out, 1)
                for y in range(2 * NE):
                    act.wait_ge(gu_done, 2 * y + 1)
                    if y >= 2:
                        act.wait_ge(h_done, y - 1)
                    nc.scalar.activation(sg[:, y % 2], ps[:, 2 * (y % 2), :], ACT.Silu).then_inc(sg_out, 1)

            @block.vector
            def _(dve):
                link = Chain(dve, own)
                V = nc.vector

                def rank(dst, x, n, below):
                    link(V.memset(beats[:, :, 0:n, :], 0.0))
                    for c in range(4):
                        for a, b, op in ((0, c, ALU.is_gt), (c + 1, 4, ALU.is_ge)):
                            if a < b:
                                link(V.tensor_tensor(beats[:, c, 0:n, a:b], x[:, :, c:c + 1].broadcast_to([P, n, b - a]),
                                                     x[:, :, a:b], op))
                    for c in range(1, 4):
                        link(V.tensor_tensor(beats[:, 0, 0:n, :], beats[:, 0, 0:n, :], beats[:, c, 0:n, :], ALU.add))
                    link(V.tensor_scalar(dst, beats[:, 0, 0:n, :], below, None, ALU.is_lt))

                def by4(x, n=16):
                    return x[:].rearrange("p (a b) -> p a b", a=n)

                dve.wait_ge(loaded, 16 * len(loads))
                dve.wait_ge(s_out, 1)
                link(V.tensor_tensor(by4(biased, TT), by4(s, TT), br[:].unsqueeze(1).broadcast_to([P, TT, NE]), ALU.add))
                rank(by4(sel), by4(biased), 16, 2.0)
                link(V.tensor_tensor(w[:], sel[:], biased[:], ALU.mult))
                link(V.reduce_sum(gs[:], by4(w), AX.X))
                rank(by4(gsel, 4), by4(gs, 4), 4, 1.0)
                link(V.tensor_tensor(w[:], sel[:], s[:], ALU.mult))
                link(V.tensor_tensor(by4(w), by4(w), gsel[:].unsqueeze(2).broadcast_to([P, 16, 4]), ALU.mult))
                link(V.reduce_sum(ws[:, 0], by4(w, TT), AX.X))
                link(V.reciprocal(ws[:, 1], ws[:, 0]))
                V.tensor_tensor(by4(gate, TT), by4(w, TT), ws[:, 1].unsqueeze(2).broadcast_to([P, TT, NE]), ALU.mult)\
                    .then_inc(gate_done, 1)
                dve.wait_ge(gt_done, 1)
                V.tensor_copy(gateT[:], ps[0:NE, 7, :]).then_inc(gt_out, 1)
                for y in range(2 * NE):
                    g, u = divmod(y, 2 * EG)
                    dve.wait_ge(sg_out, y + 1)
                    dve.wait_ge(gu_done, 2 * y + 2)
                    dve.wait_ge(b_done, y // 2 + 1)
                    if y:
                        dve.wait_ge(h_done, y)
                    link(V.tensor_tensor(t1[:, y % 2], sg[:, y % 2], ps[:, 2 * (y % 2) + 1, :], ALU.mult))
                    V.tensor_tensor(hT[:, u, :], t1[:, y % 2], ps[:, 4 + (y // 2) % 2, :], ALU.mult).then_inc(h_done, 1)
                    if u == 2 * EG - 1:
                        for t in range(TT):
                            dve.wait_ge(y_done, TT * g + t + 1)
                            if g:
                                dve.wait_ge(y_out, TT * (g - 1) + t + 1)
                            x = h[:, t, :].rearrange("p (a c) -> p a c", a=2)
                            V.scalar_tensor_tensor(x, x, ALPHA if g == 0 else 1.0, ps[:, 2 * t:2 * t + 2, :],
                                                   ALU.mult, ALU.add).then_inc(y_out, 1)

            @block.sync
            def _(sp):
                W.send(sp)

    def second_block(self, out, stop=None):
        A, sb = self.A, self.sb
        with ExitStack() as ctx:
            xT = sb(ctx, "xT", [P, KD, SEQ])
            pick = sb(ctx, "pick", [NE, NE, P])
            g, b = sb(ctx, "ln_g", [P, D]), sb(ctx, "ln_b", [P, D])
            h = self.h

            def ln_loads(i, j):
                return [(g[:], A["ln_g_2"][i, j].partition_broadcast(P)), (b[:], A["ln_b_2"][i, j].partition_broadcast(P))]

            pa, pb = self.p2["pick"]
            self.recycle_semaphores()
            self.norm_stage("x0", TILES2, h, None, xT, None, None, None, 0.0)
            with ExitStack() as gl:
                m = {"xT": xT, "qd": sb(gl, "qd", [P, GH, SEQ]), "kn": sb(gl, "kn", [P, GH, SEQ]),
                     "kt": sb(gl, "kt", [P, GH, SEQ]), "v": sb(gl, "gv", [P, TT, D]), "r": sb(gl, "gr", [P, TT, D]),
                     "dec": sb(gl, "dec", [P, GH, 8])}
                self.gla_project(m)
                m["o"] = sb(gl, "go", [P, TT, D])
                self.gla_chunks(m)
                self.gla_out(m)
            if stop == "gla":
                return
            pick_load = [(pick[:], A["const2"][0:NE, pa:pb].rearrange("p (e c) -> p e c", e=NE))]
            self.norm_stage("l0", TILES2, h, h, xT, "ln", g, b, LN_EPS, loads=ln_loads(0, 0) + pick_load)
            if stop == "ln0":
                return
            self.moe_stage("m0", self.n_moe[0], xT, pick)
            if stop == "moe0":
                return
            self.recycle_semaphores()
            self.norm_stage("l1", TILES2, h, h, xT, "ln", g, b, LN_EPS, loads=ln_loads(0, 1))
            self.nsa(xT)
            if stop == "nsa":
                return
            self.recycle_semaphores()
            self.norm_stage("l2", TILES2, h, h, xT, "ln", g, b, LN_EPS, loads=ln_loads(1, 0))
            self.moe_stage("m1", self.n_moe[1], xT, pick)
            self.norm_stage("l3", TILES2, h, h, None, "ln", g, b, LN_EPS, loads=ln_loads(1, 1), to_dram=out[0])

    def nsa(self, xT):
        A, sb, h = self.A, self.sb, self.h
        with ExitStack() as ctx:
            m = {"xT": xT, "qT": sb(ctx, "nqT", [P, KD, SEQ]), "kd": sb(ctx, "nkd", [P, 2, NG, SEQ]),
                 "vsw": sb(ctx, "nvsw", [P, TT, 512]), "gates": sb(ctx, "ngates", [P, TT, 48]),
                 "kcT": sb(ctx, "nkcT", [P, 2, 2, NCMP]), "vc": sb(ctx, "nvc", [NCMP, NG, 64])}
            with ExitStack() as cc:
                m["kc"] = sb(cc, "nkc", [P, 2, 2, 2, SEQ])
                self.nsa_project(m)
                self.nsa_compress(m)
            self.nsa_attention(m)
            self.nsa_out(m)

    def nsa_project(self, m):
        nc, ps, W, A = self.nc, self.ps, self.W, self.A
        with self.new_stage() as ctx:
            sb = self.sb
            xT, kd = m["xT"], m["kd"]
            raw = sb(ctx, "np_raw", [P, 2, SEQ])
            t2 = sb(ctx, "np_t2", [P, 2, SEQ])
            cos, sin = sb(ctx, "np_cos", [P, SEQ]), sb(ctx, "np_sin", [P, SEQ])
            swap = sb(ctx, "np_swap", [P, P])
            pe_ = sb(ctx, "np_pe", [P, 32])
            anyb = sb(ctx, "np_any", [P, TT])
            loaded, pr_done, raw_out, sw_done, rope_done, kc_out, v_done, v_out, g_done, g_out, dup, own, cosd = self.sems(
                "np", "loaded", "pr_done", "raw_out", "sw_done", "rope_done", "kc_out", "v_done", "v_out", "g_done",
                "g_out", "dup", "own", "cos_done")
            loads = [(cos[:], self.const(2, "cos")), (sin[:], self.const(2, "sin")), (swap[:], self.const(2, "swap")),
                     (anyb[:], self.const(2, "cmpany"))]
            loads += [(pe_[64 * g:64 * g + 64, :], A["nsa_cmp_pe_2"].rearrange("o t d -> d (o t)")) for g in range(2)]
            rope = [(self.n_nq[i // 2], i % 2, ("q", i)) for i in range(8)]
            flat = [(self.n_nkv[j], i, (j, i)) for j in range(2) for i in range(2)]
            rope2 = [(self.n_nkv[2 + j], i, ("k", j, i)) for j in range(2) for i in range(2)]
            tiles = [("rope", *x) for x in rope] + [("flat", *x) for x in flat] + [("rope", *x) for x in rope2]
            NT = len(tiles)
            nrope = [sum(t[0] == "rope" for t in tiles[:i]) for i in range(NT + 1)]
            block = ctx.enter_context(nc.Block())

            @block.tensor
            def _(pe):
                for it in range(NT + 1):
                    if it < NT:
                        kind, n, i, what = tiles[it]
                        W.arrived(pe, n)
                        if it >= 4:
                            r = nrope[it - 3]
                            if r:
                                pe.wait_ge(raw_out, r)
                            if it - 3 - r:
                                pe.wait_ge(kc_out, it - 3 - r)
                        self.fm_product(n, KD, 256, i * P, lambda k, a, b: xT[:, k, a:b], [(it % 4, 0, SEQ)], pr_done)
                        if i:
                            W.retired_by(n, pr_done, it + 1)
                    u = it - 1
                    if u >= 0 and tiles[u][0] == "rope":
                        r = nrope[u]
                        if r == 0:
                            pe.wait_ge(loaded, 16 * len(loads))
                        pe.wait_ge(raw_out, r + 1)
                        if r >= 2:
                            pe.wait_ge(rope_done, r - 1)
                        nc.tensor.matmul(ps[:, 4 + r % 2, :], swap[:], raw[:, r % 2], start=True, stop=True)\
                            .then_inc(sw_done, 1)
                for t in range(TT):
                    bank = (6 + t) % 8
                    if t == 2:
                        pe.wait_ge(raw_out, nrope[NT])
                        pe.wait_ge(kc_out, 4)
                    for j, n in enumerate(self.n_nv):
                        W.arrived(pe, n)
                        v = slab_view(KD, 256)(W.slot(n))
                        for k in range(KD):
                            ins = nc.tensor.matmul(ps[:, bank, 256 * j:256 * j + 256], xT[:, k, P * t:P * (t + 1)], v[:, k, :],
                                                   start=(k == 0), stop=(k == KD - 1))
                    ins.then_inc(v_done, 1)
                for n in self.n_nv:
                    W.retired_by(n, v_done, TT)
                W.arrived(pe, self.n_gate)
                v = slab_view(KD, 48)(W.slot(self.n_gate))
                for t in range(TT):
                    for k in range(KD):
                        ins = nc.tensor.matmul(ps[:, 2, 48 * t:48 * t + 48], xT[:, k, P * t:P * (t + 1)], v[:, k, :],
                                               start=(k == 0), stop=(k == KD - 1))
                ins.then_inc(g_done, 1)
                W.retired_by(self.n_gate, g_done, 1)

            @block.scalar
            def _(act):
                for to, frm in loads:
                    act.dma_start(to, frm).then_inc(loaded, 16)
                for it, (kind, n, i, what) in enumerate(tiles):
                    if kind == "rope":
                        r = nrope[it]
                        act.wait_ge(pr_done, it + 1)
                        if r >= 2:
                            act.wait_ge(cosd, r - 1)
                            act.wait_ge(sw_done, r - 1)
                        nc.scalar.copy(raw[:, r % 2], ps[:, it % 4, :]).then_inc(raw_out, 1)
                for t in range(TT):
                    act.wait_ge(v_done, t + 1)
                    nc.scalar.copy(m["vsw"][:, t, :], ps[:, (6 + t) % 8, :]).then_inc(v_out, 1)
                act.wait_ge(g_done, 1)
                nc.scalar.activation(m["gates"][:].rearrange("p t c -> p (t c)"), ps[:, 2, 0:48 * TT], ACT.Sigmoid)\
                    .then_inc(g_out, 1)

            @block.vector
            def _(dve):
                link = Chain(dve, own)
                V = nc.vector
                dve.wait_ge(loaded, 16 * len(loads))
                flats = 0
                for it, (kind, n, i, what) in enumerate(tiles):
                    if kind == "flat":
                        dve.wait_ge(pr_done, it + 1)
                        src = ps[:, it % 4, :].rearrange("p (n t) -> p n t", t=16)
                        for half in range(2):
                            ins = V.tensor_tensor(m["kc"][:, what[0], half, what[1], :].rearrange("p (n t) -> p n t", t=16), src,
                                                  pe_[:, 16 * half:16 * half + 16].unsqueeze(1).broadcast_to([P, 32, 16]), ALU.add)
                            if half:
                                ins.then_inc(kc_out, 1)
                            else:
                                link(ins)
                        continue
                    r = nrope[it]
                    s = r % 2
                    scale = 0.125 if what[0] == "q" else 1.0
                    dve.wait_ge(raw_out, r + 1)
                    if r:
                        dve.wait_ge(rope_done, r)
                    V.scalar_tensor_tensor(t2[:, 0], raw[:, s], scale, cos[:], ALU.mult, ALU.mult).then_inc(cosd, 1)
                    dve.wait_ge(sw_done, r + 1)
                    link(V.scalar_tensor_tensor(t2[:, 1], ps[:, 4 + s, :], scale, sin[:], ALU.mult, ALU.mult))
                    dve.wait_ge(cosd, r + 1)
                    if what[0] == "q":
                        V.tensor_tensor(m["qT"][:, what[1], :], t2[:, 0], t2[:, 1], ALU.add).then_inc(rope_done, 1)
                    else:
                        for g in range(2):
                            q = slice(64 * g, 64 * g + 64)
                            ins = V.tensor_tensor(kd[q, what[1], 2 * what[2] + g, :], t2[q, 0], t2[q, 1], ALU.add)
                            if g:
                                ins.then_inc(rope_done, 1)
                            else:
                                link(ins)
                dve.wait_ge(g_out, 1)
                g4 = m["gates"][:].rearrange("p t (h c) -> p t h c", c=3)
                V.tensor_tensor(g4[:, :, :, 0], g4[:, :, :, 0], anyb[:].unsqueeze(2).broadcast_to([P, TT, NH]), ALU.mult)\
                    .then_inc(g_out, 1)

            @block.sync
            def _(sp):
                W.send(sp)
                for j in range(2):
                    for i in range(2):
                        sp.wait_ge(rope_done, 8 + 2 * j + i + 1)
                        for g in range(2):
                            a, b = slice(64 * g, 64 * g + 64), slice(64 - 64 * g, 128 - 64 * g)
                            sp.dma_start(kd[b, j, 2 * i + g, :], kd[a, j, 2 * i + g, :]).then_inc(dup, 16)
                sp.wait_ge(dup, 16 * 8)

    def nsa_compress(self, m):
        nc, ps, W, A = self.nc, self.ps, self.W, self.A
        with self.new_stage() as ctx:
            sb = self.sb
            C2 = 2 * NCMP
            h1 = sb(ctx, "cm_h1", [P, 2, 2, 2, C2])
            w2k = sb(ctx, "cm_w2k", [P, 2, P])
            w2v = sb(ctx, "cm_w2v", [P, 2, 64])
            raw = sb(ctx, "cm_raw", [P, 2 * C2])
            t1 = sb(ctx, "cm_t1", [P, 2 * C2])
            cs = sb(ctx, "cm_cs", [P, 2 * NCMP])
            swap = sb(ctx, "cm_swap", [P, P])
            loaded, h_done, h_out, k_done, k_out, sw_done, v_done, v_out, own = self.sems(
                "cm", "loaded", "h_done", "h_out", "k_done", "k_out", "sw_done", "v_done", "v_out", "own")
            w2 = A["nsa_w_cmp_k2_2"][0].rearrange("(k p) d -> p k d", p=P)
            loads = [(w2k[:, :, 0:64], w2), (w2k[:, :, 64:128], w2),
                     (w2v[:], A["nsa_w_cmp_v2_2"][0].rearrange("(k p) d -> p k d", p=P)),
                     (cs[:, 0:NCMP], self.const(2, "coscmp")), (cs[:, NCMP:2 * NCMP], self.const(2, "sincmp")),
                     (swap[:], self.const(2, "swap"))]
            kc = m["kc"]
            block = ctx.enter_context(nc.Block())

            @block.tensor
            def _(pe):
                for kv in range(2):
                    for q in range(4):
                        n = self.n_cmp[kv][q]
                        W.arrived(pe, n)
                        w = slab_view(8, 256)(W.slot(n))
                        for p8 in range(8):
                            pos = 8 * q + p8
                            half, p16 = divmod(pos, 16)
                            for par in range(2):
                                r = slice(64 * par, 64 * par + 64)
                                x = kc[r, kv, half].rearrange("p u (n t) -> p u n t", t=16)[:, :, half:half + NCMP, p16]
                                for hd in range(2):
                                    ins = nc.tensor.matmul(ps[:, 4 * kv + 2 * hd + par, 0:C2], w[r, p8, hd * P:(hd + 1) * P], x,
                                                           start=(pos == 0), stop=(pos == 31))
                        if q < 3:
                            W.retire(n, ins)
                        else:
                            ins.then_inc(h_done, 1)
                            W.retired_by(n, h_done, kv + 1)
                pe.wait_ge(loaded, 16 * len(loads))
                pe.wait_ge(h_out, 1)
                for k in range(2):
                    ins = nc.tensor.matmul(ps[:, 0, 0:2 * C2], w2k[:, k, :], h1[:, 0, k].rearrange("p a c -> p (a c)"),
                                           start=(k == 0), stop=(k == 1))
                ins.then_inc(k_done, 1)
                pe.wait_ge(h_out, 2)
                for g in range(NG):
                    par, u = g % 2, g // 2
                    for k in range(2):
                        ins = nc.tensor.matmul(ps[0:NCMP, 1, 64 * g:64 * g + 64], h1[:, 1, k, par, NCMP * u:NCMP * (u + 1)],
                                               w2v[:, k, :], start=(k == 0), stop=(k == 1))
                ins.then_inc(v_done, 1)
                pe.wait_ge(k_out, 1)
                nc.tensor.matmul(ps[:, 2, 0:2 * C2], swap[:], raw[:], start=True, stop=True).then_inc(sw_done, 1)

            @block.scalar
            def _(act):
                for to, frm in loads:
                    act.dma_start(to, frm).then_inc(loaded, 16)
                for kv in range(2):
                    act.wait_ge(h_done, kv + 1)
                    nc.scalar.activation(h1[:, kv].rearrange("p k a c -> p (k a) c"), ps[:, 4 * kv:4 * kv + 4, 0:C2], ACT.Silu)\
                        .then_inc(h_out, 1)
                act.wait_ge(k_done, 1)
                nc.scalar.copy(raw[:], ps[:, 0, 0:2 * C2]).then_inc(k_out, 1)
                act.wait_ge(v_done, 1)
                nc.scalar.copy(m["vc"][:].rearrange("p g d -> p (g d)"), ps[0:NCMP, 1, 0:256]).then_inc(v_out, 1)

            @block.vector
            def _(dve):
                link = Chain(dve, own)
                V = nc.vector
                dve.wait_ge(loaded, 16 * len(loads))
                dve.wait_ge(k_out, 1)

                def by4(x):
                    return x.rearrange("p (g n) -> p g n", g=4)

                def table(i):
                    return cs[:, i * NCMP:(i + 1) * NCMP].unsqueeze(1).broadcast_to([P, 4, NCMP])

                link(V.tensor_tensor(by4(t1[:]), by4(raw[:]), table(0), ALU.mult))
                dve.wait_ge(sw_done, 1)
                kcT = m["kcT"][:].rearrange("p a u n -> p (a u) n")
                link(V.tensor_tensor(kcT, by4(ps[:, 2, 0:2 * C2]), table(1), ALU.mult))
                link(V.tensor_tensor(kcT, kcT, by4(t1[:]), ALU.add))

            @block.sync
            def _(sp):
                W.send(sp)

    def nsa_attention(self, m):
        nc, ps, W = self.nc, self.ps, self.W
        with self.new_stage() as ctx:
            sb = self.sb
            qT, kd, vsw, gates, kcT, vc, oT = m["qT"], m["kd"], m["vsw"], m["gates"], m["kcT"], m["vc"], m["xT"]
            p = sb(ctx, "na_p", [P, 2, 2, SEQ])
            pc = sb(ctx, "na_pc", [P, 2, 32])
            pT = sb(ctx, "na_pT", [P, 2, 2, SEQ])
            pcT = sb(ctx, "na_pcT", [NCMP, 2, P])
            st = sb(ctx, "na_st", [P, 2, 16])
            causal = sb(ctx, "na_causal", [P, P])
            cmask = sb(ctx, "na_cmask", [P, TT, NCMP])
            loaded, s_done, c_read, maxed, exped, w_done, t_done, t_out, o_done, o_out, own = self.sems(
                "na", "loaded", "s_done", "c_read", "maxed", "exped", "w_done", "t_done", "t_out", "o_done", "o_out", "own")
            loads = [(causal[:], self.const(2, "causal")),
                     (cmask[:], self.const(2, "cmpmask").rearrange("p (t n) -> p t n", t=TT))]
            units = [(hd, i) for hd in range(NH) for i in range(TT)]
            N = len(units)
            block = ctx.enter_context(nc.Block())

            @block.tensor
            def _(pe):
                for it in range(N + 2):
                    if it < N:
                        hd, i = units[it]
                        g = hd // 4
                        r = slice(64 * (hd % 2), 64 * (hd % 2) + 64)
                        q = qT[r, hd // 2, P * i:P * (i + 1)]
                        nk = P * (i + 1)
                        if it >= 2:
                            pe.wait_ge(exped, 3 * (it - 1))
                            pe.wait_ge(t_out, it - 1)
                        elif it:
                            pe.wait_ge(c_read, it)
                        for j in range(2):
                            nc.tensor.matmul(ps[:, 2 * (it % 2) + j, 0:nk], q, kd[r, j, g, 0:nk], start=True, stop=True)
                        nc.tensor.matmul(ps[:, 4, 0:NCMP], q, kcT[r, g % 2, g // 2, :], start=True, stop=True)\
                            .then_inc(s_done, 1)
                    u = it - 1
                    if 0 <= u < N:
                        i = units[u][1]
                        pe.wait_ge(w_done, u + 1)
                        if it < N:
                            pe.wait_ge(c_read, it + 1)
                        if u:
                            pe.wait_ge(t_out, u)
                        for j in range(2):
                            for b in range(i + 1):
                                nc.tensor.transpose(ps[:, 5 + j, P * b:P * (b + 1)], p[:, u % 2, j, P * b:P * (b + 1)],
                                                    self.ident[:])
                        nc.tensor.transpose(ps[0:NCMP, 4, P:2 * P], pc[:, u % 2, 0:NCMP], self.ident[:]).then_inc(t_done, 1)
                    u = it - 2
                    if u >= 0:
                        hd, i = units[u]
                        g = hd // 4
                        r = slice(64 * (hd % 2), 64 * (hd % 2) + 64)
                        pe.wait_ge(t_out, u + 1)
                        if u:
                            pe.wait_ge(o_out, u)
                        for j in range(2):
                            for b in range(i + 1):
                                nc.tensor.matmul(ps[r, 7, 0:P], vsw[:, b, 256 * j + 64 * g:256 * j + 64 * g + 64],
                                                 pT[:, u % 2, j, P * b:P * (b + 1)], start=(j == 0 and b == 0), stop=False)
                        nc.tensor.matmul(ps[r, 7, 0:P], vc[:, g, :], pcT[:, u % 2, :], start=False, stop=True)\
                            .then_inc(o_done, 1)

            @block.scalar
            def _(act):
                for to, frm in loads:
                    act.dma_start(to, frm).then_inc(loaded, 16)
                for it in range(N + 1):
                    if it < N:
                        i, s = units[it][1], it % 2
                        nk = P * (i + 1)
                        act.wait_ge(maxed, it + 1)
                        for j in range(2):
                            nc.scalar.activation(p[:, s, j, 0:nk], ps[:, 2 * s + j, 0:nk], ACT.Exp, bias=st[:, s, j:j + 1],
                                                 accum_out=st[:, s, 4 + j:5 + j]).then_inc(exped, 1)
                        nc.scalar.activation(pc[:, s, 0:NCMP], pc[:, s, 0:NCMP], ACT.Exp, bias=st[:, s, 2:3],
                                             accum_out=st[:, s, 6:7]).then_inc(exped, 1)
                    u = it - 1
                    if u >= 0:
                        nk = P * (units[u][1] + 1)
                        act.wait_ge(t_done, u + 1)
                        if u >= 2:
                            act.wait_ge(o_done, u - 1)
                        nc.scalar.copy(pT[:, u % 2, :, 0:nk], ps[:, 5:7, 0:nk])
                        nc.scalar.copy(pcT[:, u % 2, :], ps[0:NCMP, 4, P:2 * P]).then_inc(t_out, 1)

            @block.vector
            def _(dve):
                link = Chain(dve, own)
                V = nc.vector
                dve.wait_ge(loaded, 16 * len(loads))
                for it in range(N + 3):
                    if it < N:
                        hd, i = units[it]
                        s, nk = it % 2, P * (i + 1)
                        dve.wait_ge(s_done, it + 1)
                        V.tensor_tensor(pc[:, s, 0:NCMP], ps[:, 4, 0:NCMP], cmask[:, i, :], ALU.add).then_inc(c_read, 1)
                        S2 = ps[:, 2 * s:2 * s + 2, :]
                        link(V.tensor_tensor(S2[:, :, P * i:nk], S2[:, :, P * i:nk],
                                             causal[:].unsqueeze(1).broadcast_to([P, 2, P]), ALU.add))
                        link(V.tensor_reduce(st[:, s, 0:2], S2[:, :, 0:nk], AX.X, ALU.max, negate=True))
                        dve.wait_ge(c_read, it + 1)
                        V.tensor_reduce(st[:, s, 2:3], pc[:, s, 0:NCMP], AX.X, ALU.max, negate=True).then_inc(maxed, 1)
                    u = it - 1
                    if 0 <= u < N:
                        hd, i = units[u]
                        s, nk = u % 2, P * (i + 1)
                        dve.wait_ge(exped, 3 * u + 3)
                        link(V.reciprocal(st[:, s, 8:11], st[:, s, 4:7]))
                        link(V.tensor_tensor(st[:, s, 12:14], st[:, s, 8:10], gates[:, i, 3 * hd + 1:3 * hd + 3], ALU.mult))
                        link(V.tensor_tensor(st[:, s, 14:15], st[:, s, 10:11], gates[:, i, 3 * hd:3 * hd + 1], ALU.mult))
                        for j in range(2):
                            link(V.tensor_scalar(p[:, s, j, 0:nk], p[:, s, j, 0:nk], st[:, s, 12 + j:13 + j], None, ALU.mult))
                        V.tensor_scalar(pc[:, s, 0:NCMP], pc[:, s, 0:NCMP], st[:, s, 14:15], None, ALU.mult).then_inc(w_done, 1)
                    u = it - 3
                    if u >= 0:
                        hd, i = units[u]
                        r = slice(64 * (hd % 2), 64 * (hd % 2) + 64)
                        dve.wait_ge(o_done, u + 1)
                        V.tensor_copy(oT[r, hd // 2, P * i:P * (i + 1)], ps[r, 7, 0:P]).then_inc(o_out, 1)

            @block.sync
            def _(sp):
                W.send(sp)

    def nsa_out(self, m):
        nc, ps, W, h = self.nc, self.ps, self.W, self.h
        with self.new_stage() as ctx:
            y_done, y_out = self.sems("no", "y_done", "y_out")
            block = ctx.enter_context(nc.Block())

            @block.tensor
            def _(pe):
                self.tm_product(pe, self.n_no, lambda k, t: m["xT"][:, k, P * t:P * (t + 1)], y_done)

            @block.vector
            def _(dve):
                for t in range(TT):
                    dve.wait_ge(y_done, t + 1)
                    x = h[:, t, :].rearrange("p (a c) -> p a c", a=2)
                    nc.vector.scalar_tensor_tensor(x, x, ALPHA, ps[:, 2 * t:2 * t + 2, :], ALU.mult, ALU.add).then_inc(y_out, 1)

            @block.sync
            def _(sp):
                W.send(sp)


def build(nc, A, out, places1, places2, stop=None):
    with ExitStack() as root:
        root.enter_context(nc.allow_non_contiguous_dma(reason="small parameters"))
        K = Program(nc, A, places1, places2, root)
        K.first_block(stop)
        if stop not in ("n1", "s5", "mix", "first"):
            K.second_block(out, stop)
        if stop:
            with nc.Block() as block:
                @block.sync
                def _(sp):
                    for n in range(K.W.sent - RING, K.W.sent):
                        K.W.arrived(sp, n)


_STOP = None


def kernel(**inputs):
    import numpy as _np
    import concourse.bacc as _bacc
    from concourse import mybir as _mybir
    from concourse.bass_utils import run_bass_kernel_spmd as _run

    nc = _bacc.Bacc("TRN2", target_bir_lowering=False, num_devices=1)
    c1, places1, c2, places2 = constants()
    arrays, A = {}, {}
    given = dict(inputs)
    given["const1"], given["const2"] = c1, c2
    for name, a in given.items():
        a = _np.ascontiguousarray(a)
        arrays[f"in_{name}"] = a
        A[name] = nc.dram_tensor(f"in_{name}", a.shape, _mybir.dt.from_np(a.dtype), kind="ExternalInput").ap()
    out = nc.dram_tensor("out", (1, SEQ, D), F32, kind="ExternalOutput").ap()
    build(nc, A, out, places1, places2, _STOP)
    r = _run(nc, [arrays], core_ids=[0])
    return r.results[0]["out"]
```

```python
from contextlib import ExitStack, contextmanager
import math

import numpy as np
import concourse.bass as bass
from concourse import mybir

F32 = mybir.dt.float32
I32 = mybir.dt.int32
U32 = mybir.dt.uint32
ALU = mybir.AluOpType
ACT = mybir.ActivationFunctionType
AX = mybir.AxisListType

P = 128
D = 1024
KD = D // P
SEQ = 512
META = 16
T1 = SEQ + META
HALF = T1 // 2
TT = SEQ // P
EPS = 1e-6
LN_EPS = 1e-5
NEG = -1e30

H1 = 4
PAIRS = 16
SC = 16
NCH = T1 // SC
FF = 2816
ATT = 512
FT = FF // P
GH = 4
NH = 16
NG = 4
NCMP = 31
NE = 16
ALPHA = 4 ** 0.25
EG = 4
NGRP = NE // EG
NB = SEQ // P + NGRP - 1
XROW = D + EG

RING = 6


def constants():
    c = {}
    eye = np.eye(P, dtype=np.float32)
    c["ident"] = eye
    half = np.zeros((P, P), np.float32)
    half[:64, :64] = half[64:, 64:] = 1 / 64
    c["mean64"] = half
    c["mean128"] = np.full((P, P), 1 / 128, np.float32)
    q = np.arange(P)[:, None]
    dist = q - (np.arange(T1)[None] - 400)
    c["alibi"] = np.where(dist >= 0, -dist.astype(np.float32), np.float32(NEG)).astype(np.float32)
    odd = (np.arange(P) // 16) % 2
    c["parity"] = np.stack([odd == 0, odd == 1], 1).astype(np.float32)
    c1 = np.concatenate([c[k] for k in ("ident", "mean64", "mean128", "alibi", "parity")], 1)
    s = {}
    s["causal"] = np.where(q >= np.arange(P)[None], 0, NEG).astype(np.float32)
    end = np.arange(NCMP) * 16 + 31
    pos = np.arange(SEQ).reshape(TT, P)
    s["cmpmask"] = np.where(end[None, None] <= pos.T[:, :, None], 0, NEG).astype(np.float32).reshape(P, -1)
    s["cmpany"] = (end[0] <= pos.T).astype(np.float32)
    j = np.arange(P) % 64
    s["glamask"] = (j[:, None] <= np.arange(64)[None]).astype(np.float32)
    s["restart"] = np.broadcast_to((np.arange(SEQ) % 64 != 0).astype(np.float32), (P, SEQ))
    inv = np.power(np.float32(500000.0), -np.arange(8, dtype=np.float32) * np.float32(2.0 / 16)).astype(np.float32)

    def rope(p):
        ang = (p.astype(np.float32)[:, None] * inv[None]).astype(np.float32).astype(np.float64)
        cs = np.ones((P, len(p)), np.float32)
        sn = np.zeros((P, len(p)), np.float32)
        for b in (0, 64):
            for k in range(8):
                cs[b + k] = cs[b + 8 + k] = np.cos(ang[:, k])
                sn[b + k] = -np.sin(ang[:, k])
                sn[b + 8 + k] = np.sin(ang[:, k])
        return cs, sn

    s["cos"], s["sin"] = rope(np.arange(SEQ))
    s["coscmp"], s["sincmp"] = rope(end)
    swap = np.zeros((P, P), np.float32)
    for b in (0, 64):
        for k in range(8):
            swap[b + k + 8, b + k] = 1
            swap[b + k, b + 8 + k] = 1
    s["swap"] = swap
    s["before"] = (np.arange(P)[:, None] < np.arange(P)[None]).astype(np.float32)
    s["block"] = np.broadcast_to(np.arange(NB, dtype=np.float32), (P, NB))
    c2 = np.concatenate(list(s.values()), 1)

    def places(d, names):
        at, out = 0, {}
        for n in names:
            w = d[n].shape[1]
            out[n] = (at, at + w)
            at += w
        return out

    return (np.ascontiguousarray(c1, np.float32), places(c, ("ident", "mean64", "mean128", "alibi", "parity")),
            np.ascontiguousarray(c2, np.float32), places(s, list(s)))


class Chain:

    def __init__(self, eng, sem):
        self.eng, self.sem, self.n = eng, sem, 0

    def __call__(self, ins):
        self.n += 1
        ins.then_inc(self.sem, 1)
        self.eng.wait_ge(self.sem, self.n)


class Weights:

    def __init__(self, ring, landed, used):
        self.ring, self.landed, self.used = ring, landed, used
        self.parts, self.target, self.total = [], [], [0] * RING
        self.sent, self.n_used, self.free = 0, 0, {}
        self.held = None

    def add(self, *parts):
        n = len(self.parts)
        self.parts.append(parts)
        self.total[n % RING] += 16 * len(parts)
        self.target.append(self.total[n % RING])
        return n

    def slot(self, n):
        return self.ring[:, n % RING, :]

    def retire(self, n, ins):
        ins.then_inc(self.used, 1)
        self.n_used += 1
        self.free[n] = (self.used, self.n_used)

    def retired_by(self, n, sem, value):
        self.free[n] = (sem, value)

    def send(self, sp):
        while self.sent < len(self.parts) and (self.sent < RING or self.sent - RING in self.free):
            n = self.sent
            if n == self.held:
                break
            if n >= RING and self.free[n - RING]:
                sp.wait_ge(*self.free[n - RING])
            for view, src in self.parts[n]:
                sp.dma_start(view(self.slot(n)), src() if callable(src) else src).then_inc(self.landed[n % RING], 16)
            self.sent += 1

    def arrived(self, pe, n):
        pe.wait_ge(self.landed[n % RING], self.target[n])


def slab_view(k, w):
    return lambda s: s[:, 0:k * w].rearrange("p (k w) -> p k w", k=k)


def tile_of(v, r=P):
    return v[0:r]


TILES1 = [(P, t, META + P * t) for t in range(TT)] + [(META, TT, 0)]
TILES2 = [(P, t, P * t) for t in range(TT)]
HALVES = ((0, HALF), (HALF, T1))


class Program:

    def __init__(self, nc, A, places1, places2, root):
        self.nc, self.A, self.p1, self.p2, self.root, self.stage_sems = nc, A, places1, places2, root, []
        self.ps = root.enter_context(nc.psum_tensor("ps", [P, 8, 512], F32))
        self.ring = self.sb(root, "ring", [P, RING, 2048])
        self.ident = self.sb(root, "ident", [P, P])
        self.h = self.sb(root, "h", [P, TT + 1, D])
        self.x_slots = nc.dram_tensor("x_slots", (NB * P, XROW), F32).ap()
        self.y_slots = nc.dram_tensor("y_slots", (NB * P, D), F32).ap()
        self.W = Weights(self.ring, self.sems("slab_landed", *range(RING)), self.sem("slab_used"))
        self.out_stored = self.sem("out_stored")
        self.stage_sems = []
        self.group = [None] * NB
        self.weight_order()
        self.W.held = self.n_moe[0][0][0]

    @contextmanager
    def new_stage(self):
        with ExitStack() as ctx:
            yield ctx

    def recycle_semaphores(self):
        self.nc.clear_and_free_semaphores(self.stage_sems)
        self.stage_sems = []
        self.nc.all_engine_barrier()
        self.W.free = {n: None for n in self.W.free}

    def sem(self, name):
        s = self.nc.alloc_semaphore(name=name)
        self.stage_sems.append(s)
        return s

    def sems(self, tag, *names):
        return [self.sem(f"{tag}_{x}") for x in names]

    def sb(self, ctx, name, shape, dt=F32):
        return ctx.enter_context(self.nc.sbuf_tensor(name, shape, dt))

    def const(self, which, name):
        a, b = (self.p1 if which == 1 else self.p2)[name]
        return self.A[f"const{which}"][:, a:b]

    def fm_slabs(self, w, c0, n, width=256):
        k = w.shape[0] // P
        return [self.W.add((slab_view(k, width), w[:, c0 + i * width:c0 + (i + 1) * width]
                            .rearrange("(k p) w -> p k w", p=P))) for i in range(n)]

    def tm_slabs(self, w, c0=0):
        return [self.W.add((slab_view(2, D), w[i * 256:(i + 1) * 256, c0:c0 + D]
                            .rearrange("(k p) w -> p k w", p=P))) for i in range(w.shape[0] // 256)]

    def cmp_slabs(self, w):
        return [self.W.add((slab_view(8, 256), w[i * 1024:(i + 1) * 1024, :].rearrange("(k p) w -> p k w", p=P)))
                for i in range(2)]

    def moe_slabs(self, l):
        units = [[None] * 3 for _ in range(NB * EG)]
        for it in range(len(units) + 2):
            for u, down in ((it, False), (it - 2, True)):
                if not 0 <= u < len(units):
                    continue
                blk, e = divmod(u, EG)

                def expert(name, blk=blk, e=e):
                    return self.A[name][l][bass.ds(self.group[blk] * EG + e, 1)]

                if down:
                    units[u][2] = self.W.add((slab_view(2, D), lambda expert=expert: expert("moe_w_down_2")
                                              .rearrange("o (k p) w -> p (o k) w", p=P)))
                    continue
                for half in range(2):
                    units[u][half] = self.W.add(*[
                        (lambda s, j=j: s.rearrange("p (k w) -> p k w", k=4)[:, :, 256 * j:256 * j + 256],
                         lambda name=name, half=half, expert=expert: expert(name)[:, 512 * half:512 * half + 512, :]
                         .rearrange("o (k p) w -> p (o k) w", p=P))
                        for j, name in enumerate(("moe_w_gate_2", "moe_w_up_2"))])
        return units

    def weight_order(self):
        A = self.A
        self.n_in = self.fm_slabs(A["w_in"][0], 0, 16)
        self.n_glu = self.fm_slabs(A["ssm_glu_w"][0], 0, 1, 512)
        self.n_so, self.n_ao = [], []
        for i in range(2):
            self.n_so += self.fm_slabs(A["w_ssm_out"][0], i * 512, 1, 512)
            self.n_ao += self.fm_slabs(A["w_att_out"][0], i * 512, 1, 512)
        self.n_o = self.tm_slabs(A["w_o"][0])
        self.n_up = []
        for i in range(FT // 2):
            self.n_up.append((self.fm_slabs(A["w_up"][0], i * 256, 1)[0],
                              self.fm_slabs(A["w_up"][0], FF + i * 256, 1)[0]))
        self.n_dn = self.tm_slabs(A["w_down"][0])
        w = A["gla_w_in_2"][0]
        self.n_gqk = self.fm_slabs(w, 0, 4)
        self.n_glow = self.fm_slabs(w, 2048, 1, 16)
        self.n_gv = self.tm_slabs(w, 1024)
        self.n_gr = self.tm_slabs(w, 2064)
        self.n_go = self.tm_slabs(A["gla_w_out_2"][0])
        self.n_moe = [self.moe_slabs(0)]
        w = A["nsa_w_in_2"][0]
        self.n_nq = self.fm_slabs(w, 0, 4)
        self.n_nkv = [self.fm_slabs(w, c, 1)[0] for c in (1024, 1280, 1536, 2048)]
        self.n_cmp = [self.cmp_slabs(A["nsa_w_cmp_k1_2"][0]), self.cmp_slabs(A["nsa_w_cmp_v1_2"][0])]
        self.n_gate = self.fm_slabs(w, 2560, 1, 48)[0]
        self.n_nv = [self.fm_slabs(w, c, 1)[0] for c in (1792, 2304)]
        self.n_no = self.tm_slabs(A["nsa_w_out_2"][0])
        self.n_moe.append(self.moe_slabs(1))

    def fm_product(self, slab, kt, w, col, rhs, spans, done, m=P):
        v = slab_view(kt, w)(self.W.slot(slab))
        for bank, a, b in spans:
            for k in range(kt):
                ins = self.nc.tensor.matmul(self.ps[0:m, bank, 0:b - a], v[:, k, col:col + m], rhs(k, a, b),
                                            start=(k == 0), stop=(k == kt - 1))
        ins.then_inc(done, 1)
        return ins

    def tm_product(self, pe, slabs, lhsT, done, before=0, bank_free=None):
        n = 2 * len(slabs)
        for i, s in enumerate(slabs):
            self.W.arrived(pe, s)
            v = slab_view(2, D)(self.W.slot(s))
            for kk in range(2):
                k = 2 * i + kk
                for t in range(TT):
                    if k == 0 and bank_free:
                        bank_free(t)
                    for hf in range(2):
                        ins = self.nc.tensor.matmul(self.ps[:, 2 * t + hf, :], lhsT(k, t),
                                                    v[:, kk, hf * 512:hf * 512 + 512],
                                                    start=(k == 0), stop=(k == n - 1))
                    if k == n - 1:
                        ins.then_inc(done, 1)
            if i < len(slabs) - 1:
                self.W.retire(s, ins)
            else:
                self.W.retired_by(s, done, before + TT)

    def norm_stage(self, tag, tiles, src, dst, dstT, kind, gam, bet, eps, loads=(), to_dram=None):
        nc, ps, W = self.nc, self.ps, self.W
        with self.new_stage() as ctx:
            n = len(tiles)
            y = self.sb(ctx, tag + "_y", [P, 2, D])
            junk = self.sb(ctx, tag + "_junk", [P, D])
            st = self.sb(ctx, tag + "_st", [P, 5, 8])
            epsb = self.sb(ctx, tag + "_eps", [P, 1])
            loaded, epsset, centred, rs, normed, turned, evac, dve_own, act_own = self.sems(
                tag, "loaded", "epsset", "centred", "rs", "normed", "turned", "evac", "dve_own", "act_own")
            block = ctx.enter_context(nc.Block())

            @block.scalar
            def _(act):
                for to, frm in loads:
                    act.dma_start(to, frm).then_inc(loaded, 16)
                if kind:
                    act.wait_ge(epsset, 1)
                    link = Chain(act, act_own)
                    for i, (r, t, c0) in enumerate(tiles):
                        if kind == "ln":
                            act.wait_ge(centred, i + 1)
                        link(nc.scalar.activation(junk[0:r], src[0:r, t, :], ACT.Square,
                                                  accum_out=st[0:r, 0, t:t + 1]))
                        link(nc.scalar.activation(st[0:r, 1, t:t + 1], st[0:r, 0, t:t + 1], ACT.Ln,
                                                  bias=epsb[0:r, :], scale=1 / D))
                        nc.scalar.activation(st[0:r, 2, t:t + 1], st[0:r, 1, t:t + 1], ACT.Exp,
                                             scale=-0.5).then_inc(rs, 1)
                if dstT is None:
                    return
                for i, (r, t, c0) in enumerate(tiles):
                    for hf in range(2):
                        act.wait_ge(turned, 2 * i + hf + 1)
                        v = ps[:, (2 * i + hf) % 8, :].rearrange("p (k c) -> p k c", k=4)[:, :, 0:r]
                        nc.scalar.copy(dstT[:, 4 * hf:4 * hf + 4, c0:c0 + r], v).then_inc(evac, 1)

            @block.vector
            def _(dve):
                if not kind:
                    return
                nc.vector.memset(epsb[:], eps).then_inc(epsset, 1)
                link = Chain(dve, dve_own)
                if kind == "ln":
                    for i, (r, t, c0) in enumerate(tiles):
                        x = src[0:r, t, :]
                        link(nc.vector.reduce_sum(st[0:r, 3, t:t + 1], x, AX.X))
                        link(nc.vector.tensor_scalar(st[0:r, 4, t:t + 1], st[0:r, 3, t:t + 1], -1 / D, None, ALU.mult))
                        nc.vector.tensor_scalar(x, x, st[0:r, 4, t:t + 1], None, ALU.add).then_inc(centred, 1)
                    dve.wait_ge(centred, n)
                if loads:
                    dve.wait_ge(loaded, 16 * len(loads))
                for i, (r, t, c0) in enumerate(tiles):
                    x = src[0:r, t, :]
                    dve.wait_ge(rs, i + 1)
                    if kind == "rms":
                        if i >= 2:
                            dve.wait_ge(turned, 2 * (i - 1))
                        nc.vector.scalar_tensor_tensor(y[0:r, i % 2, :], x, st[0:r, 2, t:t + 1], gam[0:r, :],
                                                       ALU.mult, ALU.mult).then_inc(normed, 1)
                    else:
                        link(nc.vector.scalar_tensor_tensor(dst[0:r, t, :], x, st[0:r, 2, t:t + 1], gam[0:r, :],
                                                            ALU.mult, ALU.mult))
                        nc.vector.tensor_tensor(dst[0:r, t, :], dst[0:r, t, :], bet[0:r, :], ALU.add)\
                            .then_inc(normed, 1)

            @block.tensor
            def _(pe):
                if dstT is None:
                    return
                for i, (r, t, c0) in enumerate(tiles):
                    if kind:
                        pe.wait_ge(normed, i + 1)
                    for k in range(KD):
                        n4 = 2 * i + k // 4
                        if k % 4 == 0 and n4 >= 8:
                            pe.wait_ge(evac, n4 - 7)
                        s = y[0:r, i % 2, k * P:(k + 1) * P] if kind == "rms" else \
                            (dst if kind else src)[0:r, t, k * P:(k + 1) * P]
                        ins = nc.tensor.transpose(ps[:, n4 % 8, (k % 4) * P:(k % 4) * P + r], s, self.ident[0:r, 0:r])
                        if k % 4 == 3:
                            ins.then_inc(turned, 1)

            @block.sync
            def _(sp):
                W.send(sp)
                if to_dram is not None:
                    for i, (r, t, c0) in enumerate(tiles):
                        sp.wait_ge(normed, i + 1)
                        sp.dma_start(to_dram[t * P:(t + 1) * P, :], dst[:, t, :]).then_inc(self.out_stored, 16)
                    sp.wait_ge(self.out_stored, 16 * n)

    def s5_prepare(self, m, first_loads):
        nc, ps, W, A = self.nc, self.ps, self.W, self.A
        with self.new_stage() as ctx:
            ident = self.ident
            prm = self.sb(ctx, "s5_prm", [P, 28, PAIRS])
            ki = self.sb(ctx, "s5_ki", [P, PAIRS], I32)
            bre, bim = (self.sb(ctx, n, [P, PAIRS, 16]) for n in ("s5_bre", "s5_bim"))
            bt = self.sb(ctx, "s5_bt", [P, 2, PAIRS, 16])
            bpad = self.sb(ctx, "s5_bpad", [P, 2, PAIRS, 2, 16])
            craw = self.sb(ctx, "s5_craw", [P, 2, 4, 64])
            cpad = self.sb(ctx, "s5_cpad", [P, 2, 4, 2, 64])
            parity = self.sb(ctx, "s5_parity", [P, 2])
            loaded, par, padded, turned, sin_in, sin_out, own = self.sems(
                "s5", "loaded", "par", "padded", "turned", "sin_in", "sin_out", "own")
            names = ("are", "aim", "ldt", "dt", "th", "mag", "lr", "li", "sn", "sh", "nre", "den", "rden",
                     "fre", "fim", "x", "kf", "r", "q", "p2", "t0", "t1", "at", "one")
            v = {n: prm[:, i, :] for i, n in enumerate(names)}
            loads = [(v["are"], A["ssm_a_re"].rearrange("o (j g) p -> (o g p) j", g=2)),
                     (v["aim"], A["ssm_a_im"].rearrange("o (j g) p -> (o g p) j", g=2)),
                     (bre[:], A["ssm_b_re"].rearrange("o (j g) p c -> (o g p) j c", g=2)),
                     (bim[:], A["ssm_b_im"].rearrange("o (j g) p c -> (o g p) j c", g=2)),
                     (craw[:, 0], A["ssm_c_re"].rearrange("o (t j) c p -> (o j c) t p", t=4)),
                     (craw[:, 1], A["ssm_c_im"].rearrange("o (t j) c p -> (o j c) t p", t=4)),
                     (m["dcol"][:], A["ssm_d"].rearrange("o (t j) c -> (o j c) t", t=4)),
                     (parity[:], self.const(1, "parity"))]
            for g in range(2):
                loads.append((prm[64 * g:64 * g + 64, 2, :],
                              A["ssm_log_dt"].rearrange("o (j g) -> (o g) j", g=2)[g].partition_broadcast(64)))
            pw = m["pw"]
            block = ctx.enter_context(nc.Block())

            @block.scalar
            def _(act):
                for to, frm in loads:
                    act.dma_start(to, frm).then_inc(loaded, 16)
                act.wait_ge(sin_in, 1)
                nc.scalar.activation(v["sn"], v["r"], ACT.Sin).then_inc(sin_out, 1)
                nc.scalar.activation(v["sh"], v["r"], ACT.Sin, scale=0.5).then_inc(sin_out, 1)
                for i in range(4):
                    act.wait_ge(turned, i + 1)
                    nc.scalar.copy(m["s5m"][:, i, :, :], ps[:, i, :].rearrange("p (t c) -> p t c", t=4))

            @block.vector
            def _(dve):
                link = Chain(dve, own)
                V = nc.vector
                dve.wait_ge(loaded, 16 * (len(loads) + len(first_loads)))

                def round_of(x, scale):
                    link(V.tensor_scalar(v["kf"], x, scale, 12582912.0, ALU.mult, ALU.add))
                    link(V.tensor_scalar(v["kf"], v["kf"], 12582912.0, None, ALU.subtract))

                def reduce_by(x, parts):
                    src = x
                    for c in parts:
                        link(V.scalar_tensor_tensor(v["r"], v["kf"], -c, src, ALU.mult, ALU.add))
                        src = v["r"]

                def exp_of(dst, x):
                    link(V.tensor_scalar(v["x"], x, -87.0, 88.0, ALU.max, ALU.min))
                    round_of(v["x"], 1.4426950408889634)
                    reduce_by(v["x"], (0.693359375, -2.12194440e-4))
                    link(V.tensor_scalar(v["q"], v["r"], 1 / 5040, None, ALU.mult))
                    for c in (1 / 720, 1 / 120, 1 / 24, 1 / 6, 1 / 2, 1.0):
                        link(V.scalar_tensor_tensor(v["q"], v["q"], c, v["r"], ALU.add, ALU.mult))
                    link(V.tensor_scalar(v["kf"], v["kf"], 127.0, 8388608.0, ALU.add, ALU.mult))
                    link(V.tensor_copy(ki[:], v["kf"]))
                    link(V.scalar_tensor_tensor(dst, v["q"], 1.0, ki[:].bitcast(F32), ALU.add, ALU.mult))

                def mul(d, a, b):
                    link(V.tensor_tensor(d, a, b, ALU.mult))

                exp_of(v["dt"], v["ldt"])
                mul(v["at"], v["are"], v["dt"])
                exp_of(v["mag"], v["at"])
                mul(v["th"], v["aim"], v["dt"])
                round_of(v["th"], 1 / (2 * math.pi))
                reduce_by(v["th"], (6.28125, 0.0019340515136718750, 1.2556659146e-06))
                V.tensor_scalar(v["r"], v["r"], 3.1415925, -3.1415925, ALU.min, ALU.max).then_inc(sin_in, 1)
                dve.wait_ge(sin_out, 2)
                mul(v["li"], v["mag"], v["sn"])
                mul(v["t0"], v["sh"], v["sh"])
                link(V.tensor_scalar(v["t0"], v["t0"], -2.0, 1.0, ALU.mult, ALU.add))
                mul(v["lr"], v["mag"], v["t0"])
                link(V.tensor_scalar(v["nre"], v["lr"], -1.0, None, ALU.add))
                mul(v["t0"], v["are"], v["are"])
                mul(v["t1"], v["aim"], v["aim"])
                link(V.tensor_tensor(v["den"], v["t0"], v["t1"], ALU.add))
                link(V.reciprocal(v["rden"], v["den"]))
                for d, x0, x1, op in (("fre", "nre", "li", ALU.add), ("fim", "li", "nre", ALU.subtract)):
                    mul(v["t0"], v[x0], v["are"])
                    mul(v["t1"], v[x1], v["aim"])
                    link(V.tensor_tensor(v["t0"], v["t0"], v["t1"], op))
                    mul(v[d], v["t0"], v["rden"])
                link(V.memset(bpad[:], 0.0))

                def over_c(x):
                    return x.unsqueeze(2).broadcast_to([P, PAIRS, 16])

                for part, (x0, x1, op) in enumerate(((bre, bim, ALU.subtract), (bim, bre, ALU.add))):
                    mul(bt[:, 0], over_c(v["fre"]), x0[:])
                    mul(bt[:, 1], over_c(v["fim"]), x1[:])
                    for g in range(2):
                        q = slice(64 * g, 64 * g + 64)
                        link(V.tensor_tensor(bpad[q, part, :, g, :], bt[q, 0], bt[q, 1], op))
                for part in range(2):
                    for g in range(2):
                        link(V.tensor_scalar(cpad[:, part, :, g, :], craw[:, part], parity[:, g:g + 1],
                                             1.0 if part == 0 else -1.0, ALU.mult, ALU.mult))
                V.tensor_copy(v["one"], v["lr"]).then_inc(padded, 1)
                link(V.tensor_copy(pw[:, 0, :, 0], v["lr"]))
                link(V.tensor_copy(pw[:, 1, :, 0], v["li"]))
                for k in range(1, SC):
                    a, b = pw[:, 0, :, k - 1], pw[:, 1, :, k - 1]
                    mul(v["t0"], a, v["lr"])
                    mul(v["t1"], b, v["li"])
                    link(V.tensor_tensor(pw[:, 0, :, k], v["t0"], v["t1"], ALU.subtract))
                    mul(v["t0"], a, v["li"])
                    mul(v["t1"], b, v["lr"])
                    link(V.tensor_tensor(pw[:, 1, :, k], v["t0"], v["t1"], ALU.add))
                link(V.tensor_scalar(pw[:, 2], pw[:, 1], -1.0, None, ALU.mult))

            @block.tensor
            def _(pe):
                pe.wait_ge(loaded, 16 * (len(loads) + len(first_loads)))
                pe.wait_ge(padded, 1)
                for i in range(4):
                    for t in range(4):
                        src = bpad[:, i, 4 * t:4 * t + 4].rearrange("p j g c -> p (j g c)") if i < 2 else \
                            cpad[:, i - 2, t].rearrange("p g c -> p (g c)")
                        ins = nc.tensor.transpose(ps[:, i, t * P:(t + 1) * P], src, ident[:])
                    ins.then_inc(turned, 1)

            @block.sync
            def _(sp):
                for to, frm in first_loads:
                    sp.dma_start(to, frm).then_inc(loaded, 16)
                sp.wait_ge(loaded, 16 * (len(loads) + len(first_loads)))
                W.send(sp)

    def project_and_s5(self, m):
        nc, ps, W = self.nc, self.ps, self.W
        with self.new_stage() as ctx:
            HP = PAIRS // 2
            z = self.sb(ctx, "z", [P, 2, HP, T1])
            ab = self.sb(ctx, "ab", [P, 2, 2, HP * NCH])
            proj_done, proj_out, x_done, x_out, z_done, y_done, y_out, own = self.sems(
                "pj", "proj_done", "proj_out", "x_done", "x_out", "z_done", "y_done", "y_out", "own")
            hT, uT, gT, s5m, pw = m["hT"], m["qkvT"], m["gateT"], m["s5m"], m["pw"]
            order = [("p", i) for i in range(4)] + [("x", 0)] + [("p", i) for i in range(4, 18)] + [("y", 0), ("x", 1)] + \
                [("p", i) for i in range(18, 32)] + [("y", 1)]
            block = ctx.enter_context(nc.Block())

            @block.tensor
            def _(pe):
                for what, i in order:
                    if what == "p":
                        W.arrived(pe, self.n_in[i // 2])
                        if i >= 2:
                            pe.wait_ge(proj_out, i - 1)
                        b = 2 * (i % 2)
                        ins = self.fm_product(self.n_in[i // 2], KD, 256, (i % 2) * P, lambda k, a, c: hT[:, k, a:c],
                                              [(b, *HALVES[0]), (b + 1, *HALVES[1])], proj_done)
                        if i % 2:
                            W.retired_by(self.n_in[i // 2], proj_done, i + 1)
                    elif what == "x":
                        pe.wait_ge(proj_out, 4)
                        if i:
                            pe.wait_ge(y_out, 2)
                        for lp in range(HP):
                            u, r = divmod(i * HP + lp, 4)
                            r *= 32
                            for part in range(2):
                                n = i * 16 + lp * 2 + part
                                if lp * 2 + part >= 2:
                                    pe.wait_ge(x_out, n - 1)
                                for hf, (a, c) in enumerate(HALVES):
                                    ins = nc.tensor.matmul(ps[:, 4 + 2 * (n % 2) + hf, 0:HALF], s5m[r:r + 32, part, u, :],
                                                           uT[r:r + 32, u, a:c], start=True, stop=True)
                                ins.then_inc(x_done, 1)
                    else:
                        pe.wait_ge(z_done, i + 1)
                        for tl in range(2):
                            u = 2 * i + tl
                            for hf, (a, c) in enumerate(HALVES):
                                for j in range(4):
                                    r = 32 * j
                                    for part in range(2):
                                        ins = nc.tensor.matmul(ps[r:r + 32, 4 + 2 * tl + hf, 0:HALF],
                                                               s5m[:, 2 + part, u, r:r + 32],
                                                               z[:, part, 4 * tl + j, a:c],
                                                               start=(part == 0), stop=(part == 1))
                            ins.then_inc(y_done, 1)

            @block.scalar
            def _(act):
                for what, i in order:
                    if what == "p":
                        act.wait_ge(proj_done, i + 1)
                        b = 2 * (i % 2)
                        src = ps[:, b:b + 2, 0:HALF]
                        if i < 16:
                            dst, f = uT[:, i, :], ACT.Copy
                        else:
                            dst, f = gT[:, i - 16, :], ACT.Sigmoid
                        nc.scalar.activation(dst.rearrange("p (a c) -> p a c", a=2), src, f).then_inc(proj_out, 1)
                    elif what == "x":
                        for n in range(16 * i, 16 * i + 16):
                            act.wait_ge(x_done, n + 1)
                            b = 4 + 2 * (n % 2)
                            nc.scalar.copy(z[:, n % 2, (n // 2) % HP, :].rearrange("p (a c) -> p a c", a=2),
                                           ps[:, b:b + 2, 0:HALF]).then_inc(x_out, 1)

            @block.vector
            def _(dve):
                link = Chain(dve, own)
                z5 = z[:].rearrange("p r j (n t) -> p r j n t", t=SC)

                def step(dst, src, k, half, n):
                    def power(r):
                        return pw[:, r, half * HP:(half + 1) * HP, k].unsqueeze(2).broadcast_to([P, HP, n])
                    A4 = ab[:, 0, :, 0:HP * n].rearrange("p r (j n) -> p r j n", j=HP)
                    B4 = ab[:, 1, :, 0:HP * n].rearrange("p r (j n) -> p r j n", j=HP)
                    V = nc.vector
                    for r in range(2):
                        V.tensor_tensor(A4[:, r], src(r), power(0), ALU.mult).then_inc(own, 1)
                        V.tensor_tensor(B4[:, r], src(1 - r), power(2 if r == 0 else 1), ALU.mult).then_inc(own, 1)
                    link.n += 4
                    dve.wait_ge(own, link.n)
                    link(V.tensor_tensor(ab[:, 0, :, 0:HP * n], ab[:, 0, :, 0:HP * n], ab[:, 1, :, 0:HP * n], ALU.add))
                    for r in range(2):
                        V.tensor_tensor(dst(r), dst(r), A4[:, r], ALU.add).then_inc(own, 1)
                    link.n += 2
                    dve.wait_ge(own, link.n)

                for half in range(2):
                    dve.wait_ge(x_out, 16 * half + 16)
                    for t in range(1, SC):
                        step(lambda r: z5[:, r, :, :, t], lambda r: z5[:, r, :, :, t - 1], 0, half, NCH)
                    for n in range(1, NCH):
                        step(lambda r: z5[:, r, :, n:n + 1, SC - 1], lambda r: z5[:, r, :, n - 1:n, SC - 1], SC - 1, half, 1)
                    for t in range(SC - 1):
                        step(lambda r: z5[:, r, :, 1:, t], lambda r: z5[:, r, :, :-1, SC - 1], t, half, NCH - 1)
                    nc.vector.tensor_copy(ab[:, 0, 0, 0:1], ab[:, 0, 0, 1:2]).then_inc(z_done, 1)
                    for tl in range(2):
                        dve.wait_ge(y_done, 2 * half + tl + 1)
                        u = 2 * half + tl
                        o = uT[:, u, :].rearrange("p (a c) -> p a c", a=2)
                        nc.vector.scalar_tensor_tensor(o, o, m["dcol"][:, u:u + 1], ps[:, 4 + 2 * tl:6 + 2 * tl, 0:HALF],
                                                       ALU.mult, ALU.add).then_inc(y_out, 1)

            @block.sync
            def _(sp):
                W.send(sp)



    def qk_norm_stage(self, m):
        nc, ps, W, A = self.nc, self.ps, self.W, self.A
        with self.new_stage() as ctx:
            sq = self.sb(ctx, "qn_sq", [P, 2, T1])
            r = self.sb(ctx, "qn_r", [P, 2, T1])
            mean64 = self.sb(ctx, "mean64", [P, P])
            gc = self.sb(ctx, "qn_gc", [P, 2])
            lam4 = self.sb(ctx, "lam4", [P, 4, 64])
            lt = self.sb(ctx, "lt", [P, 4])
            eps = self.sb(ctx, "qn_eps", [P, 1])
            loaded, start, sq_done, mean_done, r_done, q_out, v_done, v_out, lam_in, lam_exp, own, actown = self.sems(
                "qn", "loaded", "start", "sq_done", "mean_done", "r_done", "q_out", "v_done", "v_out", "lam_in",
                "lam_exp", "own", "act_own")
            qk = m["qkvT"]
            loads = [(mean64[:], self.const(1, "mean64")), (m["alibi"][:], self.const(1, "alibi"))]
            for i, n in enumerate(("q_norm_g", "k_norm_g")):
                for g in range(2):
                    loads.append((gc[64 * g:64 * g + 64, i:i + 1], A[n].rearrange("o d -> d o")))
            for i, n in enumerate(("lam_q1", "lam_k1", "lam_q2", "lam_k2")):
                loads.append((lam4[:, i, :], A[n][0].partition_broadcast(P)))
            KT = [(META, 0)] + [(P, META + P * t) for t in range(TT)]
            block = ctx.enter_context(nc.Block())

            @block.tensor
            def _(pe):
                for b, (n, c0) in enumerate(KT):
                    if b == 4:
                        pe.wait_ge(v_out, 1)
                    for hd in range(H1):
                        ins = nc.tensor.transpose(ps[0:n, b % 4, hd * P:(hd + 1) * P], qk[:, 12 + hd, c0:c0 + n],
                                                  self.ident[:])
                    ins.then_inc(v_done, 1)
                pe.wait_ge(loaded, 16 * len(loads))
                for i in range(8):
                    pe.wait_ge(sq_done, i + 1)
                    if i >= 2:
                        pe.wait_ge(r_done, i - 1)
                    for hf, (a, c) in enumerate(HALVES):
                        ins = nc.tensor.matmul(ps[:, 4 + 2 * (i % 2) + hf, 0:HALF], mean64[:], sq[:, i % 2, a:c],
                                               start=True, stop=True)
                    ins.then_inc(mean_done, 1)

            @block.scalar
            def _(act):
                for to, frm in loads:
                    act.dma_start(to, frm).then_inc(loaded, 16)
                act.wait_ge(start, 1)
                link = Chain(act, actown)

                def square(i):
                    if i >= 2:
                        act.wait_ge(mean_done, i - 1)
                    nc.scalar.activation(sq[:, i % 2], qk[:, 4 + i], ACT.Square).then_inc(sq_done, 1)

                square(0)
                square(1)
                for i in range(8):
                    act.wait_ge(mean_done, i + 1)
                    if i >= 2:
                        act.wait_ge(q_out, i - 1)
                    b = 4 + 2 * (i % 2)
                    rr = r[:, i % 2].rearrange("p (a c) -> p a c", a=2)
                    link(nc.scalar.activation(rr, ps[:, b:b + 2, 0:HALF], ACT.Ln, bias=eps[:]))
                    nc.scalar.activation(rr, rr, ACT.Exp, scale=-0.5).then_inc(r_done, 1)
                    if i + 2 < 8:
                        square(i + 2)
                act.wait_ge(lam_in, 1)
                nc.scalar.activation(lt[:, 2:4], lt[:, 0:2], ACT.Exp).then_inc(lam_exp, 1)

            @block.vector
            def _(dve):
                link = Chain(dve, own)
                V = nc.vector
                V.memset(eps[:], EPS).then_inc(start, 1)
                dve.wait_ge(loaded, 16 * len(loads))
                link(V.tensor_scalar(gc[:, 0:1], gc[:, 0:1], 0.125, None, ALU.mult))
                for i in range(2):
                    link(V.tensor_tensor(lam4[:, 2 * i], lam4[:, 2 * i], lam4[:, 2 * i + 1], ALU.mult))
                    ins = V.reduce_sum(lt[:, i:i + 1], lam4[:, 2 * i], AX.X)
                    if i == 0:
                        link(ins)
                    else:
                        ins.then_inc(lam_in, 1)
                for b, (n, c0) in enumerate(KT):
                    dve.wait_ge(v_done, b + 1)
                    V.tensor_copy(m["v"][0:n, b, :], ps[0:n, b % 4, :]).then_inc(v_out, 1)
                for i in range(8):
                    dve.wait_ge(r_done, i + 1)
                    V.scalar_tensor_tensor(qk[:, 4 + i], qk[:, 4 + i], gc[:, i // 4:i // 4 + 1], r[:, i % 2],
                                           ALU.mult, ALU.mult).then_inc(q_out, 1)
                dve.wait_ge(lam_exp, 1)
                link(V.tensor_tensor(lt[:, 0:1], lt[:, 3:4], lt[:, 2:3], ALU.subtract))
                link(V.tensor_scalar(m["mlam"][:], lt[:, 0:1], -0.2, None, ALU.add))

            @block.sync
            def _(sp):
                W.send(sp)

    def diff_attention(self, m):
        nc, ps, W = self.nc, self.ps, self.W
        units = [(hd, i) for hd in range(H1) for i in range(TT + 1)]
        shape = [(META, META, 0)] + [(P, META + P * i, META + P * (i - 1)) for i in range(1, TT + 1)]
        KT = [(META, 0)] + [(P, META + P * t) for t in range(TT)]
        with self.new_stage() as ctx:
            s = self.sb(ctx, "da_s", [P, 2, 2, T1])
            w = self.sb(ctx, "da_w", [P, 2, T1])
            wT = self.sb(ctx, "da_wT", [P, 2, 5, P])
            st = self.sb(ctx, "da_st", [P, 2, 8])
            s_done, s_read, maxed, exped, w_done, t_done, t_out, o_done, o_out, own = self.sems(
                "da", "s_done", "s_read", "maxed", "exped", "w_done", "t_done", "t_out", "o_done", "o_out", "own")
            qk, v, oT, alibi = m["qkvT"], m["v"], m["oT"], m["alibi"]
            N = len(units)
            flat = ps[:].rearrange("p b c -> p (b c)")
            block = ctx.enter_context(nc.Block())

            @block.tensor
            def _(pe):
                for it in range(N + 2):
                    if it < N:
                        hd, i = units[it]
                        nq, nk, q0 = shape[i]
                        if it:
                            pe.wait_ge(s_read, it)
                        for j in range(2):
                            for a in range(0, nk, 512):
                                c = min(nk, a + 512)
                                ins = nc.tensor.matmul(flat[0:nq, 1024 * j + a:1024 * j + c],
                                                       qk[64 * j:64 * j + 64, 4 + hd, q0:q0 + nq],
                                                       qk[64 * j:64 * j + 64, 8 + hd, a:c], start=True, stop=True)
                        ins.then_inc(s_done, 1)
                    u = it - 1
                    if 0 <= u < N:
                        hd, i = units[u]
                        nq, nk, q0 = shape[i]
                        pe.wait_ge(w_done, u + 1)
                        if u:
                            pe.wait_ge(t_out, u)
                        for b in range(i + 1):
                            n, c0 = KT[b]
                            ins = nc.tensor.transpose(flat[0:n, 2048 + P * b:2048 + P * b + nq], w[0:nq, u % 2, c0:c0 + n],
                                                      self.ident[0:nq, 0:nq])
                        ins.then_inc(t_done, 1)
                    u = it - 2
                    if u >= 0:
                        hd, i = units[u]
                        nq, nk, q0 = shape[i]
                        pe.wait_ge(t_out, u + 1)
                        if u >= 2:
                            pe.wait_ge(o_out, u - 1)
                        for b in range(i + 1):
                            n, c0 = KT[b]
                            ins = nc.tensor.matmul(ps[:, 6 + u % 2, 0:nq], v[0:n, b, hd * P:(hd + 1) * P],
                                                   wT[0:n, u % 2, b, 0:nq], start=(b == 0), stop=(b == i))
                        ins.then_inc(o_done, 1)

            @block.scalar
            def _(act):
                for it in range(N + 1):
                    if it < N:
                        nq, nk, q0 = shape[units[it][1]]
                        act.wait_ge(maxed, it + 1)
                        for j in range(2):
                            x = s[0:nq, it % 2, j, 0:nk]
                            nc.scalar.activation(x, x, ACT.Exp, bias=st[0:nq, it % 2, j:j + 1],
                                                 accum_out=st[0:nq, it % 2, 2 + j:3 + j]).then_inc(exped, 1)
                    u = it - 1
                    if u >= 0:
                        i = units[u][1]
                        nq = shape[i][0]
                        act.wait_ge(t_done, u + 1)
                        if u >= 2:
                            act.wait_ge(o_done, u - 1)
                        ins = nc.scalar.copy(wT[0:META, u % 2, 0, 0:nq], flat[0:META, 2048:2048 + nq])
                        if i:
                            ins = nc.scalar.copy(wT[:, u % 2, 1:i + 1, 0:nq],
                                                 flat[:, 2048 + P:2048 + P + P * i].rearrange("p (b c) -> p b c", b=i)[:, :, 0:nq])
                        ins.then_inc(t_out, 1)

            @block.vector
            def _(dve):
                link = Chain(dve, own)
                V = nc.vector
                for it in range(N + 3):
                    if it < N:
                        hd, i = units[it]
                        nq, nk, q0 = shape[i]
                        dve.wait_ge(s_done, it + 1)
                        for j in range(2):
                            V.scalar_tensor_tensor(s[0:nq, it % 2, j, 0:nk], alibi[0:nq, 400 - q0:400 - q0 + nk],
                                                   2.0 ** (-2 * (hd + 1)), flat[0:nq, 1024 * j:1024 * j + nk],
                                                   ALU.mult, ALU.add).then_inc(s_read if j else own, 1)
                        link.n += 1
                        dve.wait_ge(own, link.n)
                        dve.wait_ge(s_read, it + 1)
                        V.tensor_reduce(st[0:nq, it % 2, 0:2], s[0:nq, it % 2, :, 0:nk], AX.X, ALU.max,
                                        negate=True).then_inc(maxed, 1)
                    u = it - 1
                    if 0 <= u < N:
                        nq, nk, q0 = shape[units[u][1]]
                        x = st[0:nq, u % 2]
                        dve.wait_ge(exped, 2 * u + 2)
                        link(V.reciprocal(x[:, 4:6], x[:, 2:4]))
                        link(V.tensor_scalar(x[:, 5:6], x[:, 5:6], m["mlam"][0:nq, :], None, ALU.mult))
                        if u >= 2:
                            dve.wait_ge(t_done, u - 1)
                        link(V.tensor_scalar(w[0:nq, u % 2, 0:nk], s[0:nq, u % 2, 0, 0:nk], x[:, 4:5], None, ALU.mult))
                        V.scalar_tensor_tensor(w[0:nq, u % 2, 0:nk], s[0:nq, u % 2, 1, 0:nk], x[:, 5:6],
                                               w[0:nq, u % 2, 0:nk], ALU.mult, ALU.add).then_inc(w_done, 1)
                    u = it - 3
                    if u >= 0:
                        hd, i = units[u]
                        nq, nk, q0 = shape[i]
                        dve.wait_ge(o_done, u + 1)
                        V.tensor_copy(oT[:, hd, q0:q0 + nq], ps[:, 6 + u % 2, 0:nq]).then_inc(o_out, 1)

            @block.sync
            def _(sp):
                W.send(sp)

    def mix_stage(self, m):
        nc, ps, W, A = self.nc, self.ps, self.W, self.A
        with self.new_stage() as ctx:
            sq = self.sb(ctx, "mx_sq", [P, H1, T1])
            r = self.sb(ctx, "mx_r", [P, 2, T1])
            sg = self.sb(ctx, "mx_sg", [P, 2, T1])
            mean128 = self.sb(ctx, "mean128", [P, P])
            gb = self.sb(ctx, "mx_gb", [P, 4])
            sub = self.sb(ctx, "mx_sub", [P, 1])
            eps = self.sb(ctx, "mx_eps", [P, 1])
            tmp = self.sb(ctx, "mx_tmp", [P, 2, T1])
            loaded, start, sq_done, mean_done, r_done, att_done, y_done, glu_done, sg_done, ys_done, pr_done, mx_done, \
                o_done, o_out, meta_done, own, actown = self.sems(
                    "mx", "loaded", "start", "sq_done", "mean_done", "r_done", "att_done", "y_done", "glu_done",
                    "sg_done", "ys_done", "pr_done", "mx_done", "o_done", "o_out", "meta_done", "own", "act_own")
            yT, ysT, oT, gT, mixT, h = m["qkvT"][:, 0:4], m["qkvT"][:, 4:8], m["oT"], m["gateT"], m["hT"], self.h
            loads = [(mean128[:], self.const(1, "mean128")), (gb[:], A["ssm_glu_b"].rearrange("o (t p) -> p (o t)", p=P)),
                     (sub[:], A["subln_g"].rearrange("o p -> p o"))]
            block = ctx.enter_context(nc.Block())

            def pair(b):
                return ps[:, b:b + 2, 0:HALF]

            @block.tensor
            def _(pe):
                pe.wait_ge(loaded, 16 * len(loads))
                for hd in range(H1):
                    pe.wait_ge(sq_done, hd + 1)
                    for hf, (a, c) in enumerate(HALVES):
                        ins = nc.tensor.matmul(ps[:, 2 * hd + hf, 0:HALF], mean128[:], sq[:, hd, a:c], start=True, stop=True)
                    ins.then_inc(mean_done, 1)
                W.arrived(pe, self.n_glu[0])
                pe.wait_ge(y_done, 1)
                for i in range(4):
                    pe.wait_ge(r_done, i + 1)
                    self.fm_product(self.n_glu[0], 4, 512, i * P, lambda k, a, c: yT[:, k, a:c],
                                    [(2 * i, *HALVES[0]), (2 * i + 1, *HALVES[1])], glu_done)
                W.retired_by(self.n_glu[0], glu_done, 4)
                pe.wait_ge(ys_done, 4)
                pe.wait_ge(att_done, 4)
                for i in range(KD):
                    q = i // 4
                    if i >= 2:
                        pe.wait_ge(mx_done, i - 1)
                    b = 4 * (i % 2)
                    if i % 4 == 0:
                        W.arrived(pe, self.n_so[q])
                        W.arrived(pe, self.n_ao[q])
                    for j, (n, x) in enumerate(((self.n_so[q], ysT), (self.n_ao[q], oT))):
                        self.fm_product(n, 4, 512, (i % 4) * P, lambda k, a, c, x=x: x[:, k, a:c],
                                        [(b + 2 * j, *HALVES[0]), (b + 2 * j + 1, *HALVES[1])], pr_done)
                    if i % 4 == 3:
                        W.retired_by(self.n_so[q], pr_done, 2 * i + 2)
                        W.retired_by(self.n_ao[q], pr_done, 2 * i + 2)
                pe.wait_ge(mx_done, KD)
                for i, n in enumerate(self.n_o):
                    W.arrived(pe, n)
                    v = slab_view(2, D)(W.slot(n))
                    for kk in range(2):
                        for t in range(TT):
                            for hf in range(2):
                                ins = nc.tensor.matmul(ps[:, 2 * t + hf, :], mixT[:, 2 * i + kk, META + P * t:META + P * (t + 1)],
                                                       v[:, kk, 512 * hf:512 * hf + 512], start=(i == 0 and kk == 0),
                                                       stop=(i == 3 and kk == 1))
                            if i == 3 and kk == 1:
                                ins.then_inc(o_done, 1)
                pe.wait_ge(o_out, 1)
                for i, n in enumerate(self.n_o):
                    v = slab_view(2, D)(W.slot(n))
                    for kk in range(2):
                        for hf in range(2):
                            ins = nc.tensor.matmul(ps[0:META, hf, :], mixT[:, 2 * i + kk, 0:META],
                                                   v[:, kk, 512 * hf:512 * hf + 512], start=(i == 0 and kk == 0),
                                                   stop=(i == 3 and kk == 1))
                    if i < 3:
                        W.retire(n, ins)
                ins.then_inc(meta_done, 1)
                W.retired_by(self.n_o[3], meta_done, 1)

            @block.scalar
            def _(act):
                for to, frm in loads:
                    act.dma_start(to, frm).then_inc(loaded, 16)
                act.wait_ge(start, 1)
                link = Chain(act, actown)
                for hd in range(H1):
                    nc.scalar.activation(sq[:, hd], oT[:, hd], ACT.Square).then_inc(sq_done, 1)
                nc.scalar.activation(yT, yT, ACT.Gelu_apprx_tanh).then_inc(y_done, 1)
                for hd in range(H1):
                    act.wait_ge(mean_done, hd + 1)
                    if hd >= 2:
                        act.wait_ge(att_done, hd - 1)
                    rr = r[:, hd % 2].rearrange("p (a c) -> p a c", a=2)
                    link(nc.scalar.activation(rr, pair(2 * hd), ACT.Ln, bias=eps[:]))
                    nc.scalar.activation(rr, rr, ACT.Exp, scale=-0.5).then_inc(r_done, 1)
                act.wait_ge(loaded, 16 * len(loads))
                for i in range(4):
                    act.wait_ge(glu_done, i + 1)
                    if i >= 2:
                        act.wait_ge(ys_done, i - 1)
                    nc.scalar.activation(sg[:, i % 2].rearrange("p (a c) -> p a c", a=2), pair(2 * i), ACT.Sigmoid,
                                         bias=gb[:, i:i + 1]).then_inc(sg_done, 1)

            @block.vector
            def _(dve):
                link = Chain(dve, own)
                V = nc.vector
                V.memset(eps[:], EPS).then_inc(start, 1)
                dve.wait_ge(loaded, 16 * len(loads))
                link(V.tensor_scalar(sub[:], sub[:], 0.8, None, ALU.mult))
                for hd in range(H1):
                    dve.wait_ge(r_done, hd + 1)
                    V.scalar_tensor_tensor(oT[:, hd], oT[:, hd], sub[:], r[:, hd % 2], ALU.mult, ALU.mult)\
                        .then_inc(att_done, 1)
                dve.wait_ge(y_done, 1)
                for i in range(4):
                    dve.wait_ge(sg_done, i + 1)
                    V.tensor_tensor(ysT[:, i], yT[:, i], sg[:, i % 2], ALU.mult).then_inc(ys_done, 1)
                for i in range(KD):
                    b = 4 * (i % 2)
                    dve.wait_ge(pr_done, 2 * i + 2)
                    if i:
                        dve.wait_ge(mx_done, i)
                    g = [gT[:, 8 * j + i].rearrange("p (a c) -> p a c", a=2) for j in range(2)]
                    t2 = [tmp[:, j].rearrange("p (a c) -> p a c", a=2) for j in range(2)]
                    for j in range(2):
                        link(V.tensor_tensor(t2[j], g[j], pair(b + 2 * j), ALU.mult))
                    V.tensor_tensor(mixT[:, i], tmp[:, 0], tmp[:, 1], ALU.add).then_inc(mx_done, 1)
                for t in range(TT):
                    dve.wait_ge(o_done, t + 1)
                    x = h[:, t, :].rearrange("p (a c) -> p a c", a=2)
                    V.tensor_tensor(x, x, ps[:, 2 * t:2 * t + 2, :], ALU.add).then_inc(o_out, 1)
                dve.wait_ge(meta_done, 1)
                x = h[0:META, TT, :].rearrange("p (a c) -> p a c", a=2)
                V.tensor_tensor(x, x, ps[0:META, 0:2, :], ALU.add).then_inc(o_out, 1)

            @block.sync
            def _(sp):
                W.send(sp)

    def ffn_stage(self, hT, gT):
        nc, ps, W, A, h = self.nc, self.ps, self.W, self.A, self.h
        with self.new_stage() as ctx:
            a_sb = self.sb(ctx, "ff_a", [P, 2, T1])
            c = self.sb(ctx, "ff_c", [P, 2, SEQ])
            ge = self.sb(ctx, "ff_ge", [P, 2, SEQ])
            cw = self.sb(ctx, "ff_cw", [P, 4, FT])
            loaded, a_done, a_out, b_done, c_done, ge_done, g_done, o_done, o_out, own = self.sems(
                "ff", "loaded", "a_done", "a_out", "b_done", "c_done", "ge_done", "g_done", "o_done", "o_out", "own")
            loads = [(cw[:, j, :], A["conv_w"][0, j].rearrange("(t p) -> p t", p=P)) for j in range(3)]
            loads.append((cw[:, 3, :], A["conv_b"][0].rearrange("(t p) -> p t", p=P)))
            block = ctx.enter_context(nc.Block())

            @block.tensor
            def _(pe):
                for i in range(FT):
                    na, nb = self.n_up[i // 2]
                    W.arrived(pe, na)
                    if i >= 2:
                        pe.wait_ge(a_out, i - 1)
                    s = i % 2
                    self.fm_product(na, KD, 256, s * P, lambda k, a, b: hT[:, k, a:b],
                                    [(2 * s, *HALVES[0]), (2 * s + 1, *HALVES[1])], a_done)
                    W.arrived(pe, nb)
                    if i >= 2:
                        pe.wait_ge(g_done, i - 1)
                    self.fm_product(nb, KD, 256, s * P, lambda k, a, b: hT[:, k, a:b], [(4 + s, META, T1)], b_done)
                    if s:
                        W.retired_by(na, a_done, i + 1)
                        W.retired_by(nb, b_done, i + 1)
                pe.wait_ge(g_done, FT)
                pe.wait_ge(a_out, FT)
                self.tm_product(pe, self.n_dn, lambda k, t: gT[:, k, P * t:P * (t + 1)], o_done)

            @block.scalar
            def _(act):
                for to, frm in loads:
                    act.dma_start(to, frm).then_inc(loaded, 16)
                for it in range(FT + 1):
                    if it < FT:
                        s = it % 2
                        act.wait_ge(a_done, it + 1)
                        if it >= 2:
                            act.wait_ge(c_done, it - 1)
                        nc.scalar.copy(a_sb[:, s].rearrange("p (a c) -> p a c", a=2), ps[:, 2 * s:2 * s + 2, 0:HALF])\
                            .then_inc(a_out, 1)
                    i = it - 1
                    if i >= 0:
                        act.wait_ge(c_done, i + 1)
                        if i >= 2:
                            act.wait_ge(g_done, i - 1)
                        nc.scalar.activation(ge[:, i % 2], c[:, i % 2], ACT.Gelu_apprx_tanh).then_inc(ge_done, 1)

            @block.vector
            def _(dve):
                link = Chain(dve, own)
                V = nc.vector
                dve.wait_ge(loaded, 16 * len(loads))
                for it in range(FT + 1):
                    if it < FT:
                        s = it % 2
                        dve.wait_ge(a_out, it + 1)
                        if it >= 2:
                            dve.wait_ge(ge_done, it - 1)
                        link(V.tensor_scalar(c[:, s], a_sb[:, s, META - 2:T1 - 2], cw[:, 0, it:it + 1], cw[:, 3, it:it + 1],
                                             ALU.mult, ALU.add))
                        link(V.scalar_tensor_tensor(c[:, s], a_sb[:, s, META - 1:T1 - 1], cw[:, 1, it:it + 1], c[:, s],
                                                    ALU.mult, ALU.add))
                        V.scalar_tensor_tensor(c[:, s], a_sb[:, s, META:T1], cw[:, 2, it:it + 1], c[:, s],
                                               ALU.mult, ALU.add).then_inc(c_done, 1)
                    i = it - 1
                    if i >= 0:
                        dve.wait_ge(ge_done, i + 1)
                        dve.wait_ge(b_done, i + 1)
                        V.tensor_tensor(gT[:, i], ge[:, i % 2], ps[:, 4 + i % 2, :], ALU.mult).then_inc(g_done, 1)
                for t in range(TT):
                    dve.wait_ge(o_done, t + 1)
                    x = h[:, t, :].rearrange("p (a c) -> p a c", a=2)
                    V.tensor_tensor(x, x, ps[:, 2 * t:2 * t + 2, :], ALU.add).then_inc(o_out, 1)

            @block.sync
            def _(sp):
                W.send(sp)

    def first_block(self, stop=None):
        A, sb = self.A, self.sb
        with ExitStack() as ctx:
            m = {"hT": sb(ctx, "hT", [P, KD, T1]), "s5m": sb(ctx, "s5m", [P, 4, 4, P]),
                 "pw": sb(ctx, "pw", [P, 3, PAIRS, SC]), "dcol": sb(ctx, "dcol", [P, 4])}
            with ExitStack() as mid:
                m["qkvT"] = sb(mid, "qkvT", [P, 16, T1])
                m["gateT"] = sb(mid, "gateT", [P, 16, T1])
                loads = [(self.h[:, t, :], A["x"][0, t * P:(t + 1) * P, :]) for t in range(TT)]
                loads += [(self.h[0:META, TT, :], A["meta_tokens"]), (self.ident[:], self.const(1, "ident"))]
                self.s5_prepare(m, loads)
                with ExitStack() as n1:
                    g1 = sb(n1, "g1", [P, D])
                    self.norm_stage("n1", TILES1, self.h, None, m["hT"], "rms", g1, None, EPS,
                                    loads=[(g1[:], A["norm1_g"][0].partition_broadcast(P))])
                self.project_and_s5(m)
                if stop == "s5":
                    return
                m["v"] = sb(mid, "v", [P, TT + 1, ATT])
                m["oT"] = sb(mid, "oT", [P, H1, T1])
                m["alibi"] = sb(mid, "alibi", [P, T1])
                m["mlam"] = sb(mid, "mlam", [P, 1])
                self.recycle_semaphores()
                self.qk_norm_stage(m)
                self.diff_attention(m)
                self.mix_stage(m)
            if stop == "mix":
                return
            with ExitStack() as n2:
                g2 = sb(n2, "g2", [P, D])
                self.norm_stage("n2", TILES1, self.h, None, m["hT"], "rms", g2, None, EPS,
                                loads=[(g2[:], A["norm2_g"][0].partition_broadcast(P))])
            gT = sb(ctx, "ffgT", [P, FT, SEQ])
            self.ffn_stage(m["hT"], gT)

    def gla_project(self, m):
        nc, ps, W, A = self.nc, self.ps, self.W, self.A
        with self.new_stage() as ctx:
            sb = self.sb
            xT, qd, kn, kt = m["xT"], m["qd"], m["kn"], m["kt"]
            glow = sb(ctx, "gl_low", [16, SEQ])
            wup = sb(ctx, "gl_wup", [16, 512])
            bg = sb(ctx, "gl_bg", [P, GH])
            one = sb(ctx, "gl_one", [P, 1])
            restart = sb(ctx, "gl_restart", [P, SEQ])
            X, mn, e = (sb(ctx, n, [P, GH, SEQ]) for n in ("gl_x", "gl_mn", "gl_e"))
            loaded, start, qk_done, qk_out, low_done, low_out, z_done, z_out, e_done, cs_done, eb_done, dd_done, et_done, \
                v_done, v_out, r_done, r_out, own, actown = self.sems(
                    "gp", "loaded", "start", "qk_done", "qk_out", "low_done", "low_out", "z_done", "z_out", "e_done",
                    "cs_done", "eb_done", "dd_done", "et_done", "v_done", "v_out", "r_done", "r_out", "own", "act_own")
            loads = [(wup[:], A["gla_w_gate_up_2"][0]), (bg[:], A["gla_b_gate_2"].rearrange("o (t p) -> p (o t)", p=P)),
                     (restart[:], self.const(2, "restart"))]
            block = ctx.enter_context(nc.Block())

            @block.tensor
            def _(pe):
                for i in range(8):
                    n = self.n_gqk[i // 2]
                    W.arrived(pe, n)
                    self.fm_product(n, KD, 256, (i % 2) * P, lambda k, a, b: xT[:, k, a:b], [(i, 0, SEQ)], qk_done)
                    if i % 2:
                        W.retired_by(n, qk_done, i + 1)
                n = self.n_glow[0]
                W.arrived(pe, n)
                pe.wait_ge(qk_out, 1)
                self.fm_product(n, KD, 16, 0, lambda k, a, b: xT[:, k, a:b], [(0, 0, SEQ)], low_done, m=16)
                W.retired_by(n, low_done, 1)
                pe.wait_ge(low_out, 1)
                pe.wait_ge(loaded, 16 * len(loads))
                for hd in range(GH):
                    pe.wait_ge(qk_out, hd + 2)
                    nc.tensor.matmul(ps[:, 1 + hd, :], wup[:, hd * P:(hd + 1) * P], glow[:], start=True, stop=True)\
                        .then_inc(z_done, 1)
                pe.wait_ge(qk_out, 8)
                pe.wait_ge(z_out, GH)
                self.tm_product(pe, self.n_gv, lambda k, t: xT[:, k, P * t:P * (t + 1)], v_done)
                self.tm_product(pe, self.n_gr, lambda k, t: xT[:, k, P * t:P * (t + 1)], r_done,
                                bank_free=lambda t: pe.wait_ge(v_out, t + 1))

            @block.scalar
            def _(act):
                for to, frm in loads:
                    act.dma_start(to, frm).then_inc(loaded, 16)
                act.wait_ge(start, 1)
                for i in range(8):
                    act.wait_ge(qk_done, i + 1)
                    nc.scalar.copy((qd if i < 4 else kt)[:, i % 4, :], ps[:, i, :]).then_inc(qk_out, 1)
                act.wait_ge(low_done, 1)
                nc.scalar.copy(glow[:], ps[0:16, 0, :]).then_inc(low_out, 1)
                link = Chain(act, actown)
                for hd in range(GH):
                    act.wait_ge(z_out, hd + 1)
                    link(nc.scalar.activation(e[:, hd], e[:, hd], ACT.Exp, scale=-1.0))
                    nc.scalar.activation(e[:, hd], e[:, hd], ACT.Ln, bias=one[:]).then_inc(e_done, 1)
                for hd in range(GH):
                    act.wait_ge(cs_done, hd + 1)
                    nc.scalar.activation(e[:, hd], X[:, hd], ACT.Exp, scale=1 / 16).then_inc(eb_done, 1)
                    act.wait_ge(dd_done, hd + 1)
                    nc.scalar.activation(kn[:, hd], X[:, hd], ACT.Exp, scale=-1 / 16).then_inc(eb_done, 1)
                    nc.scalar.activation(mn[:, hd], mn[:, hd], ACT.Exp, scale=-1 / 16).then_inc(et_done, 1)
                for t in range(TT):
                    act.wait_ge(v_done, t + 1)
                    nc.scalar.copy(m["v"][:, t, :].rearrange("p (a c) -> p a c", a=2), ps[:, 2 * t:2 * t + 2, :])\
                        .then_inc(v_out, 1)
                for t in range(TT):
                    act.wait_ge(r_done, t + 1)
                    nc.scalar.activation(m["r"][:, t, :].rearrange("p (a c) -> p a c", a=2), ps[:, 2 * t:2 * t + 2, :],
                                         ACT.Silu).then_inc(r_out, 1)

            @block.vector
            def _(dve):
                link = Chain(dve, own)
                V = nc.vector
                V.memset(one[:], 1.0).then_inc(start, 1)
                dve.wait_ge(loaded, 16 * len(loads))
                for hd in range(GH):
                    dve.wait_ge(z_done, hd + 1)
                    link(V.tensor_scalar(X[:, hd], ps[:, 1 + hd, :], bg[:, hd:hd + 1], None, ALU.add))
                    link(V.tensor_scalar(mn[:, hd], X[:, hd], 0.0, None, ALU.min))
                    V.scalar_tensor_tensor(e[:, hd], mn[:, hd], -2.0, X[:, hd], ALU.mult, ALU.add).then_inc(z_out, 1)
                for hd in range(GH):
                    dve.wait_ge(e_done, hd + 1)
                    dve.wait_ge(z_out, GH)
                    link(V.tensor_tensor(mn[:, hd], mn[:, hd], e[:, hd], ALU.subtract))
                    V.tensor_tensor_scan(X[:, hd], restart[:], mn[:, hd], 0.0, ALU.mult, ALU.add).then_inc(cs_done, 1)
                    dve.wait_ge(cs_done, hd + 1)
                    c3 = X[:, hd].rearrange("p (n t) -> p n t", t=64)
                    V.tensor_tensor(mn[:, hd].rearrange("p (n t) -> p n t", t=64), c3,
                                    c3[:, :, 63:64].broadcast_to([P, 8, 64]), ALU.subtract).then_inc(dd_done, 1)
                dve.wait_ge(qk_out, 8)
                for hd in range(GH):
                    dve.wait_ge(eb_done, 2 * hd + 2)
                    V.tensor_copy(m["dec"][:, hd, :], e[:, hd].rearrange("p (n t) -> p n t", t=64)[:, :, 63]).then_inc(own, 1)
                    V.scalar_tensor_tensor(qd[:, hd], qd[:, hd], float(P) ** -0.5, e[:, hd], ALU.mult, ALU.mult).then_inc(own, 1)
                    V.tensor_tensor(kn[:, hd], kt[:, hd], kn[:, hd], ALU.mult).then_inc(own, 1)
                    link.n += 3
                    dve.wait_ge(own, link.n)
                    dve.wait_ge(et_done, hd + 1)
                    link(V.tensor_tensor(kt[:, hd], kt[:, hd], mn[:, hd], ALU.mult))

            @block.sync
            def _(sp):
                W.send(sp)

    def gla_chunks(self, m):
        nc, ps, W = self.nc, self.ps, self.W
        with self.new_stage() as ctx:
            sb = self.sb
            qd, kn, kt, v, o = m["qd"], m["kn"], m["kt"], m["v"], m["o"]
            ktok = sb(ctx, "gl_ktok", [P, TT, 512])
            S = sb(ctx, "gl_S", [P, 4, 64])
            state = sb(ctx, "gl_state", [P, 2, GH, 256])
            mask = sb(ctx, "gl_mask", [P, 64])
            loaded, zeroed, kt_done, kt_out, s_done, s_out, kv_done, st_done, o_done, o_out = self.sems(
                "gc", "loaded", "zeroed", "kt_done", "kt_out", "s_done", "s_out", "kv_done", "st_done", "o_done", "o_out")
            units = [(n, hd) for n in range(8) for hd in range(GH)]
            N = len(units)
            block = ctx.enter_context(nc.Block())

            def rows(n):
                return slice(64 * (n % 2), 64 * (n % 2) + 64)

            @block.tensor
            def _(pe):
                for t in range(TT):
                    for hd in range(GH):
                        ins = nc.tensor.transpose(ps[:, t, hd * P:(hd + 1) * P], kt[:, hd, t * P:(t + 1) * P], self.ident[:])
                    ins.then_inc(kt_done, 1)
                pe.wait_ge(kt_out, TT)
                for it in range(N + 2):
                    if it < N:
                        n, hd = units[it]
                        c = slice(64 * n, 64 * n + 64)
                        if it >= 2:
                            pe.wait_ge(s_out, it - 1)
                        nc.tensor.matmul(ps[rows(n), it % 2, 0:64], kn[:, hd, c], qd[:, hd, c], start=True, stop=True)\
                            .then_inc(s_done, 1)
                        if it >= 2:
                            pe.wait_ge(st_done, it - 1)
                        nc.tensor.matmul(ps[:, 6 + it % 2, 0:256], ktok[rows(n), n // 2, hd * P:(hd + 1) * P],
                                         v[rows(n), n // 2, 256 * hd:256 * hd + 256], start=True, stop=True)\
                            .then_inc(kv_done, 1)
                    u = it - 2
                    if u >= 0:
                        n, hd = units[u]
                        pe.wait_ge(s_out, u + 1)
                        if n >= 2:
                            pe.wait_ge(o_out, GH * (n // 2 - 1) + hd + 1)
                        dst = ps[rows(n), 2 + hd, 0:256]
                        ins = nc.tensor.matmul(dst, S[rows(n), u % 4, :], v[rows(n), n // 2, 256 * hd:256 * hd + 256],
                                               start=True, stop=(n == 0))
                        if n:
                            pe.wait_ge(st_done, u - 3)
                            ins = nc.tensor.matmul(dst, qd[:, hd, 64 * n:64 * n + 64], state[:, n % 2, hd, :],
                                                   start=False, stop=True)
                        ins.then_inc(o_done, 1)

            @block.scalar
            def _(act):
                act.dma_start(mask[:], self.const(2, "glamask")).then_inc(loaded, 16)
                for t in range(TT):
                    act.wait_ge(kt_done, t + 1)
                    nc.scalar.copy(ktok[:, t, :], ps[:, t, :]).then_inc(kt_out, 1)
                for t in range(TT):
                    for hd in range(GH):
                        act.wait_ge(o_done, GH * (2 * t + 1) + hd + 1)
                        nc.scalar.copy(o[:, t, 256 * hd:256 * hd + 256], ps[:, 2 + hd, 0:256])\
                            .then_inc(o_out, 1)

            @block.vector
            def _(dve):
                V = nc.vector
                V.memset(S[:], 0.0).then_inc(zeroed, 1)
                dve.wait_ge(zeroed, 1)
                dve.wait_ge(loaded, 16)
                for it in range(N):
                    n, hd = units[it]
                    dve.wait_ge(s_done, it + 1)
                    if it >= 4:
                        dve.wait_ge(o_done, it - 3)
                    V.copy_predicated(S[rows(n), it % 4, :], mask[rows(n), :].bitcast(U32), ps[rows(n), it % 2, 0:64])\
                        .then_inc(s_out, 1)
                    dve.wait_ge(kv_done, it + 1)
                    new = state[:, (n + 1) % 2, hd, :]
                    if n == 0:
                        V.tensor_copy(new, ps[:, 6 + it % 2, 0:256]).then_inc(st_done, 1)
                    else:
                        dve.wait_ge(st_done, it - 3)
                        if n >= 2:
                            dve.wait_ge(o_done, it - 3)
                        V.scalar_tensor_tensor(new, state[:, n % 2, hd, :], m["dec"][:, hd, n:n + 1],
                                               ps[:, 6 + it % 2, 0:256], ALU.mult, ALU.add).then_inc(st_done, 1)

            @block.sync
            def _(sp):
                W.send(sp)

    def gla_out(self, m):
        nc, ps, W, A, h = self.nc, self.ps, self.W, self.A, self.h
        with self.new_stage() as ctx:
            sb = self.sb
            o, oT = m["o"], m["xT"]
            junk = sb(ctx, "go_junk", [P, 256])
            st = sb(ctx, "go_st", [P, 3, 16])
            gn = sb(ctx, "go_gn", [P, 256])
            eps = sb(ctx, "go_eps", [P, 1])
            loaded, start, rs, o_ready, turned, t_out, y_done, y_out, own, actown = self.sems(
                "go", "loaded", "start", "rs", "o_ready", "turned", "t_out", "y_done", "y_out", "own", "act_own")
            block = ctx.enter_context(nc.Block())

            @block.tensor
            def _(pe):
                for t in range(TT):
                    pe.wait_ge(o_ready, t + 1)
                    for k in range(KD):
                        ins = nc.tensor.transpose(ps[:, 2 * t + k // 4, (k % 4) * P:(k % 4) * P + P], o[:, t, k * P:(k + 1) * P],
                                                  self.ident[:])
                    ins.then_inc(turned, 1)
                pe.wait_ge(t_out, TT)
                self.tm_product(pe, self.n_go, lambda k, t: oT[:, k, P * t:P * (t + 1)], y_done)

            @block.scalar
            def _(act):
                act.dma_start(gn[:], A["gla_norm_g_2"][0].partition_broadcast(P)).then_inc(loaded, 16)
                act.wait_ge(start, 1)
                link = Chain(act, actown)
                for t in range(TT):
                    for hd in range(GH):
                        link(nc.scalar.activation(junk[:], o[:, t, 256 * hd:256 * hd + 256], ACT.Square,
                                                  accum_out=st[:, 0, 4 * t + hd:4 * t + hd + 1]))
                link(nc.scalar.activation(st[:, 1], st[:, 0], ACT.Ln, bias=eps[:], scale=1 / 256))
                nc.scalar.activation(st[:, 2], st[:, 1], ACT.Exp, scale=-0.5).then_inc(rs, 1)
                for t in range(TT):
                    act.wait_ge(turned, t + 1)
                    nc.scalar.copy(oT[:, :, P * t:P * (t + 1)],
                                   ps[:, 2 * t:2 * t + 2, :].rearrange("p b (k c) -> p (b k) c", k=4)).then_inc(t_out, 1)

            @block.vector
            def _(dve):
                link = Chain(dve, own)
                V = nc.vector
                V.memset(eps[:], LN_EPS).then_inc(start, 1)
                dve.wait_ge(loaded, 16)
                dve.wait_ge(rs, 1)
                for t in range(TT):
                    for hd in range(GH):
                        x = o[:, t, 256 * hd:256 * hd + 256]
                        link(V.scalar_tensor_tensor(x, x, st[:, 2, 4 * t + hd:4 * t + hd + 1], gn[:], ALU.mult, ALU.mult))
                    V.tensor_tensor(o[:, t, :], o[:, t, :], m["r"][:, t, :], ALU.mult).then_inc(o_ready, 1)
                for t in range(TT):
                    dve.wait_ge(y_done, t + 1)
                    x = h[:, t, :].rearrange("p (a c) -> p a c", a=2)
                    V.scalar_tensor_tensor(x, x, ALPHA, ps[:, 2 * t:2 * t + 2, :], ALU.mult, ALU.add).then_inc(y_out, 1)

            @block.sync
            def _(sp):
                W.send(sp)

    def moe_stage(self, tag, units, next_held, xT, first):
        nc, ps, W, A, h = self.nc, self.ps, self.W, self.A, self.h
        with self.new_stage() as ctx:
            sb = self.sb
            wr = sb(ctx, tag + "_wr", [P, KD, NE])
            br = sb(ctx, tag + "_br", [P, NE])
            s, biased, sel, w, gate = (sb(ctx, f"{tag}_{n}", [P, TT * NE]) for n in ("s", "biased", "sel", "w", "gate"))
            beats = sb(ctx, tag + "_beats", [P, 4, 16, 4])
            gs, gsel, place = (sb(ctx, f"{tag}_{n}", [P, 16]) for n in ("gs", "gsel", "place"))
            ws = sb(ctx, tag + "_ws", [P, 2, TT])
            before, ones = sb(ctx, tag + "_before", [P, P]), sb(ctx, tag + "_ones", [P, P])
            count, nblk, first_blk = (sb(ctx, f"{tag}_{n}", [P, NGRP]) for n in ("count", "nblk", "first_blk"))
            blockno, gidf = sb(ctx, tag + "_blockno", [P, NB]), sb(ctx, tag + "_gidf", [P, NB])
            gid = sb(ctx, tag + "_gid", [P, NB], I32)
            slotf = sb(ctx, tag + "_slotf", [P, TT])
            slot = sb(ctx, tag + "_slot", [P, TT], U32)
            rows = sb(ctx, tag + "_rows", [P, TT, XROW])
            xb = sb(ctx, tag + "_xb", [P, 2, XROW])
            gw = sb(ctx, tag + "_gw", [P, 2, EG])
            xbT = sb(ctx, tag + "_xbT", [P, 2, KD, P])
            sg = sb(ctx, tag + "_sg", [P, 2, 256])
            hb = sb(ctx, tag + "_hb", [P, 2, 256])
            hT = sb(ctx, tag + "_hT", [P, 2, 2, P])
            yb = sb(ctx, tag + "_yb", [P, 2, D])
            yg = sb(ctx, tag + "_yg", [P, TT, D])
            (loaded, zeroed, ones_set, rows_in, lg_done, s_out, g_done, cum_done, gid_done, slot_done, sent, xt_done, xt_out,
             gu_done, sg_out, h_done, t_done, t_out, d_done, y_out, y_in, h_out, own) = self.sems(
                tag, "loaded", "zeroed", "ones_set", "rows_in", "lg_done", "s_out", "g_done", "cum_done", "gid_done", "slot_done",
                "sent", "xt_done", "xt_out", "gu_done", "sg_out", "h_done", "t_done", "t_out", "d_done",
                "y_out", "y_in", "h_out", "own")
            x_in, y_stored = self.sems(tag + "_x_in", 0, 1), self.sems(tag + "_y_stored", 0, 1)
            loads = [(wr[:], A["moe_w_router_2"].rearrange("(k p) e -> p k e", p=P)),
                     (br[:], A["moe_b_router_2"].partition_broadcast(P)),
                     (before[:], self.const(2, "before")), (blockno[:], self.const(2, "block"))]
            NU = len(units)
            block = ctx.enter_context(nc.Block())

            @block.tensor
            def _(pe):
                pe.wait_ge(loaded, 16 * len(loads))
                for t in range(TT):
                    for k in range(KD):
                        ins = nc.tensor.matmul(ps[:, 0, NE * t:NE * (t + 1)], xT[:, k, P * t:P * (t + 1)], wr[:, k, :],
                                               start=(k == 0), stop=(k == KD - 1))
                ins.then_inc(lg_done, 1)
                pe.wait_ge(g_done, 1)
                pe.wait_ge(ones_set, 1)
                for t in range(TT):
                    nc.tensor.matmul(ps[:, 1, 4 * t:4 * t + 4], before[:], gsel[:, 4 * t:4 * t + 4], start=True, stop=(t == 0))
                    for t2 in range(t):
                        nc.tensor.matmul(ps[:, 1, 4 * t:4 * t + 4], ones[:], gsel[:, 4 * t2:4 * t2 + 4], start=False,
                                         stop=(t2 == t - 1))
                for t in range(TT):
                    ins = nc.tensor.matmul(ps[:, 1, 16:20], ones[:], gsel[:, 4 * t:4 * t + 4], start=(t == 0), stop=(t == TT - 1))
                ins.then_inc(cum_done, 1)

                def turn_x(blk, q):
                    if q == 0:
                        pe.wait_ge(x_in[blk % 2], 16 * (blk // 2 + 1))
                    if 2 * blk + q:
                        pe.wait_ge(xt_out, 2 * blk + q)
                    for k in range(4):
                        ins = nc.tensor.transpose(ps[:, 7, P * k:P * (k + 1)], xb[:, blk % 2, P * (4 * q + k):P * (4 * q + k + 1)],
                                                  self.ident[:])
                    ins.then_inc(xt_done, 1)

                turn_x(0, 0)
                turn_x(0, 1)
                for it in range(NU + 2):
                    if it < NU:
                        blk, e = divmod(it, EG)
                        if e == 0:
                            pe.wait_ge(xt_out, 2 * blk + 2)
                        if it >= 2:
                            pe.wait_ge(h_done, it - 1)
                        elif it == 1:
                            pe.wait_ge(slot_done, 1)
                        for half in range(2):
                            n = units[it][half]
                            W.arrived(pe, n)
                            v = slab_view(4, 512)(W.slot(n))
                            for k in range(4):
                                ins = nc.tensor.matmul(ps[:, it % 2, :], xbT[:, blk % 2, 4 * half + k, :], v[:, k, :],
                                                       start=(half == 0 and k == 0), stop=(half == 1 and k == 3))
                            if half == 0:
                                W.retire(n, ins)
                        ins.then_inc(gu_done, 1)
                        W.retired_by(n, gu_done, it + 1)
                        if e in (1, 2) and blk + 1 < NB:
                            turn_x(blk + 1, e - 1)
                    u = it - 1
                    if 0 <= u < NU:
                        pe.wait_ge(h_done, u + 1)
                        if u:
                            pe.wait_ge(t_out, u)
                        for k in range(2):
                            ins = nc.tensor.transpose(ps[:, 2, P * k:P * (k + 1)], hb[:, u % 2, P * k:P * (k + 1)], self.ident[:])
                        ins.then_inc(t_done, 1)
                    u = it - 2
                    if u >= 0:
                        blk, e = divmod(u, EG)
                        n = units[u][2]
                        W.arrived(pe, n)
                        pe.wait_ge(t_out, u + 1)
                        if e == 0 and blk >= 2:
                            pe.wait_ge(y_out, blk - 1)
                        v = slab_view(2, D)(W.slot(n))
                        for k in range(2):
                            for hf in range(2):
                                ins = nc.tensor.matmul(ps[:, 3 + 2 * (blk % 2) + hf, :], hT[:, u % 2, k, :],
                                                       v[:, k, 512 * hf:512 * hf + 512], start=(e == 0 and k == 0),
                                                       stop=(e == EG - 1 and k == 1))
                        ins.then_inc(d_done, 1)
                        W.retired_by(n, d_done, u + 1)

            @block.scalar
            def _(act):
                for to, frm in loads:
                    act.dma_start(to, frm).then_inc(loaded, 16)
                for t in range(TT):
                    nc.scalar.copy(rows[:, t, 0:D], h[:, t, :]).then_inc(rows_in, 1)
                act.wait_ge(lg_done, 1)
                nc.scalar.activation(s[:], ps[:, 0, 0:TT * NE], ACT.Sigmoid).then_inc(s_out, 1)

                def load_x(blk):
                    if blk >= 2:
                        act.wait_ge(xt_done, 2 * (blk - 1))
                        act.wait_ge(h_done, EG * (blk - 1))
                    act.dma_start(xb[:, blk % 2, :], self.x_slots[P * blk:P * (blk + 1), :]).then_inc(x_in[blk % 2], 16)

                def copy_x(blk, q):
                    act.wait_ge(xt_done, 2 * blk + q + 1)
                    nc.scalar.copy(xbT[:, blk % 2, 4 * q:4 * q + 4, :].rearrange("p k c -> p (k c)"), ps[:, 7, :])\
                        .then_inc(xt_out, 1)

                act.wait_ge(sent, 16 * (TT + (NB if first else 0)))
                load_x(0)
                load_x(1)
                copy_x(0, 0)
                copy_x(0, 1)
                for it in range(NU + 1):
                    if it < NU:
                        blk, e = divmod(it, EG)
                        act.wait_ge(gu_done, it + 1)
                        if it >= 2:
                            act.wait_ge(h_done, it - 1)
                        nc.scalar.activation(sg[:, it % 2], ps[:, it % 2, 0:256], ACT.Silu).then_inc(sg_out, 1)
                        if e in (1, 2) and blk + 1 < NB:
                            copy_x(blk + 1, e - 1)
                    u = it - 1
                    if u >= 0:
                        act.wait_ge(t_done, u + 1)
                        if u >= 2:
                            act.wait_ge(d_done, u - 1)
                        nc.scalar.copy(hT[:, u % 2].rearrange("p k c -> p (k c)"), ps[:, 2, 0:256]).then_inc(t_out, 1)
                        if u % EG == EG - 1 and u // EG + 2 < NB:
                            load_x(u // EG + 2)

            @block.gpsimd
            def _(pool):
                if first:
                    nc.gpsimd.memset(yg[:, 0:2, :], 0.0).then_inc(zeroed, 1)
                    pool.wait_ge(zeroed, 1)
                    z = yg[:, 0:2, :].rearrange("p a c -> p (a c)")[:, 0:XROW]
                    for blk in range(NB):
                        pool.dma_start(self.x_slots[P * blk:P * (blk + 1), :], z).then_inc(sent, 16)
                base = 16 * NB if first else 0
                if first:
                    pool.wait_ge(sent, base)
                pool.wait_ge(slot_done, 1)
                for t in range(TT):
                    nc.gpsimd.indirect_dma_start(self.x_slots, bass.IndirectOffsetOnAxis(slot[:, t:t + 1], 0),
                                                 rows[:, t, :], None).then_inc(sent, 16)
                for blk in range(NB):
                    pool.wait_ge(y_out, blk + 1)
                    pool.dma_start(self.y_slots[P * blk:P * (blk + 1), :], yb[:, blk % 2, :]).then_inc(y_stored[blk % 2], 16)
                for i in range(2):
                    pool.wait_ge(y_stored[i], 16 * ((NB + 1 - i) // 2))
                for t in range(TT):
                    nc.gpsimd.indirect_dma_start(yg[:, t, :], None, self.y_slots,
                                                 bass.IndirectOffsetOnAxis(slot[:, t:t + 1], 0)).then_inc(y_in, 16)

            @block.vector
            def _(dve):
                link = Chain(dve, own)
                V = nc.vector

                def rank(dst, x, n, below):
                    link(V.memset(beats[:, :, 0:n, :], 0.0))
                    for c in range(4):
                        for a, b, op in ((0, c, ALU.is_gt), (c + 1, 4, ALU.is_ge)):
                            if a < b:
                                link(V.tensor_tensor(beats[:, c, 0:n, a:b], x[:, :, c:c + 1].broadcast_to([P, n, b - a]),
                                                     x[:, :, a:b], op))
                    for c in range(1, 4):
                        link(V.tensor_tensor(beats[:, 0, 0:n, :], beats[:, 0, 0:n, :], beats[:, c, 0:n, :], ALU.add))
                    link(V.tensor_scalar(dst, beats[:, 0, 0:n, :], below, None, ALU.is_lt))

                def by4(x, n=16):
                    return x[:, :].rearrange("p (a b) -> p a b", a=n)

                V.memset(ones[:], 1.0).then_inc(ones_set, 1)
                dve.wait_ge(loaded, 16 * len(loads))
                dve.wait_ge(s_out, 1)
                link(V.tensor_tensor(by4(biased, TT), by4(s, TT), br[:].unsqueeze(1).broadcast_to([P, TT, NE]), ALU.add))
                rank(by4(sel), by4(biased), 16, 2.0)
                link(V.tensor_tensor(w[:], sel[:], biased[:], ALU.mult))
                link(V.reduce_sum(gs[:], by4(w), AX.X))
                rank(by4(gsel, 4), by4(gs, 4), 4, 1.0)
                link(V.tensor_copy(place[:], gsel[:]))
                link(V.tensor_copy(gs[:], gsel[:]))
                V.tensor_copy(count[:, 0:1], gsel[:, 0:1]).then_inc(g_done, 1)
                dve.wait_ge(g_done, 1)
                link(V.tensor_tensor(w[:], sel[:], s[:], ALU.mult))
                link(V.tensor_tensor(by4(w), by4(w), gs[:].unsqueeze(2).broadcast_to([P, 16, 4]), ALU.mult))
                link(V.reduce_sum(ws[:, 0], by4(w, TT), AX.X))
                link(V.reciprocal(ws[:, 1], ws[:, 0]))
                link(V.tensor_tensor(by4(gate, TT), by4(w, TT), ws[:, 1].unsqueeze(2).broadcast_to([P, TT, NE]), ALU.mult))
                link(V.reduce_sum(rows[:, :, D:XROW], gate[:].rearrange("p (t g e) -> p t e g", t=TT, g=NGRP), AX.X))
                dve.wait_ge(cum_done, 1)
                link(V.tensor_copy(count[:], ps[:, 1, 16:20]))
                link(V.tensor_scalar(nblk[:], count[:], 0.0, None, ALU.is_gt))
                for k in range(1, SEQ // P):
                    link(V.scalar_tensor_tensor(nblk[:], count[:], float(P * k), nblk[:], ALU.is_gt, ALU.add))
                link(V.memset(first_blk[:], 0.0))
                for g in range(1, NGRP):
                    link(V.tensor_tensor(first_blk[:, g:g + 1], first_blk[:, g - 1:g], nblk[:, g - 1:g], ALU.add))
                link(V.tensor_scalar(gidf[:], blockno[:], first_blk[:, 1:2], None, ALU.is_ge))
                for g in range(2, NGRP):
                    link(V.scalar_tensor_tensor(gidf[:], blockno[:], first_blk[:, g:g + 1], gidf[:], ALU.is_ge, ALU.add))
                V.tensor_copy(gid[:], gidf[:]).then_inc(gid_done, 1)
                link(V.tensor_scalar(first_blk[:], first_blk[:], float(P), None, ALU.mult))
                link(V.tensor_tensor(by4(gs, TT), by4(ps[:, 1, 0:16], TT), first_blk[:].unsqueeze(1).broadcast_to([P, TT, NGRP]),
                                     ALU.add))
                link(V.tensor_tensor(gs[:], gs[:], place[:], ALU.mult))
                link(V.reduce_sum(slotf[:], by4(gs, TT), AX.X))
                dve.wait_ge(rows_in, TT)
                V.tensor_copy(slot[:], slotf[:]).then_inc(slot_done, 1)
                for it in range(NU):
                    blk, e = divmod(it, EG)
                    dve.wait_ge(sg_out, it + 1)
                    if e == 0:
                        dve.wait_ge(x_in[blk % 2], 16 * (blk // 2 + 1))
                        link(V.tensor_copy(gw[:, blk % 2, :], xb[:, blk % 2, D:XROW]))
                    if it >= 2:
                        dve.wait_ge(t_done, it - 1)
                    V.scalar_tensor_tensor(hb[:, it % 2], sg[:, it % 2], gw[:, blk % 2, e:e + 1], ps[:, it % 2, 256:512],
                                           ALU.mult, ALU.mult).then_inc(h_done, 1)
                    done = [it - 3] if it < NU - 1 else [it]
                    for u in done:
                        if u >= 0 and u % EG == EG - 1:
                            blk = u // EG
                            dve.wait_ge(d_done, u + 1)
                            if blk >= 2:
                                dve.wait_ge(y_stored[blk % 2], 16 * (blk // 2))
                            V.tensor_copy(yb[:, blk % 2, :].rearrange("p (a c) -> p a c", a=2),
                                          ps[:, 3 + 2 * (blk % 2):5 + 2 * (blk % 2), :]).then_inc(y_out, 1)
                for t in range(TT):
                    dve.wait_ge(y_in, 16 * TT)
                    V.scalar_tensor_tensor(h[:, t, :], h[:, t, :], ALPHA, yg[:, t, :], ALU.mult, ALU.add).then_inc(h_out, 1)

            @block.sync
            def _(sp):
                sp.wait_ge(gid_done, 1)
                self.group = [sp.value_load(gid[0:1, b:b + 1], min_val=0, max_val=NGRP - 1) for b in range(NB)]
                W.held = next_held
                W.send(sp)

    def second_block(self, out, stop=None):
        A, sb = self.A, self.sb
        with ExitStack() as ctx:
            xT = sb(ctx, "xT", [P, KD, SEQ])
            g, b = sb(ctx, "ln_g", [P, D]), sb(ctx, "ln_b", [P, D])
            h = self.h

            def ln_loads(i, j):
                return [(g[:], A["ln_g_2"][i, j].partition_broadcast(P)), (b[:], A["ln_b_2"][i, j].partition_broadcast(P))]

            self.recycle_semaphores()
            self.norm_stage("x0", TILES2, h, None, xT, None, None, None, 0.0)
            with ExitStack() as gl:
                m = {"xT": xT, "qd": sb(gl, "qd", [P, GH, SEQ]), "kn": sb(gl, "kn", [P, GH, SEQ]),
                     "kt": sb(gl, "kt", [P, GH, SEQ]), "v": sb(gl, "gv", [P, TT, D]), "r": sb(gl, "gr", [P, TT, D]),
                     "dec": sb(gl, "dec", [P, GH, 8])}
                self.gla_project(m)
                m["o"] = sb(gl, "go", [P, TT, D])
                self.gla_chunks(m)
                self.gla_out(m)
            if stop == "gla":
                return
            self.norm_stage("l0", TILES2, h, h, xT, "ln", g, b, LN_EPS, loads=ln_loads(0, 0))
            if stop == "ln0":
                return
            self.moe_stage("m0", self.n_moe[0], self.n_moe[1][0][0], xT, True)
            if stop == "moe0":
                return
            self.recycle_semaphores()
            self.norm_stage("l1", TILES2, h, h, xT, "ln", g, b, LN_EPS, loads=ln_loads(0, 1))
            self.nsa(xT)
            if stop == "nsa":
                return
            self.recycle_semaphores()
            self.norm_stage("l2", TILES2, h, h, xT, "ln", g, b, LN_EPS, loads=ln_loads(1, 0))
            self.moe_stage("m1", self.n_moe[1], None, xT, False)
            self.norm_stage("l3", TILES2, h, h, None, "ln", g, b, LN_EPS, loads=ln_loads(1, 1), to_dram=out[0])

    def nsa(self, xT):
        A, sb, h = self.A, self.sb, self.h
        with ExitStack() as ctx:
            m = {"xT": xT, "qT": sb(ctx, "nqT", [P, KD, SEQ]), "kd": sb(ctx, "nkd", [P, 2, NG, SEQ]),
                 "vsw": sb(ctx, "nvsw", [P, TT, 512]), "gates": sb(ctx, "ngates", [P, TT, 48]),
                 "o": sb(ctx, "no_o", [P, TT, D]), "kcT": sb(ctx, "nkcT", [P, NG, NCMP]), "vc": sb(ctx, "nvc", [P, NG, 256])}
            with ExitStack() as cc:
                m["kpair"] = sb(cc, "nkpair", [P, 2, 2, NG, SEQ // 2])
                self.nsa_project(m)
                self.nsa_compress(m)
            self.nsa_values_and_compressed(m)
            self.nsa_attention(m)
            self.nsa_out(m)

    def nsa_project(self, m):
        nc, ps, W, A = self.nc, self.ps, self.W, self.A
        with self.new_stage() as ctx:
            sb = self.sb
            xT, kd = m["xT"], m["kd"]
            raw = sb(ctx, "np_raw", [P, 2, SEQ])
            t2 = sb(ctx, "np_t2", [P, 2, SEQ])
            cos, sin = sb(ctx, "np_cos", [P, SEQ]), sb(ctx, "np_sin", [P, SEQ])
            swap = sb(ctx, "np_swap", [P, P])
            pe_ = sb(ctx, "np_pe", [P, 32])
            kc = sb(ctx, "np_kc", [P, 2, 2, 2, 2, SEQ // 2])
            loaded, pr_done, raw_out, sw_done, rope_done, kc_out, dup, paired, own, cosd = self.sems(
                "np", "loaded", "pr_done", "raw_out", "sw_done", "rope_done", "kc_out", "dup", "paired", "own", "cos_done")
            loads = [(cos[:], self.const(2, "cos")), (sin[:], self.const(2, "sin")), (swap[:], self.const(2, "swap"))]
            loads += [(pe_[64 * g:64 * g + 64, :], A["nsa_cmp_pe_2"].rearrange("o t d -> d (o t)")) for g in range(2)]
            rope = [(self.n_nq[i // 2], i % 2, ("q", i)) for i in range(8)]
            flat = [(self.n_nkv[j], i, (j, i)) for j in range(2) for i in range(2)]
            rope2 = [(self.n_nkv[2 + j], i, ("k", j, i)) for j in range(2) for i in range(2)]
            tiles = [("rope", *x) for x in rope] + [("flat", *x) for x in flat] + [("rope", *x) for x in rope2]
            NT = len(tiles)
            nrope = [sum(t[0] == "rope" for t in tiles[:i]) for i in range(NT + 1)]
            block = ctx.enter_context(nc.Block())

            @block.tensor
            def _(pe):
                for it in range(NT + 1):
                    if it < NT:
                        kind, n, i, what = tiles[it]
                        W.arrived(pe, n)
                        if it >= 4:
                            r = nrope[it - 3]
                            if r:
                                pe.wait_ge(raw_out, r)
                            if it - 3 - r:
                                pe.wait_ge(kc_out, it - 3 - r)
                        self.fm_product(n, KD, 256, i * P, lambda k, a, b: xT[:, k, a:b], [(it % 4, 0, SEQ)], pr_done)
                        if i:
                            W.retired_by(n, pr_done, it + 1)
                    u = it - 1
                    if u >= 0 and tiles[u][0] == "rope":
                        r = nrope[u]
                        if r == 0:
                            pe.wait_ge(loaded, 16 * len(loads))
                        pe.wait_ge(raw_out, r + 1)
                        if r >= 2:
                            pe.wait_ge(rope_done, r - 1)
                        nc.tensor.matmul(ps[:, 4 + r % 2, :], swap[:], raw[:, r % 2], start=True, stop=True)\
                            .then_inc(sw_done, 1)

            @block.scalar
            def _(act):
                for to, frm in loads:
                    act.dma_start(to, frm).then_inc(loaded, 16)
                for it, (kind, n, i, what) in enumerate(tiles):
                    if kind == "rope":
                        r = nrope[it]
                        act.wait_ge(pr_done, it + 1)
                        if r >= 2:
                            act.wait_ge(cosd, r - 1)
                            act.wait_ge(sw_done, r - 1)
                        nc.scalar.copy(raw[:, r % 2], ps[:, it % 4, :]).then_inc(raw_out, 1)

            @block.vector
            def _(dve):
                link = Chain(dve, own)
                V = nc.vector
                dve.wait_ge(loaded, 16 * len(loads))
                flats = 0
                for it, (kind, n, i, what) in enumerate(tiles):
                    if kind == "flat":
                        dve.wait_ge(pr_done, it + 1)
                        src = ps[:, it % 4, :].rearrange("p (n t e) -> p e n t", t=8, e=2)
                        for half in range(2):
                            for e in range(2):
                                offs = pe_[:, 16 * half:16 * half + 16].rearrange("p (t e) -> p e t", e=2)[:, e]
                                ins = V.tensor_tensor(kc[:, what[0], half, what[1], e, :].rearrange("p (n t) -> p n t", t=8),
                                                      src[:, e], offs.unsqueeze(1).broadcast_to([P, 32, 8]), ALU.add)
                                if half and e:
                                    ins.then_inc(kc_out, 1)
                                else:
                                    link(ins)
                        continue
                    r = nrope[it]
                    s = r % 2
                    scale = 0.125 if what[0] == "q" else 1.0
                    dve.wait_ge(raw_out, r + 1)
                    if r:
                        dve.wait_ge(rope_done, r)
                    V.scalar_tensor_tensor(t2[:, 0], raw[:, s], scale, cos[:], ALU.mult, ALU.mult).then_inc(cosd, 1)
                    dve.wait_ge(sw_done, r + 1)
                    link(V.scalar_tensor_tensor(t2[:, 1], ps[:, 4 + s, :], scale, sin[:], ALU.mult, ALU.mult))
                    dve.wait_ge(cosd, r + 1)
                    if what[0] == "q":
                        V.tensor_tensor(m["qT"][:, what[1], :], t2[:, 0], t2[:, 1], ALU.add).then_inc(rope_done, 1)
                    else:
                        for g in range(2):
                            q = slice(64 * g, 64 * g + 64)
                            ins = V.tensor_tensor(kd[q, what[1], 2 * what[2] + g, :], t2[q, 0], t2[q, 1], ALU.add)
                            if g:
                                ins.then_inc(rope_done, 1)
                            else:
                                link(ins)

            @block.sync
            def _(sp):
                W.send(sp)
                for kv in range(2):
                    sp.wait_ge(kc_out, 2 * kv + 2)
                    for half in range(2):
                        for gp in range(2):
                            for e in range(2):
                                to = m["kpair"][64 * e:64 * e + 64, kv, half].rearrange("p (u g) n -> p g u n", g=2)[:, gp]
                                sp.dma_start(to, kc[64 * gp:64 * gp + 64, kv, half, :, e, :]).then_inc(paired, 16)
                for j in range(2):
                    for i in range(2):
                        sp.wait_ge(rope_done, 8 + 2 * j + i + 1)
                        for g in range(2):
                            a, b = slice(64 * g, 64 * g + 64), slice(64 - 64 * g, 128 - 64 * g)
                            sp.dma_start(kd[b, j, 2 * i + g, :], kd[a, j, 2 * i + g, :]).then_inc(dup, 16)
                sp.wait_ge(dup, 16 * 8)
                sp.wait_ge(paired, 16 * 16)

    def nsa_compress(self, m):
        nc, ps, W, A = self.nc, self.ps, self.W, self.A
        with self.new_stage() as ctx:
            sb = self.sb
            C4 = NG * NCMP
            h1 = sb(ctx, "cm_h1", [P, 2, 2, C4])
            h1v = sb(ctx, "cm_h1v", [P, 2, NG, 4, 32])
            w2k = sb(ctx, "cm_w2k", [P, 2, P])
            w2v = sb(ctx, "cm_w2v", [P, 2, 64])
            raw = sb(ctx, "cm_raw", [P, C4])
            t1 = sb(ctx, "cm_t1", [P, NG, NCMP])
            cs = sb(ctx, "cm_cs", [P, 2 * NCMP])
            swap = sb(ctx, "cm_swap", [P, P])
            loaded, h_done, h_out, rep_done, k_done, k_out, sw_done, v_done, v_out, zeroed, own = self.sems(
                "cm", "loaded", "h_done", "h_out", "rep_done", "k_done", "k_out", "sw_done", "v_done", "v_out", "zeroed", "own")
            w2 = A["nsa_w_cmp_k2_2"][0].rearrange("(k p) d -> p k d", p=P)
            loads = [(w2k[:, :, 0:64], w2), (w2k[:, :, 64:128], w2),
                     (w2v[:], A["nsa_w_cmp_v2_2"][0].rearrange("(k p) d -> p k d", p=P)),
                     (cs[:, 0:NCMP], self.const(2, "coscmp")), (cs[:, NCMP:2 * NCMP], self.const(2, "sincmp")),
                     (swap[:], self.const(2, "swap"))]
            block = ctx.enter_context(nc.Block())

            @block.tensor
            def _(pe):
                for kv in range(2):
                    for q in range(2):
                        n = self.n_cmp[kv][q]
                        W.arrived(pe, n)
                        w = slab_view(8, 256)(W.slot(n))
                        x = m["kpair"][:, kv, q].rearrange("p g (n t) -> p g n t", t=8)
                        for k in range(8):
                            for hd in range(2):
                                ins = nc.tensor.matmul(ps[:, 2 * kv + hd, 0:C4], w[:, k, hd * P:(hd + 1) * P],
                                                       x[:, :, q:q + NCMP, k], start=(q == 0 and k == 0),
                                                       stop=(q == 1 and k == 7))
                        if q == 0:
                            W.retire(n, ins)
                        else:
                            ins.then_inc(h_done, 1)
                            W.retired_by(n, h_done, kv + 1)
                pe.wait_ge(loaded, 16 * len(loads))
                pe.wait_ge(h_out, 1)
                for k in range(2):
                    ins = nc.tensor.matmul(ps[:, 4, 0:C4], w2k[:, k, :], h1[:, 0, k], start=(k == 0), stop=(k == 1))
                ins.then_inc(k_done, 1)
                pe.wait_ge(rep_done, 1)
                for g in range(NG):
                    for k in range(2):
                        ins = nc.tensor.matmul(ps[:, 5, 64 * g:64 * g + 64], h1v[:, k, g].rearrange("p h n -> p (h n)"),
                                               w2v[:, k, :], start=(k == 0), stop=(k == 1))
                ins.then_inc(v_done, 1)
                pe.wait_ge(k_out, 1)
                nc.tensor.matmul(ps[:, 6, 0:C4], swap[:], raw[:], start=True, stop=True).then_inc(sw_done, 1)

            @block.scalar
            def _(act):
                for to, frm in loads:
                    act.dma_start(to, frm).then_inc(loaded, 16)
                for kv in range(2):
                    act.wait_ge(h_done, kv + 1)
                    nc.scalar.activation(h1[:, kv], ps[:, 2 * kv:2 * kv + 2, 0:C4], ACT.Silu).then_inc(h_out, 1)
                act.wait_ge(k_done, 1)
                nc.scalar.copy(raw[:], ps[:, 4, 0:C4]).then_inc(k_out, 1)
                act.wait_ge(zeroed, 2)
                act.wait_ge(v_done, 1)
                for hh in range(4):
                    r = slice(32 * hh, 32 * hh + 32)
                    nc.scalar.copy(m["vc"][r, :, 64 * hh:64 * hh + 64], ps[r, 5, 0:256].rearrange("p (g d) -> p g d", g=NG))\
                        .then_inc(v_out, 1)

            @block.gpsimd
            def _(pool):
                nc.gpsimd.memset(h1v[:], 0.0).then_inc(zeroed, 1)
                nc.gpsimd.memset(m["vc"][:], 0.0).then_inc(zeroed, 1)

            @block.vector
            def _(dve):
                link = Chain(dve, own)
                V = nc.vector
                dve.wait_ge(loaded, 16 * len(loads))
                dve.wait_ge(zeroed, 2)
                dve.wait_ge(h_out, 2)
                for k in range(2):
                    ins = V.tensor_copy(h1v[:, k, :, :, 0:NCMP], h1[:, 1, k].rearrange("p (g n) -> p g n", g=NG)
                                        .unsqueeze(2).broadcast_to([P, NG, 4, NCMP]))
                    if k:
                        ins.then_inc(rep_done, 1)
                    else:
                        link(ins)
                dve.wait_ge(k_out, 1)

                def by4(x):
                    return x.rearrange("p (g n) -> p g n", g=4)

                def table(i):
                    return cs[:, i * NCMP:(i + 1) * NCMP].unsqueeze(1).broadcast_to([P, 4, NCMP])

                link(V.tensor_tensor(t1[:], by4(raw[:]), table(0), ALU.mult))
                dve.wait_ge(sw_done, 1)
                link(V.tensor_tensor(m["kcT"][:], by4(ps[:, 6, 0:C4]), table(1), ALU.mult))
                link(V.tensor_tensor(m["kcT"][:], m["kcT"][:], t1[:], ALU.add))

            @block.sync
            def _(sp):
                W.send(sp)

    def nsa_values_and_compressed(self, m):
        nc, ps, W, A = self.nc, self.ps, self.W, self.A
        with self.new_stage() as ctx:
            sb = self.sb
            xT, qT, kcT, vc, gates = m["xT"], m["qT"], m["kcT"], m["vc"], m["gates"]
            pc = sb(ctx, "vc_p", [P, TT, NH, 32])
            pcT = sb(ctx, "vc_pT", [P, TT, NG, P])
            st = sb(ctx, "vc_st", [P, TT, 3, NH])
            cmask = sb(ctx, "vc_cmask", [P, TT, NCMP])
            anyb = sb(ctx, "vc_any", [P, TT])
            loaded, zeroed, s_done, s_read, g_done, g_out, v_done, v_out, shifted, exped, p_done, t_done, t_out, o_done, o_out, own = \
                self.sems("vc", "loaded", "zeroed", "s_done", "s_read", "g_done", "g_out", "v_done", "v_out", "shifted", "exped",
                          "p_done", "t_done", "t_out", "o_done", "o_out", "own")
            loads = [(cmask[:], self.const(2, "cmpmask").rearrange("p (t n) -> p t n", t=TT)), (anyb[:], self.const(2, "cmpany"))]
            block = ctx.enter_context(nc.Block())

            @block.tensor
            def _(pe):
                for i in range(TT):
                    for hd in range(NH):
                        r = slice(64 * (hd % 2), 64 * (hd % 2) + 64)
                        c = 256 * (i % 2) + 32 * (hd // 2)
                        ins = nc.tensor.matmul(ps[:, 2 * (i // 2) + hd % 2, c:c + NCMP], qT[r, hd // 2, P * i:P * (i + 1)],
                                               kcT[r, hd // 4, :], start=True, stop=True)
                    if i % 2:
                        ins.then_inc(s_done, 1)
                W.arrived(pe, self.n_gate)
                v = slab_view(KD, 48)(W.slot(self.n_gate))
                for t in range(TT):
                    for k in range(KD):
                        ins = nc.tensor.matmul(ps[:, 4, 48 * t:48 * t + 48], xT[:, k, P * t:P * (t + 1)], v[:, k, :],
                                               start=(k == 0), stop=(k == KD - 1))
                ins.then_inc(g_done, 1)
                W.retired_by(self.n_gate, g_done, 1)
                for t in range(TT):
                    bank = 5 + t if t < 3 else 4
                    if t == 3:
                        pe.wait_ge(g_out, 1)
                    for j, n in enumerate(self.n_nv):
                        W.arrived(pe, n)
                        v = slab_view(KD, 256)(W.slot(n))
                        for k in range(KD):
                            ins = nc.tensor.matmul(ps[:, bank, 256 * j:256 * j + 256], xT[:, k, P * t:P * (t + 1)], v[:, k, :],
                                                   start=(k == 0), stop=(k == KD - 1))
                    ins.then_inc(v_done, 1)
                for n in self.n_nv:
                    W.retired_by(n, v_done, TT)
                pe.wait_ge(v_out, TT)
                for it in range(TT + 1):
                    if it < TT:
                        pe.wait_ge(p_done, it + 1)
                        pe.wait_ge(s_read, TT)
                        for g in range(NG):
                            ins = nc.tensor.transpose(ps[:, it, P * g:P * (g + 1)],
                                                      pc[:, it, 4 * g:4 * g + 4, :].rearrange("p h n -> p (h n)"), self.ident[:])
                        ins.then_inc(t_done, 1)
                    i = it - 1
                    if i >= 0:
                        pe.wait_ge(t_out, i + 1)
                        if i >= 2:
                            pe.wait_ge(o_out, i - 1)
                        for g in range(NG):
                            ins = nc.tensor.matmul(ps[:, 4 + 2 * (i % 2) + g // 2, 256 * (g % 2):256 * (g % 2) + 256],
                                                   pcT[:, i, g, :], vc[:, g, :], start=True, stop=True)
                        ins.then_inc(o_done, 1)

            @block.scalar
            def _(act):
                for to, frm in loads:
                    act.dma_start(to, frm).then_inc(loaded, 16)
                act.wait_ge(g_done, 1)
                nc.scalar.activation(gates[:].rearrange("p t c -> p (t c)"), ps[:, 4, 0:48 * TT], ACT.Sigmoid).then_inc(g_out, 1)
                for i in range(TT):
                    act.wait_ge(shifted, i + 1)
                    nc.scalar.activation(pc[:, i, :, 0:NCMP], pc[:, i, :, 0:NCMP], ACT.Exp).then_inc(exped, 1)
                    act.wait_ge(v_done, i + 1)
                    nc.scalar.copy(m["vsw"][:, i, :], ps[:, 5 + i if i < 3 else 4, :]).then_inc(v_out, 1)
                for i in range(TT):
                    act.wait_ge(t_done, i + 1)
                    nc.scalar.copy(pcT[:, i].rearrange("p g q -> p (g q)"), ps[:, i, :]).then_inc(t_out, 1)
                    act.wait_ge(o_done, i + 1)
                    b = 4 + 2 * (i % 2)
                    nc.scalar.copy(m["o"][:, i, :].rearrange("p (a c) -> p a c", a=2), ps[:, b:b + 2, :]).then_inc(o_out, 1)

            @block.gpsimd
            def _(pool):
                nc.gpsimd.memset(pc[:], 0.0).then_inc(zeroed, 1)

            @block.vector
            def _(dve):
                link = Chain(dve, own)
                V = nc.vector
                dve.wait_ge(loaded, 16 * len(loads))
                dve.wait_ge(zeroed, 1)
                for i in range(TT):
                    x = pc[:, i, :, 0:NCMP]
                    dve.wait_ge(s_done, i // 2 + 1)
                    for par in range(2):
                        src = ps[:, 2 * (i // 2) + par, 256 * (i % 2):256 * (i % 2) + 256].rearrange("p (h n) -> p h n", n=32)
                        ins = V.tensor_tensor(x.rearrange("p (h a) n -> p a h n", a=2)[:, par], src[:, :, 0:NCMP],
                                              cmask[:, i, :].unsqueeze(1).broadcast_to([P, NH // 2, NCMP]), ALU.add)
                        if par:
                            ins.then_inc(s_read, 1)
                        else:
                            link(ins)
                    dve.wait_ge(s_read, i + 1)
                    link(V.tensor_reduce(st[:, i, 0], x, AX.X, ALU.max))
                    V.tensor_tensor(x, x, st[:, i, 0].unsqueeze(2).broadcast_to([P, NH, NCMP]), ALU.subtract).then_inc(shifted, 1)
                dve.wait_ge(g_out, 1)
                g4 = gates[:].rearrange("p t (h c) -> p t h c", c=3)
                link(V.tensor_tensor(g4[:, :, :, 0], g4[:, :, :, 0], anyb[:].unsqueeze(2).broadcast_to([P, TT, NH]), ALU.mult))
                for i in range(TT):
                    x = pc[:, i, :, 0:NCMP]
                    dve.wait_ge(exped, i + 1)
                    link(V.reduce_sum(st[:, i, 1], x, AX.X))
                    link(V.reciprocal(st[:, i, 1], st[:, i, 1]))
                    link(V.tensor_tensor(st[:, i, 2], st[:, i, 1], g4[:, i, :, 0], ALU.mult))
                    V.tensor_tensor(x, x, st[:, i, 2].unsqueeze(2).broadcast_to([P, NH, NCMP]), ALU.mult).then_inc(p_done, 1)

            @block.sync
            def _(sp):
                W.send(sp)

    def nsa_attention(self, m):
        nc, ps, W = self.nc, self.ps, self.W
        with self.new_stage() as ctx:
            sb = self.sb
            qT, kd, vsw, gates, o = m["qT"], m["kd"], m["vsw"], m["gates"], m["o"]
            p = sb(ctx, "na_p", [P, 2, 2, SEQ])
            pT = sb(ctx, "na_pT", [P, 2, 2, SEQ])
            st = sb(ctx, "na_st", [P, 4, 8])
            causal = sb(ctx, "na_causal", [P, P])
            loaded, s_done, maxed, exped, t_done, t_out, o_done, o_out, own = self.sems(
                "na", "loaded", "s_done", "maxed", "exped", "t_done", "t_out", "o_done", "o_out", "own")
            units = [(hd, i) for i in range(TT) for hd in range(NH)]
            N = len(units)
            block = ctx.enter_context(nc.Block())

            @block.tensor
            def _(pe):
                for it in range(N + 2):
                    if it < N:
                        hd, i = units[it]
                        r = slice(64 * (hd % 2), 64 * (hd % 2) + 64)
                        nk = P * (i + 1)
                        if it >= 2:
                            pe.wait_ge(exped, 2 * (it - 1))
                        for j in range(2):
                            ins = nc.tensor.matmul(ps[:, 2 * (it % 2) + j, 0:nk], qT[r, hd // 2, P * i:P * (i + 1)],
                                                   kd[r, j, hd // 4, 0:nk], start=True, stop=True)
                        ins.then_inc(s_done, 1)
                    u = it - 1
                    if 0 <= u < N:
                        i = units[u][1]
                        for j in range(2):
                            pe.wait_ge(exped, 2 * u + j + 1)
                            if u:
                                pe.wait_ge(t_out, 2 * (u - 1) + j + 1)
                            for b in range(i + 1):
                                ins = nc.tensor.transpose(ps[:, 4 + j, P * b:P * (b + 1)], p[:, u % 2, j, P * b:P * (b + 1)],
                                                          self.ident[:])
                            ins.then_inc(t_done, 1)
                    u = it - 2
                    if u >= 0:
                        hd, i = units[u]
                        if u >= 2:
                            pe.wait_ge(o_out, u - 1)
                        for j in range(2):
                            pe.wait_ge(t_out, 2 * u + j + 1)
                            c = 256 * j + 64 * (hd // 4)
                            for b in range(i + 1):
                                ins = nc.tensor.matmul(ps[:, 6 + u % 2, 64 * j:64 * j + 64], pT[:, u % 2, j, P * b:P * (b + 1)],
                                                       vsw[:, b, c:c + 64], start=(b == 0), stop=(b == i))
                        ins.then_inc(o_done, 1)

            @block.scalar
            def _(act):
                act.dma_start(causal[:], self.const(2, "causal")).then_inc(loaded, 16)
                for it in range(N + 1):
                    if it < N:
                        i, s = units[it][1], it % 2
                        nk = P * (i + 1)
                        act.wait_ge(maxed, it + 1)
                        for j in range(2):
                            if it >= 2:
                                act.wait_ge(t_done, 2 * (it - 2) + j + 1)
                            if it >= 4:
                                act.wait_ge(o_out, it - 3)
                            nc.scalar.activation(p[:, s, j, 0:nk], ps[:, 2 * s + j, 0:nk], ACT.Exp, bias=st[:, it % 4, j:j + 1],
                                                 accum_out=st[:, it % 4, 2 + j:3 + j]).then_inc(exped, 1)
                    u = it - 1
                    if u >= 0:
                        nk = P * (units[u][1] + 1)
                        if u >= 2:
                            act.wait_ge(o_done, u - 1)
                        for j in range(2):
                            act.wait_ge(t_done, 2 * u + j + 1)
                            nc.scalar.copy(pT[:, u % 2, j, 0:nk], ps[:, 4 + j, 0:nk]).then_inc(t_out, 1)

            @block.vector
            def _(dve):
                link = Chain(dve, own)
                V = nc.vector
                dve.wait_ge(loaded, 16)
                for it in range(N + 3):
                    if it < N:
                        i = units[it][1]
                        s, nk = it % 2, P * (i + 1)
                        dve.wait_ge(s_done, it + 1)
                        S2 = ps[:, 2 * s:2 * s + 2, :]
                        link(V.tensor_tensor(S2[:, :, P * i:nk], S2[:, :, P * i:nk],
                                             causal[:].unsqueeze(1).broadcast_to([P, 2, P]), ALU.add))
                        V.tensor_reduce(st[:, it % 4, 0:2], S2[:, :, 0:nk], AX.X, ALU.max, negate=True).then_inc(maxed, 1)
                    u = it - 3
                    if u >= 0:
                        hd, i = units[u]
                        q = st[:, u % 4]
                        dve.wait_ge(o_done, u + 1)
                        link(V.reciprocal(q[:, 4:6], q[:, 2:4]))
                        link(V.tensor_tensor(q[:, 6:8], q[:, 4:6], gates[:, i, 3 * hd + 1:3 * hd + 3], ALU.mult))
                        x = o[:, i, 64 * hd:64 * hd + 64]
                        link(V.scalar_tensor_tensor(x, ps[:, 6 + u % 2, 0:64], q[:, 6:7], x, ALU.mult, ALU.add))
                        V.scalar_tensor_tensor(x, ps[:, 6 + u % 2, 64:128], q[:, 7:8], x, ALU.mult, ALU.add).then_inc(o_out, 1)

            @block.sync
            def _(sp):
                W.send(sp)

    def nsa_out(self, m):
        nc, ps, W, h = self.nc, self.ps, self.W, self.h
        with self.new_stage() as ctx:
            turned, t_out, y_done, y_out = self.sems("no", "turned", "t_out", "y_done", "y_out")
            oT = m["xT"]
            block = ctx.enter_context(nc.Block())

            @block.tensor
            def _(pe):
                for t in range(TT):
                    for k in range(KD):
                        ins = nc.tensor.transpose(ps[:, 2 * t + k // 4, (k % 4) * P:(k % 4) * P + P],
                                                  m["o"][:, t, k * P:(k + 1) * P], self.ident[:])
                    ins.then_inc(turned, 1)
                pe.wait_ge(t_out, TT)
                self.tm_product(pe, self.n_no, lambda k, t: oT[:, k, P * t:P * (t + 1)], y_done)

            @block.scalar
            def _(act):
                for t in range(TT):
                    act.wait_ge(turned, t + 1)
                    nc.scalar.copy(oT[:, :, P * t:P * (t + 1)],
                                   ps[:, 2 * t:2 * t + 2, :].rearrange("p a (k c) -> p (a k) c", c=P)).then_inc(t_out, 1)

            @block.vector
            def _(dve):
                for t in range(TT):
                    dve.wait_ge(y_done, t + 1)
                    x = h[:, t, :].rearrange("p (a c) -> p a c", a=2)
                    nc.vector.scalar_tensor_tensor(x, x, ALPHA, ps[:, 2 * t:2 * t + 2, :], ALU.mult, ALU.add).then_inc(y_out, 1)

            @block.sync
            def _(sp):
                W.send(sp)


def build(nc, A, out, places1, places2, stop=None):
    with ExitStack() as root:
        root.enter_context(nc.allow_non_contiguous_dma(reason="small parameters"))
        K = Program(nc, A, places1, places2, root)
        K.first_block(stop)
        if stop not in ("n1", "s5", "mix", "first"):
            K.second_block(out, stop)
        if stop:
            with nc.Block() as block:
                @block.sync
                def _(sp):
                    for n in range(K.W.sent - RING, K.W.sent):
                        K.W.arrived(sp, n)


_STOP = None


def kernel(**inputs):
    import numpy as _np
    import concourse.bacc as _bacc
    from concourse import mybir as _mybir
    from concourse.bass_utils import run_bass_kernel_spmd as _run

    nc = _bacc.Bacc("TRN2", target_bir_lowering=False, num_devices=1)
    c1, places1, c2, places2 = constants()
    arrays, A = {}, {}
    given = dict(inputs)
    given["const1"], given["const2"] = c1, c2
    for name, a in given.items():
        a = _np.ascontiguousarray(a)
        arrays[f"in_{name}"] = a
        A[name] = nc.dram_tensor(f"in_{name}", a.shape, _mybir.dt.from_np(a.dtype), kind="ExternalInput").ap()
    out = nc.dram_tensor("out", (1, SEQ, D), F32, kind="ExternalOutput").ap()
    build(nc, A, out, places1, places2, _STOP)
    r = _run(nc, [arrays], core_ids=[0])
    return r.results[0]["out"]
```
